# Optimizing a Trainium2 kernel written in Bass

```python
import math
import jax, jax.numpy as jnp
from jax import lax
import numpy as np
import jax
import jax.numpy as jnp

D_MODEL = 1024
BATCH = 1
SEQ = 512
DEPTH = 1

HEAD_DIM = 64
N_HEADS_A = 8
N_KV_A = 2
GQA_GROUP = N_HEADS_A // N_KV_A
N_HEADS_B = 8
WIDTH_A = N_HEADS_A * HEAD_DIM
WIDTH_B = N_HEADS_B * HEAD_DIM
KV_WIDTH_A = N_KV_A * HEAD_DIM
IN_WIDTH = WIDTH_A + 2 * KV_WIDTH_A + 3 * WIDTH_B
D_FF = 2816
CONV_WIDTH = 3
GRID_W = 64
ROPE_THETA = 10000.0
ROPE_AXIS_DIM = HEAD_DIM // 2
Q_BLOCK = 128
DIL_BLOCK = 64
DILATED_PATTERNS = ((128, 1), (512, 4), (2048, 16))
NORM_EPS = 1e-6
NEG_INF = -1e30


def rms_norm(x, g):
    xf = x.astype(jnp.float32)
    y = xf * lax.rsqrt(jnp.mean(xf * xf, axis=-1, keepdims=True) + NORM_EPS)
    return (y * g.astype(jnp.float32)).astype(x.dtype)

def axial_rope_tables(seq_len):
    rows = seq_len // GRID_W
    row = jnp.repeat(jnp.arange(rows, dtype=jnp.float32), GRID_W)
    col = jnp.tile(jnp.arange(GRID_W, dtype=jnp.float32), rows)
    inv = ROPE_THETA ** (-jnp.arange(0, ROPE_AXIS_DIM, 2, dtype=jnp.float32) / ROPE_AXIS_DIM)
    ang_r = row[:, None] * inv[None, :]
    ang_c = col[:, None] * inv[None, :]
    return jnp.cos(ang_r), jnp.sin(ang_r), jnp.cos(ang_c), jnp.sin(ang_c)

def _rotate(u, c, s):
    half = u.shape[-1] // 2
    u1, u2 = u[..., :half], u[..., half:]
    c = c[:, None, :]
    s = s[:, None, :]
    return jnp.concatenate([u1 * c - u2 * s, u2 * c + u1 * s], axis=-1)

def apply_axial_rope(x, tables):
    cos_r, sin_r, cos_c, sin_c = tables
    xf = x.astype(jnp.float32)
    out = jnp.concatenate([_rotate(xf[..., :ROPE_AXIS_DIM], cos_r, sin_r),
                           _rotate(xf[..., ROPE_AXIS_DIM:], cos_c, sin_c)], axis=-1)
    return out.astype(x.dtype)

def global_gqa_attention(q, k, v):
    b, s = q.shape[0], q.shape[1]
    nb = s // Q_BLOCK
    qg = q.reshape(b, nb, Q_BLOCK, N_KV_A, GQA_GROUP, HEAD_DIM).transpose(1, 0, 2, 3, 4, 5)
    scale = HEAD_DIM ** -0.5

    def block(qb):
        sc = jnp.einsum('bqkgd,bskd->bkgqs', qb, k, preferred_element_type=jnp.float32) * scale
        p = jax.nn.softmax(sc, axis=-1)
        return jnp.einsum('bkgqs,bskd->bqkgd', p.astype(v.dtype), v)

    o = lax.map(block, qg)
    return o.transpose(1, 0, 2, 3, 4, 5).reshape(b, s, WIDTH_A)

def alibi_slopes(n_heads):
    return 2.0 ** (-8.0 * jnp.arange(1, n_heads + 1, dtype=jnp.float32) / n_heads)

def dilated_window_attention(q, k, v, window, dilation, slopes):
    b, s, h, hd = q.shape
    d = dilation
    n_side = (window // 2) // d
    L = s // d
    nb = -(-L // DIL_BLOCK)
    Lp = nb * DIL_BLOCK

    def strided(a):
        return a.reshape(b, L, d, h, hd).transpose(0, 2, 1, 3, 4)

    qs = jnp.pad(strided(q), ((0, 0), (0, 0), (0, Lp - L), (0, 0), (0, 0)))
    qb = qs.reshape(b, d, nb, DIL_BLOCK, h, hd)

    def banded(a):
        ap = jnp.pad(strided(a), ((0, 0), (0, 0), (DIL_BLOCK, Lp - L + DIL_BLOCK), (0, 0), (0, 0)))
        ap = ap.reshape(b, d, nb + 2, DIL_BLOCK, h, hd)
        return jnp.concatenate([ap[:, :, :-2], ap[:, :, 1:-1], ap[:, :, 2:]], axis=3)

    kw = banded(k)
    vw = banded(v)

    qi = jnp.arange(DIL_BLOCK)[:, None]
    kj = jnp.arange(3 * DIL_BLOCK)[None, :]
    off = kj - DIL_BLOCK - qi
    key_idx = jnp.arange(nb)[:, None, None] * DIL_BLOCK - DIL_BLOCK + kj[None]
    valid = (jnp.abs(off) <= n_side)[None] & (key_idx >= 0) & (key_idx < L)
    dist = (jnp.abs(off) * d).astype(jnp.float32)
    bias = jnp.where(valid[:, None], -slopes[None, :, None, None] * dist[None, None],
                     NEG_INF)

    sc = jnp.einsum('brnqhd,brnkhd->brnhqk', qb, kw, preferred_element_type=jnp.float32)
    sc = sc * (hd ** -0.5) + bias[None, None]
    lse = jax.nn.logsumexp(sc, axis=-1)
    p = jnp.exp(sc - lse[..., None])
    o = jnp.einsum('brnhqk,brnkhd->brnqhd', p.astype(v.dtype), vw)

    o = o.reshape(b, d, Lp, h, hd)[:, :, :L].transpose(0, 2, 1, 3, 4).reshape(b, s, h, hd)
    lse = lse.transpose(0, 1, 2, 4, 3).reshape(b, d, Lp, h)[:, :, :L]
    lse = lse.transpose(0, 2, 1, 3).reshape(b, s, h)
    return o, lse

def dilated_mixture_attention(q, k, v):
    slopes = alibi_slopes(N_HEADS_B)
    outs, lses = [], []
    for window, dilation in DILATED_PATTERNS:
        o, lse = dilated_window_attention(q, k, v, window, dilation, slopes)
        outs.append(o)
        lses.append(lse)
    w = jax.nn.softmax(jnp.stack(lses, axis=0), axis=0)
    o = jnp.sum(w[..., None].astype(q.dtype) * jnp.stack(outs, axis=0), axis=0)
    return o.reshape(q.shape[0], q.shape[1], WIDTH_B)

def conv_ffn(h, w_up, conv_w, conv_b, w_down):
    u = h @ w_up
    c = u.shape[-1]
    u = lax.conv_general_dilated(u, conv_w[:, None, :].astype(u.dtype), window_strides=(1,),
                                 padding=((CONV_WIDTH // 2, CONV_WIDTH // 2),),
                                 dimension_numbers=('NWC', 'WIO', 'NWC'),
                                 feature_group_count=c) + conv_b
    gate, val = u[..., :D_FF], u[..., D_FF:]
    return (jax.nn.gelu(gate) * val) @ w_down

def first_inputs(seed: int = 0) -> dict:
    key = jax.random.key(seed)
    ks = jax.random.split(key, 16)
    f32 = jnp.float32

    def gain(k, n):
        return 1.0 + 0.05 * jax.random.normal(k, (n,), f32)

    return {
        "x": jax.random.normal(ks[0], (BATCH, SEQ, D_MODEL), f32),
        "norm1_g": gain(ks[1], D_MODEL),
        "w_in": jax.random.normal(ks[2], (D_MODEL, IN_WIDTH), f32) * D_MODEL ** -0.5,
        "qa_norm_g": gain(ks[3], HEAD_DIM),
        "ka_norm_g": gain(ks[4], HEAD_DIM),
        "qb_norm_g": gain(ks[5], HEAD_DIM),
        "kb_norm_g": gain(ks[6], HEAD_DIM),
        "outa_norm_g": gain(ks[7], WIDTH_A),
        "outb_norm_g": gain(ks[8], WIDTH_B),
        "w_out": jax.random.normal(ks[9], (WIDTH_A + WIDTH_B, D_MODEL), f32) * (WIDTH_A + WIDTH_B) ** -0.5,
        "norm2_g": gain(ks[10], D_MODEL),
        "w_up": jax.random.normal(ks[11], (D_MODEL, 2 * D_FF), f32) * D_MODEL ** -0.5,
        "conv_w": jax.random.normal(ks[12], (CONV_WIDTH, 2 * D_FF), f32) * CONV_WIDTH ** -0.5,
        "conv_b": 0.02 * jax.random.normal(ks[13], (2 * D_FF,), f32),
        "w_down": jax.random.normal(ks[14], (D_FF, D_MODEL), f32) * D_FF ** -0.5,
    }

def first_block(x, norm1_g, w_in, qa_norm_g, ka_norm_g, qb_norm_g, kb_norm_g,
              outa_norm_g, outb_norm_g, w_out, norm2_g, w_up, conv_w, conv_b, w_down):
    b, s, _ = x.shape
    tables = axial_rope_tables(s)
    for _layer in range(DEPTH):
        hn = rms_norm(x, norm1_g)
        proj = hn @ w_in
        o1 = WIDTH_A
        o2 = o1 + KV_WIDTH_A
        o3 = o2 + KV_WIDTH_A
        o4 = o3 + WIDTH_B
        o5 = o4 + WIDTH_B
        qa = proj[..., :o1].reshape(b, s, N_HEADS_A, HEAD_DIM)
        ka = proj[..., o1:o2].reshape(b, s, N_KV_A, HEAD_DIM)
        va = proj[..., o2:o3].reshape(b, s, N_KV_A, HEAD_DIM)
        qb = proj[..., o3:o4].reshape(b, s, N_HEADS_B, HEAD_DIM)
        kb = proj[..., o4:o5].reshape(b, s, N_HEADS_B, HEAD_DIM)
        vb = proj[..., o5:].reshape(b, s, N_HEADS_B, HEAD_DIM)

        qa = apply_axial_rope(rms_norm(qa, qa_norm_g), tables)
        ka = apply_axial_rope(rms_norm(ka, ka_norm_g), tables)
        out_a = global_gqa_attention(qa, ka, va)

        out_b = dilated_mixture_attention(rms_norm(qb, qb_norm_g), rms_norm(kb, kb_norm_g), vb)

        mixed = jnp.concatenate([rms_norm(out_a, outa_norm_g), rms_norm(out_b, outb_norm_g)], axis=-1)
        x = x + mixed @ w_out

        x = x + conv_ffn(rms_norm(x, norm2_g), w_up, conv_w, conv_b, w_down)
    return x


CTX_LEN = 256
EPS = 1e-6

MIX_WIDTH = D_MODEL
SSD_INNER = MIX_WIDTH // 2
SSD_HEAD_DIM = 64
SSD_HEADS = SSD_INNER // SSD_HEAD_DIM
SSD_GROUPS = 2
SSD_HEADS_PER_GROUP = SSD_HEADS // SSD_GROUPS
SSD_STATE = 128
CONV_WIDTH_2 = 5
CONV_DIM = SSD_INNER + 2 * SSD_GROUPS * SSD_STATE
CHUNK = 128
DT_MIN = 0.001
DT_MAX = 0.1
ATTN_WIDTH = MIX_WIDTH - SSD_INNER
ATTN_Q_HEADS = ATTN_WIDTH // HEAD_DIM
ATTN_KV_HEADS = 2
Q_PER_KV = ATTN_Q_HEADS // ATTN_KV_HEADS
KV_WIDTH = ATTN_KV_HEADS * HEAD_DIM
WINDOW = 128
BLOCK = 128
ROPE_BASE = 10000.0
IN_COLS = SSD_INNER + CONV_DIM + 2 * SSD_HEADS + ATTN_WIDTH + 2 * KV_WIDTH
N_GROUPS = 4
EXPERTS_PER_GROUP = 8
N_EXPERTS = N_GROUPS * EXPERTS_PER_GROUP
TOP_K = 2
EXPERT_DIM = D_MODEL // 2
MOE_BLOCK = 128


def rms_norm_2(x, gain):
    xf = x.astype(jnp.float32)
    y = xf * lax.rsqrt(jnp.mean(xf * xf, axis=-1, keepdims=True) + EPS)
    return (y * gain).astype(x.dtype)

def _flip(t):
    return jnp.flip(t, axis=1)

def split_projection(p):
    sizes = [SSD_INNER, CONV_DIM, 2 * SSD_HEADS, ATTN_WIDTH, KV_WIDTH, KV_WIDTH]
    return jnp.split(p, np.cumsum(sizes)[:-1].tolist(), axis=-1)

def centred_dwconv(u, w, b):
    out = lax.conv_general_dilated(
        u, w[:, None, :].astype(u.dtype), window_strides=(1,),
        padding=((CONV_WIDTH_2 // 2, CONV_WIDTH_2 // 2),),
        dimension_numbers=('NWC', 'WIO', 'NWC'), feature_group_count=u.shape[-1])
    return out + b.astype(u.dtype)

def ssd_inputs(xbc, dt_raw, conv_w, conv_b, dt_bias):
    b, L = xbc.shape[:2]
    u = jax.nn.silu(centred_dwconv(xbc, conv_w, conv_b))
    xs, bm, cm = jnp.split(u, [SSD_INNER, SSD_INNER + SSD_GROUPS * SSD_STATE], axis=-1)
    xs = xs.reshape(b, L, SSD_HEADS, SSD_HEAD_DIM)
    bm = bm.reshape(b, L, SSD_GROUPS, SSD_STATE)
    cm = cm.reshape(b, L, SSD_GROUPS, SSD_STATE)
    dt = jax.nn.softplus(dt_raw.astype(jnp.float32).reshape(b, L, 2, SSD_HEADS) + dt_bias)
    return xs, bm, cm, dt

def ssd_scan(xs, dt, a, bm, cm, h0, need_y=True):
    f32 = jnp.float32
    b, L = xs.shape[:2]
    nc = L // CHUNK
    G, R, P, N = SSD_GROUPS, SSD_HEADS_PER_GROUP, SSD_HEAD_DIM, SSD_STATE
    xg = xs.astype(f32).reshape(b, nc, CHUNK, G, R, P)
    dtc = dt.astype(f32).reshape(b, nc, CHUNK, G, R)
    bc = bm.astype(f32).reshape(b, nc, CHUNK, G, N)
    a_cs = jnp.cumsum(dtc * a.reshape(G, R), axis=2)
    a_last = a_cs[:, :, -1]
    dtx = dtc[..., None] * xg
    states = jnp.einsum('bcjgn,bcjgr,bcjgrp->bcgrpn', bc, jnp.exp(a_last[:, :, None] - a_cs), dtx)

    def step(h, inp):
        s, al = inp
        return jnp.exp(al)[..., None, None] * h + s, h

    h_final, h_prev = lax.scan(step, h0.astype(f32),
                               (jnp.moveaxis(states, 1, 0), jnp.moveaxis(a_last, 1, 0)))
    if not need_y:
        return None, h_final
    cc = cm.astype(f32).reshape(b, nc, CHUNK, G, N)
    tri = jnp.tril(jnp.ones((CHUNK, CHUNK), dtype=bool))
    seg = a_cs[:, :, :, None] - a_cs[:, :, None, :]
    decay = jnp.exp(jnp.where(tri[:, :, None, None], seg, -jnp.inf))
    cb = jnp.einsum('bcign,bcjgn->bcijg', cc, bc)
    y_diag = jnp.einsum('bcijgr,bcjgrp->bcigrp', cb[..., None] * decay, dtx)
    y_off = jnp.einsum('bcign,cbgrpn->bcigrp', cc, h_prev) * jnp.exp(a_cs)[..., None]
    return (y_diag + y_off).reshape(b, L, SSD_HEADS, P), h_final

def ssd_output(y, xs, z, d_skip, gain):
    b, L = xs.shape[:2]
    y = y + d_skip.astype(jnp.float32)[:, None] * xs.astype(jnp.float32)
    y = y.reshape(b, L, SSD_INNER) * jax.nn.silu(z.astype(jnp.float32))
    return rms_norm_2(y, gain).astype(z.dtype)

def axial_rope_tables_2(rows):
    row = jnp.repeat(jnp.arange(rows), GRID_W)
    col = jnp.tile(jnp.arange(GRID_W), rows)
    n_freq = HEAD_DIM // 4
    inv_freq = ROPE_BASE ** (-jnp.arange(n_freq, dtype=jnp.float32) / n_freq)
    ang = jnp.concatenate([row[:, None] * inv_freq, col[:, None] * inv_freq], axis=-1)
    ang = jnp.concatenate([ang, ang], axis=-1)
    return jnp.cos(ang), jnp.sin(ang)

def apply_rope(t, cos, sin):
    half = HEAD_DIM // 2
    rot = jnp.concatenate([-t[..., half:], t[..., :half]], axis=-1)
    return (t * cos[:, None] + rot * sin[:, None]).astype(t.dtype)

def softmax_with_sink(logits, sink):
    full = jnp.concatenate([logits, jnp.broadcast_to(sink, logits.shape[:-1] + (1,))], axis=-1)
    return jax.nn.softmax(full, axis=-1)[..., :-1]

def windowed_attention(q, k, v, k_ctx, v_ctx, sinks):
    f32 = jnp.float32
    b, L = q.shape[:2]
    nb = L // BLOCK
    scale = HEAD_DIM ** -0.5
    qb = q.reshape(b, nb, BLOCK, ATTN_KV_HEADS, Q_PER_KV, HEAD_DIM)

    def band(t):
        tp = jnp.pad(t, ((0, 0), (BLOCK, BLOCK), (0, 0), (0, 0)))
        tp = tp.reshape(b, nb + 2, BLOCK, ATTN_KV_HEADS, HEAD_DIM)
        return jnp.concatenate([tp[:, :-2], tp[:, 1:-1], tp[:, 2:]], axis=2)

    kw, vw = band(k), band(v)
    s_loc = jnp.einsum('bnqhgd,bnkhd->bnhgqk', qb, kw, preferred_element_type=f32) * scale
    blk = jnp.arange(nb)[:, None, None] * BLOCK
    q_pos = blk + jnp.arange(BLOCK)[None, :, None]
    k_pos = blk + jnp.arange(3 * BLOCK)[None, None, :] - BLOCK
    valid = (jnp.abs(k_pos - q_pos) <= WINDOW) & (k_pos >= 0) & (k_pos < L)
    s_loc = jnp.where(valid[None, :, None, None], s_loc, -jnp.inf)
    s_ctx = jnp.einsum('bnqhgd,bkhd->bnhgqk', qb, k_ctx, preferred_element_type=f32) * scale
    sink = sinks.astype(f32).reshape(ATTN_KV_HEADS, Q_PER_KV)[:, :, None, None]
    p = softmax_with_sink(jnp.concatenate([s_loc, s_ctx], axis=-1), sink)
    p_loc = p[..., :3 * BLOCK].astype(v.dtype)
    p_ctx = p[..., 3 * BLOCK:].astype(v.dtype)
    o = (jnp.einsum('bnhgqk,bnkhd->bnqhgd', p_loc, vw)
         + jnp.einsum('bnhgqk,bkhd->bnqhgd', p_ctx, v_ctx))
    return o.reshape(b, L, ATTN_WIDTH)

def context_attention(q_c, k_c, v_c, sinks):
    b, Lc = q_c.shape[:2]
    qg = q_c.reshape(b, Lc, ATTN_KV_HEADS, Q_PER_KV, HEAD_DIM)
    s = jnp.einsum('bqhgd,bkhd->bhgqk', qg, k_c, preferred_element_type=jnp.float32) * HEAD_DIM ** -0.5
    sink = sinks.astype(jnp.float32).reshape(ATTN_KV_HEADS, Q_PER_KV)[:, :, None, None]
    p = softmax_with_sink(s, sink).astype(v_c.dtype)
    return jnp.einsum('bhgqk,bkhd->bqhgd', p, v_c).reshape(b, Lc, ATTN_WIDTH)

def hier_moe(h, w_group, b_group, w_expert, b_expert, w_gate, w_up, w_down):
    f32 = jnp.float32
    n_tok, d = h.shape
    g_prob = jax.nn.softmax((h @ w_group).astype(f32) + b_group, axis=-1)
    g_w, g_idx = lax.top_k(g_prob, 1)
    e_logits = ((h @ w_expert).astype(f32) + b_expert).reshape(n_tok, N_GROUPS, EXPERTS_PER_GROUP)
    e_sel = e_logits[jnp.arange(n_tok), g_idx[:, 0]]
    e_w, e_idx = lax.top_k(jax.nn.softmax(e_sel, axis=-1), TOP_K)
    weights = g_w * e_w / jnp.sum(e_w, axis=-1, keepdims=True)
    expert = g_idx * EXPERTS_PER_GROUP + e_idx
    n_assign = n_tok * TOP_K
    flat_e = expert.reshape(n_assign).astype(jnp.int32)
    flat_tok = jnp.repeat(jnp.arange(n_tok, dtype=jnp.int32), TOP_K)
    flat_w = weights.reshape(n_assign)
    order = jnp.argsort(flat_e)
    sorted_e = flat_e[order]
    counts = jnp.zeros((N_EXPERTS,), jnp.int32).at[flat_e].add(1)
    start = jnp.cumsum(counts) - counts
    padded = (counts + MOE_BLOCK - 1) // MOE_BLOCK * MOE_BLOCK
    ends = jnp.cumsum(padded)
    pstart = ends - padded
    dest = pstart[sorted_e] + jnp.arange(n_assign, dtype=jnp.int32) - start[sorted_e]
    n_blocks = -(-n_assign // MOE_BLOCK) + N_EXPERTS
    n_slots = n_blocks * MOE_BLOCK
    tok_buf = jnp.full((n_slots,), n_tok, jnp.int32).at[dest].set(flat_tok[order])
    w_buf = jnp.zeros((n_slots,), f32).at[dest].set(flat_w[order])
    h_pad = jnp.concatenate([h, jnp.zeros((1, d), h.dtype)], axis=0)
    x_buf = h_pad[tok_buf].reshape(n_blocks, MOE_BLOCK, d)
    blk_e = jnp.searchsorted(ends, jnp.arange(n_blocks, dtype=jnp.int32) * MOE_BLOCK, side='right')
    blk_e = jnp.minimum(blk_e, N_EXPERTS - 1)

    def expert_block(args):
        xb, e = args
        return (jax.nn.silu(xb @ w_gate[e]) * (xb @ w_up[e])) @ w_down[e]

    y_buf = lax.map(expert_block, (x_buf, blk_e)).reshape(n_slots, d)
    out = jax.ops.segment_sum(y_buf.astype(f32) * w_buf[:, None], tok_buf, num_segments=n_tok + 1)
    return out[:n_tok].astype(h.dtype)

def second_inputs(seed: int = 0) -> dict:
    key = jax.random.key(seed)
    ks = jax.random.split(key, 26)
    f32 = jnp.float32

    def nrm(k, shape, scale):
        return jax.random.normal(k, shape, f32) * scale

    u = jax.random.uniform(ks[10], (DEPTH, 2, SSD_HEADS), f32)
    dt0 = jnp.exp(u * (math.log(DT_MAX) - math.log(DT_MIN)) + math.log(DT_MIN))
    return {
        'x': nrm(ks[0], (BATCH, SEQ, D_MODEL), 1.0),
        'c': nrm(ks[1], (BATCH, D_MODEL), 1.0),
        'ctx': nrm(ks[2], (BATCH, CTX_LEN, D_MODEL), 1.0),
        'c_ctx': nrm(ks[3], (D_MODEL,), 1.0),
        'w_ada': nrm(ks[4], (DEPTH, D_MODEL, 6 * D_MODEL), 0.5 * D_MODEL ** -0.5),
        'b_ada': nrm(ks[5], (DEPTH, 6 * D_MODEL), 0.02),
        'norm1': 1.0 + nrm(ks[6], (DEPTH, D_MODEL), 0.02),
        'w_in': nrm(ks[7], (DEPTH, D_MODEL, IN_COLS), D_MODEL ** -0.5),
        'conv_w': nrm(ks[8], (DEPTH, CONV_WIDTH_2, CONV_DIM), CONV_WIDTH_2 ** -0.5),
        'conv_b': nrm(ks[9], (DEPTH, CONV_DIM), 0.02),
        'dt_bias': dt0 + jnp.log(-jnp.expm1(-dt0)),
        'a_log': jnp.log(jax.random.uniform(ks[11], (DEPTH, 2, SSD_HEADS), f32, 1.0, 16.0)),
        'd_skip': 1.0 + nrm(ks[12], (DEPTH, SSD_HEADS), 0.1),
        'ssd_norm': 1.0 + nrm(ks[13], (DEPTH, SSD_INNER), 0.02),
        'attn_sinks': nrm(ks[14], (DEPTH, ATTN_Q_HEADS), 1.0),
        'w_out': nrm(ks[15], (DEPTH, MIX_WIDTH, D_MODEL), MIX_WIDTH ** -0.5),
        'norm2': 1.0 + nrm(ks[16], (DEPTH, D_MODEL), 0.02),
        'w_group': nrm(ks[17], (DEPTH, D_MODEL, N_GROUPS), D_MODEL ** -0.5),
        'b_group': nrm(ks[18], (DEPTH, N_GROUPS), 0.01),
        'w_expert': nrm(ks[19], (DEPTH, D_MODEL, N_EXPERTS), D_MODEL ** -0.5),
        'b_expert': nrm(ks[20], (DEPTH, N_EXPERTS), 0.01),
        'w_gate': nrm(ks[21], (DEPTH, N_EXPERTS, D_MODEL, EXPERT_DIM), D_MODEL ** -0.5),
        'w_up': nrm(ks[22], (DEPTH, N_EXPERTS, D_MODEL, EXPERT_DIM), D_MODEL ** -0.5),
        'w_down': nrm(ks[23], (DEPTH, N_EXPERTS, EXPERT_DIM, D_MODEL), EXPERT_DIM ** -0.5),
        'norm_final': 1.0 + nrm(ks[24], (D_MODEL,), 0.02),
    }

def second_block(x, c, ctx, c_ctx, w_ada, b_ada, norm1, w_in, conv_w, conv_b, dt_bias, a_log,
              d_skip, ssd_norm, attn_sinks, w_out, norm2, w_group, b_group, w_expert, b_expert,
              w_gate, w_up, w_down, norm_final):
    b, n_tok, d = x.shape
    n_ctx = ctx.shape[1]
    rows = n_tok // GRID_W
    cos, sin = axial_rope_tables_2(rows)
    h0 = jnp.zeros((b, SSD_GROUPS, SSD_HEADS_PER_GROUP, SSD_HEAD_DIM, SSD_STATE), jnp.float32)
    for layer in range(DEPTH):
        last = layer == DEPTH - 1
        mod_x = jax.nn.silu(c) @ w_ada[layer] + b_ada[layer]
        mod_c = jax.nn.silu(c_ctx) @ w_ada[layer] + b_ada[layer]
        sh1, sc1, g1, sh2, sc2, g2 = jnp.split(mod_x[:, None, :], 6, axis=-1)
        csh1, csc1, cg1, csh2, csc2, cg2 = jnp.split(mod_c, 6, axis=-1)
        hx = rms_norm_2(x, norm1[layer]) * (1 + sc1) + sh1
        hc = rms_norm_2(ctx, norm1[layer]) * (1 + csc1) + csh1
        zx, xbc_x, dt_x, qx, kx, vx = split_projection(hx @ w_in[layer])
        zc, xbc_c, dt_c, qc, kc, vc = split_projection(hc @ w_in[layer])
        xs_x, bm_x, cm_x, dtv_x = ssd_inputs(xbc_x, dt_x, conv_w[layer], conv_b[layer], dt_bias[layer])
        xs_c, bm_c, cm_c, dtv_c = ssd_inputs(xbc_c, dt_c, conv_w[layer], conv_b[layer], dt_bias[layer])
        A = -jnp.exp(a_log[layer].astype(jnp.float32))
        y_cf, h_cf = ssd_scan(xs_c, dtv_c[:, :, 0], A[0], bm_c, cm_c, h0, need_y=not last)
        y_cb, h_cb = ssd_scan(_flip(xs_c), _flip(dtv_c[:, :, 1]), A[1], _flip(bm_c), _flip(cm_c), h0,
                              need_y=not last)
        y_xf, _ = ssd_scan(xs_x, dtv_x[:, :, 0], A[0], bm_x, cm_x, h_cf)
        y_xb, _ = ssd_scan(_flip(xs_x), _flip(dtv_x[:, :, 1]), A[1], _flip(bm_x), _flip(cm_x), h_cb)
        ssd_x = ssd_output(y_xf + _flip(y_xb), xs_x, zx, d_skip[layer], ssd_norm[layer])
        qx = apply_rope(qx.reshape(b, n_tok, ATTN_Q_HEADS, HEAD_DIM), cos, sin)
        kx = apply_rope(kx.reshape(b, n_tok, ATTN_KV_HEADS, HEAD_DIM), cos, sin)
        vx = vx.reshape(b, n_tok, ATTN_KV_HEADS, HEAD_DIM)
        kc = kc.reshape(b, n_ctx, ATTN_KV_HEADS, HEAD_DIM)
        vc = vc.reshape(b, n_ctx, ATTN_KV_HEADS, HEAD_DIM)
        attn_x = windowed_attention(qx, kx, vx, kc, vc, attn_sinks[layer])
        x = x + g1 * (jnp.concatenate([ssd_x, attn_x], axis=-1) @ w_out[layer])
        h2 = rms_norm_2(x, norm2[layer]) * (1 + sc2) + sh2
        moe_x = hier_moe(h2.reshape(b * n_tok, d), w_group[layer], b_group[layer], w_expert[layer],
                         b_expert[layer], w_gate[layer], w_up[layer], w_down[layer])
        x = x + g2 * moe_x.reshape(b, n_tok, d)
        if not last:
            ssd_c = ssd_output(y_cf + _flip(y_cb), xs_c, zc, d_skip[layer], ssd_norm[layer])
            attn_c = context_attention(qc.reshape(b, n_ctx, ATTN_Q_HEADS, HEAD_DIM), kc, vc, attn_sinks[layer])
            ctx = ctx + cg1 * (jnp.concatenate([ssd_c, attn_c], axis=-1) @ w_out[layer])
            h2c = rms_norm_2(ctx, norm2[layer]) * (1 + csc2) + csh2
            moe_c = hier_moe(h2c.reshape(b * n_ctx, d), w_group[layer], b_group[layer], w_expert[layer],
                             b_expert[layer], w_gate[layer], w_up[layer], w_down[layer])
            ctx = ctx + cg2 * moe_c.reshape(b, n_ctx, d)
    return rms_norm_2(x, norm_final)


def setup_inputs(seed=0):
    out = dict(first_inputs(seed))
    for name, value in second_inputs(seed + 1).items():
        if name != "x":
            out[name + "_2"] = value
    return out


def reference(
    x, norm1_g, w_in, qa_norm_g, ka_norm_g, qb_norm_g, kb_norm_g, outa_norm_g, outb_norm_g,
    w_out, norm2_g, w_up, conv_w, conv_b, w_down, c_2, ctx_2, c_ctx_2, w_ada_2, b_ada_2,
    norm1_2, w_in_2, conv_w_2, conv_b_2, dt_bias_2, a_log_2, d_skip_2, ssd_norm_2, attn_sinks_2,
    w_out_2, norm2_2, w_group_2, b_group_2, w_expert_2, b_expert_2, w_gate_2, w_up_2, w_down_2,
    norm_final_2,
):
    x = first_block(
        x, norm1_g, w_in, qa_norm_g, ka_norm_g, qb_norm_g, kb_norm_g, outa_norm_g, outb_norm_g,
        w_out, norm2_g, w_up, conv_w, conv_b, w_down,
    )
    return second_block(
        x, c_2, ctx_2, c_ctx_2, w_ada_2, b_ada_2, norm1_2, w_in_2, conv_w_2, conv_b_2,
        dt_bias_2, a_log_2, d_skip_2, ssd_norm_2, attn_sinks_2, w_out_2, norm2_2, w_group_2,
        b_group_2, w_expert_2, b_expert_2, w_gate_2, w_up_2, w_down_2, norm_final_2,
    )


_drawn_inputs = setup_inputs


def setup_inputs(seed=0):
    import zlib

    import numpy as np

    out = dict(_drawn_inputs(seed))
    spreads = {}
    factors = {'conv_b': 4.175,
     'ctx_2': 4.016,
     'b_ada_2': 3.927,
     'norm1_2': 8.0,
     'conv_b_2': 8.0,
     'd_skip_2': 200.0,
     'ssd_norm_2': 8.0,
     'attn_sinks_2': 8.0,
     'norm2_2': 7.364,
     'b_group_2': 8.0,
     'b_expert_2': 8.0,
     'norm_final_2': 23.6}
    for name, (base, spread) in spreads.items():
        noise = np.random.default_rng([zlib.crc32(name.encode()), seed]).standard_normal(out[name].shape)
        drawn = base * np.exp(spread * noise) if base else spread * noise
        out[name] = jnp.asarray(drawn.astype(out[name].dtype))
    for name, factor in factors.items():
        out[name] = (out[name] * factor).astype(out[name].dtype)
    return out
```

```python
import numpy as np
import concourse.bass as bass
from concourse import mybir
from contextlib import ExitStack

F32 = mybir.dt.float32
I32 = mybir.dt.int32
U32 = mybir.dt.uint32
ALU = mybir.AluOpType
ACT = mybir.ActivationFunctionType
AXX = mybir.AxisListType.X

P = 128
T, CTX, D = 512, 256, 1024
TT, CT = T // P, CTX // P
AT = TT + CT
KT = D // P
HD = 64
H = 8
W1 = 2304
DFF = 2816
FT = DFF // P
E = 32
EG = 8
EF = 512
BLK = 64
NOVF = 2 * T // BLK - 1
NBLK = E + NOVF
EPS = 1e-6
BIG = 1e30
RING = 3
UNIT = 4096
ARENA = 17760
BIASW = T + (TT - 1) * P


def constants():
    f = np.float32
    i = np.arange(P)
    col = i[:, None]
    row = i[None, :]
    t = {}
    t["ident"] = np.eye(P, dtype=f)
    t["upto"] = (col <= row).astype(f)
    t["from"] = (col >= row).astype(f)
    t["before"] = (col < row).astype(f)
    t["one"] = np.ones((P, 1), f)
    group_row = (i % 32 == 0).astype(f)[:, None]
    t["sum_two"] = np.concatenate([group_row, (i % 32 == 1).astype(f)[:, None]], axis=1)
    t["window"] = np.concatenate([np.where(row >= col, 0, BIG), np.zeros((P, P)), np.where(row <= col, 0, BIG),
                                  np.zeros((P, CTX))], axis=1).astype(f)
    tok = np.arange(T)
    r, c = (tok // 64).astype(f)[:, None], (tok % 64).astype(f)[:, None]

    def tiles(a):
        return a.reshape(TT, P, -1).transpose(1, 0, 2).reshape(P, -1).astype(f)

    inv = (f(10000.0) ** (-np.arange(0, 32, 2, dtype=f) / f(32))).astype(f)[None]
    ar, ac = r * inv, c * inv
    rope1 = tiles(np.concatenate([np.cos(ar), np.cos(ar), np.cos(ac), np.cos(ac)], 1)), tiles(np.concatenate(
        [-np.sin(ar), np.sin(ar), -np.sin(ac), np.sin(ac)], 1))
    inv = (f(10000.0) ** (-np.arange(16, dtype=f) / f(16))).astype(f)[None]
    a = np.concatenate([r * inv, c * inv], 1)
    t["cos2"] = tiles(np.concatenate([np.cos(a), np.cos(a)], 1))
    t["sin2"] = tiles(np.concatenate([-np.sin(a), np.sin(a)], 1))
    t["eps"] = np.full((P, 1), EPS, f)
    t["zero"] = np.zeros((P, 1), f)
    t["low"] = (i < 64).astype(f)[:, None]
    t["high"] = (i >= 64).astype(f)[:, None]
    e = np.arange(E)
    t["expert"] = np.tile(e, (P, 1)).astype(f)
    t["group"] = np.tile(e // EG, (P, 1)).astype(f)
    t["blocks_on"] = np.tile(E - 1 - e, (P, 1)).astype(f)
    t["block"] = np.tile(np.arange(NBLK), (P, 1)).astype(f)
    t["place"] = np.tile(np.arange(BLK), (P, 1)).astype(f)
    t["token1"] = (tok.reshape(TT, P).T + 1).astype(f)
    t["choice1"] = (2 * tok.reshape(TT, P).T[:, :, None] + np.arange(2) + 1).reshape(P, 2 * TT).astype(f)
    t["half2"] = (i // BLK - 2).astype(f)[:, None]
    at, out = {}, []
    for k, v in t.items():
        at[k] = (sum(x.shape[1] for x in out), v.shape[1])
        out.append(v.astype(f))
    return at, np.ascontiguousarray(np.concatenate(out, axis=1)), np.ascontiguousarray(np.concatenate(rope1, axis=1))


def distance_tables():
    off = np.abs(np.arange(P)[:, None] - (np.arange(BIASW)[None] - (TT - 1) * P))
    seen = (off <= 64).astype(np.int64) + ((off <= 256) & (off % 4 == 0)) + (off % 16 == 0)
    log = np.where(seen > 0, np.log(np.maximum(seen, 1)), -BIG)
    slope = 2.0 ** (-np.arange(1, H + 1))
    return (slope[:, None, None] * off[None] - log[None]).astype(np.float32)


class Steps:

    def __init__(self, sem, keys):
        self.sem, self.at, self.done = sem, {k: n + 1 for n, k in enumerate(keys)}, 0

    def tick(self, ins, key):
        self.done += 1
        assert self.at[key] == self.done, (key, self.done)
        ins.then_inc(self.sem, 1)

    def wait(self, eng, key):
        eng.wait_ge(self.sem, self.at[key])


class Chain:

    def __init__(self, sem):
        self.sem, self.n = sem, 0

    def link(self, eng, ins):
        self.n += 1
        ins.then_inc(self.sem, 1)
        eng.wait_ge(self.sem, self.n)


class Banks:

    def __init__(self, banks, sems):
        self.banks, self.sems, self.order, self.at = banks, sems, [], {}
        self.opened = 0

    def plan(self, key, freed):
        self.at[key] = len(self.order)
        self.order.append((key, freed))

    def open(self, pe, key):
        n = self.at[key]
        assert n == self.opened, (key, n, self.opened)
        self.opened += 1
        if n >= 8:
            steps, step = self.order[n - 8][1]
            steps.wait(pe, step)
        return self.banks[n % 8]

    def close(self, ins, key):
        ins.then_inc(self.sems[self.at[key] % 8], 1)

    def filled(self, eng, key):
        n = self.at[key]
        eng.wait_ge(self.sems[n % 8], n // 8 + 1)
        return self.banks[n % 8]



def two_blocks(nc, consts_d, rope1_d, dist_d, h_d, y_d, inp, out):
    ctx = ExitStack()
    with ctx:
        cols, _, _ = constants()
        ncols = sum(w for _, w in cols.values())

        def sb(name, shape, dt=F32):
            return ctx.enter_context(nc.sbuf_tensor(name, shape, dt))

        def sem(name):
            return ctx.enter_context(nc.semaphore(name))

        def steps(name, keys):
            return Steps(sem(name), list(keys))

        def wide(v, n):
            return v.unsqueeze(len(v.shape)).broadcast_to(list(v.shape) + [n])

        const = sb("const", [P, ncols])

        def C(name, parts=P):
            a, w = cols[name]
            return const[0:parts, a:a + w]

        ident = C("ident")
        x = sb("x_res", [P, TT, D])
        hT = sb("hT", [P, KT, T])
        hTc = sb("hTc", [P, KT, CTX])
        xn = sb("xn", [P, AT, D])
        ring = sb("ring", [P, RING, UNIT])
        gains = sb("gains", [P, 6, KT])
        convw = sb("convw", [P, 224])
        ada_bias = sb("ada_bias", [P, 6, KT])
        cvec = sb("cvec", [P, 2, KT])
        csilu = sb("csilu", [P, KT, 32])
        mod = sb("mod", [P, 6, KT, 2])
        mod_gain = sb("mod_gain", [P, 3, KT])
        gates = sb("gates", [P, 2, D])
        dt_bias, a_log = sb("dt_bias", [P, 16]), sb("a_log", [P, 16])
        d_skip, sinks, route_bias = sb("d_skip", [P, 8]), sb("sinks", [P, 8]), sb("route_bias", [P, 36])
        route_w = sb("route_w", [P, KT, 36])
        sums, roots, rstd = sb("sums", [P, 12]), sb("roots", [P, 12]), sb("rstd", [P, 12])
        head_sum, head_root = sb("head_sum", [P, 2, 8]), sb("head_root", [P, 2, 8])
        nmin, psums, rsums = sb("nmin", [P, 96]), sb("psums", [P, 96]), sb("rsums", [P, 96])
        win_min, sink_exp = sb("win_min", [P, 72]), sb("sink_exp", [P, 32])
        arena = sb("arena", [P, ARENA])

        def carve(start, *shape, of=arena):
            n = int(np.prod(shape))
            v = of[:, start:start + n]
            names = "abcd"[:len(shape)]
            if len(shape) > 1:
                v = v.rearrange(f"p ({' '.join(names)}) -> p {' '.join(names)}",
                                **{k: s for k, s in zip(names[1:], shape[1:])})
            return v

        def packed(size_of, start=0, of=arena, limit=ARENA):
            views = []
            for shape in size_of:
                views.append(carve(start, *shape, of=of))
                start += int(np.prod(shape))
            assert start <= limit, start
            return views

        hT_flat = hT[:, :, :].rearrange("p j n -> p (j n)")
        hTc_flat = hTc[:, :, :].rearrange("p j n -> p (j n)")
        spare = xn[:, TT:AT, :].rearrange("p t n -> p (t n)")

        vA, vB, pj, sq, qaT, qbT, kzA, kzB, dist, rope1, head_gain = packed(
            [(TT, 128), (TT, 512), (3, 512), (2, 512), (4, T), (4, T), (2, T), (8, T), (2, BIASW), (2, TT, HD),
             (4, HD)])
        junk1, rope_t = carve(0, D, of=spare), carve(D, 2, 512, of=spare)
        probs, probsT = packed([(2, T), (2, T)], of=hTc_flat, limit=2048)
        modrow = sq
        conv_rows = carve(0, 3, P, of=hT_flat)
        hid, conv_g, conv_v = packed([(FT, T), (2, T), (2, T)])
        zs, u, kvd, q2, xs_tok, b_tok = packed(
            [(TT, 512), (KT, T + CTX), (AT, 272), (TT, 512), (AT, 512), (AT, 256)])
        junk2 = carve(0, D)
        conv2 = carve(0, 2, T + CTX, of=spare)
        u_flat = carve(TT * 512, 4 * (T + CTX))
        slot = ring[:, 1, :]
        q2T, kz2 = carve(0, 4, T, of=slot), carve(2048, 2, T + CTX, of=slot)
        rope_q = carve(0, 2, 512, of=hTc_flat)
        wprobs = carve(TT * 512 + KT * (T + CTX) + AT * 272, 2, 640)
        wprobsT = carve(16480, 2, 640)
        state = carve(0, 2, 4, 512, of=hT_flat)
        state0, dtxw = packed([(2, 512), (2, 512)], of=hTc_flat, limit=2048)
        dtx, cbm, ytmp = packed([(2, 512), (2, 2, P), (512,)], of=spare, limit=2048)
        decay = u_flat[:, 0:2048].rearrange("p (a b c) -> p a b c", a=2, b=8)
        stmp = u_flat[:, 2048:2560]
        sm = sb("ssd_small", [P, 10, 96])
        cat = xn

        ps = [ctx.enter_context(nc.psum_tensor(f"bank{i}", [P, 512], F32)) for i in range(8)]
        banks = Banks(ps, [sem(f"bank_filled{i}") for i in range(8)])

        x_in, const_in, ctx_in = sem("x_in"), sem("const_in"), sem("ctx_in")
        dist_in = [sem("dist_in0"), sem("dist_in1")]
        unit_in = [sem(f"unit_in{i}") for i in range(RING)]
        dve_chain, act_chain, pool_chain = Chain(sem("dve_order")), Chain(sem("act_order")), Chain(sem("pool_order"))

        zero = C("zero")
        NORMS = {
            "norm1": (lambda t: x[:, t, :], TT, [(0, D)], junk1, lambda j, c: (gains[:, 0, j:j + 1], zero)),
            "mix1": (lambda t: xn[:, t, :], TT, [(0, 512), (512, D)], junk1, lambda j, c: (gains[:, 1, j:j + 1], zero)),
            "norm2": (lambda t: x[:, t, :], TT, [(0, D)], junk1, lambda j, c: (gains[:, 2, j:j + 1], zero)),
            "norm1_2": (lambda t: x[:, t, :] if t < TT else xn[:, t, :], AT, [(0, D)], junk2,
                        lambda j, c: (mod_gain[:, c, j:j + 1], mod[:, 0, j, c:c + 1])),
            "mix2": (lambda t: cat[:, t, :], TT, [(0, 512)], u_flat[:, 0:D], lambda j, c: (gains[:, 4, j:j + 1], zero)),
            "norm2_2": (lambda t: x[:, t, :], TT, [(0, D)], hTc_flat[:, 0:D],
                        lambda j, c: (mod_gain[:, 2, j:j + 1], mod[:, 3, j, 0:1])),
        }
        norm_keys = [(s, t, a) for s, (_, n, parts, _, _) in NORMS.items() for t in range(n) for a, _ in parts]
        squared = steps("norm_squared", norm_keys + [("final", t, 0) for t in range(TT)])
        rooted = steps("norm_rooted", list(NORMS) + ["final"])
        normed = steps("normed", norm_keys)

        def halves(s):
            return [(s, j, c) for j in range(KT) for c in range(2 if s == "norm1_2" else 1)]

        hT_act = steps("hT_by_act", [k for s in NORMS for k in halves(s) if k[1] % 2 == 0])
        hT_dve = steps("hT_by_dve", [k for s in NORMS for k in halves(s) if k[1] % 2 == 1])

        def hT_step(k):
            return hT_act if k[1] % 2 == 0 else hT_dve

        PROJ = [(c, t) for c in range(5) for t in range(TT)]
        HEADS_OF = [[(0, 8, 0)], [(0, 2, 1), (4, 4, 2)], [(0, 4, 2), (4, 4, 3)], [(0, 4, 3)]]
        conv_ready = steps("conv_weights", ["taps"])
        pj_ready = steps("proj_copied", range(16))
        v_tail = steps("v_tail", range(TT))
        head_summed = steps("head_summed", range(16))
        head_rooted = steps("head_rooted", range(16))
        qk_ready = steps("qk_normed", range(16))
        qk_drained = steps("qk_transposed", range(16))

        NU = 2 * H * TT
        score_min = steps("score_min", range(NU))
        prob = steps("prob", range(NU))
        pt_act = steps("probsT_by_act", range(0, NU, 2))
        pt_dve = steps("probsT_by_dve", range(1, NU, 2))
        att = steps("attended", range(NU))
        mod_silu = steps("mod_silu", ["c"])
        mod_copied = steps("mod_copied", range(12))
        mod_done = steps("mod_done", list(range(12)) + ["gains"])

        def pt_step(i):
            return pt_dve if i % 2 else pt_act

        SIDES = [(t, n) for t in range(TT) for n in range(2)]
        x1 = steps("x_after_attention", SIDES)
        tap_mid = steps("conv_middle_tap", [(f, g) for f in range(FT) for g in range(2)])
        tapped = steps("conv_tapped", [(f, g) for f in range(FT) for g in range(2)])
        gelued = steps("gelued", range(FT))
        hidden = steps("hidden", range(FT))
        down_read = steps("down_weights_read", range(5))
        x2 = steps("x_after_ffn", SIDES)

        kvd_copied = steps("kv_dt_copied", range(AT))
        XBC = [(m, c) for m in range(KT) for c in range(2)]
        mid2 = steps("conv2_middle_tap", XBC)
        tapped2 = steps("conv2_tapped", XBC)
        u_ready = steps("conv2_silu", range(KT))
        z_ready = steps("z_silu", range(TT))
        q_copied = steps("q_copied", range(TT))
        roped = steps("roped", [("k", t) for t in range(TT)] + [("q", t) for t in range(TT)])
        tok_copied = steps("tokens_first", [("xs", t) for t in range(AT)] + [("b", t) for t in range(0, AT, 2)])
        kz_ready = steps("k_transposed", range(2))
        q2_ready = steps("q_transposed", range(4))
        csilu_cleared = steps("csilu_cleared", [0])
        row_ready = sem("row_ready")
        dt_abs, dt_exp, dt_log = steps("dt_abs", [0, 1]), steps("dt_exp", [0]), steps("dt_log", [0])
        a_exp = steps("a_exp", [0])
        dta_ready = steps("dt_times_a", [0])
        cs_copied = steps("cumsums", [0])
        cs_exp = steps("cumsum_exps", [0])
        sw_ready = steps("state_weights", [0])

        TILE_AT = [[TT, TT + 1, 0, 1, 2, 3], [TT + 1, TT, 3, 2, 1, 0]]
        STATES = [(d, i) for i in range(5) for d in range(2)]
        NW = H * TT
        YS = [(t, d) for t in range(TT) for d in range(2)]
        ssd = [("state", k) for k in range(len(STATES))] + [("y", k) for k in range(len(YS) + 1)]
        weave, n = [], 0
        for i in range(NW + 2):
            weave.append(("win", i))
            while n * (NW + 2) < len(ssd) * (i + 1) and n < len(ssd):
                weave.append(ssd[n])
                n += 1
        dtxw_ready = steps("weighted_x", range(len(STATES)))
        state_ready = steps("state_ready", range(len(STATES)))
        dtx_ready = steps("dt_x", range(len(YS)))
        cb_masked = steps("cb_masked", range(TT))
        seg_ready = steps("segments", [(k, g) for k in range(len(YS)) for g in range(2)])
        decayed = steps("decay_exp", range(len(YS)))
        m_ready = steps("decay_times_cb", range(len(YS)))
        y_read = steps("y_read", [(k, w) for k in range(len(YS)) for w in ("off", "diag")] )
        y_done = steps("y_done", range(TT))
        wscore = steps("win_score", range(NW))
        wprob = steps("win_prob", range(NW))
        wpt_act = steps("win_probsT", range(NW))
        watt = steps("win_attended", range(NW))
        x3 = steps("x_after_mixers", SIDES)

        def near(t):
            return max(0, t - 1), min(TT - 1, t + 1)

        banks.plan("conv_weights", (conv_ready, "taps"))

        def plan_norm(s):
            for k in halves(s):
                banks.plan(("hT",) + k, (hT_step(k), k))

        plan_norm("norm1")
        for n in range(len(PROJ) + 2):
            if n < len(PROJ):
                banks.plan(("proj", n), (pj_ready, n) if n < 16 else (v_tail, n - 16))
            if 2 <= n < 18:
                banks.plan(("qkT", n - 2), (qk_drained, n - 2))
        for i in range(NU + 2):
            if i < NU:
                banks.plan(("score", i), (prob, i) if i < NU // 2 else (score_min, i))
            if 1 <= i <= NU:
                banks.plan(("probsT", i - 1), (pt_step(i - 1), i - 1))
            if i >= 2:
                banks.plan(("att", i - 2), (att, i - 2))
            if i % 5 == 2 and i // 5 < 12:
                banks.plan(("modrow", i // 5), (mod_copied, i // 5))
            if i % 5 == 4 and i // 5 < 12:
                banks.plan(("mod", i // 5), (mod_done, i // 5))
        plan_norm("mix1")
        for k in SIDES:
            banks.plan(("out1",) + k, (x1, k))
        plan_norm("norm2")
        for f in range(FT):
            for g in range(2):
                banks.plan(("up", f, g), (tapped, (f, g)))
        for k in SIDES:
            banks.plan(("down",) + k, (x2, k))
        plan_norm("norm1_2")
        for t in range(AT):
            banks.plan(("kvd", t), (kvd_copied, t))
        for k in XBC:
            banks.plan(("xbc",) + k, (tapped2, k))
        for t in range(TT):
            banks.plan(("z", t), (z_ready, t))
        for t in range(TT):
            banks.plan(("q2", t), (q_copied, t))
        banks.plan("cumsum", (cs_copied, 0))
        for t in range(AT):
            banks.plan(("xs", t), (tok_copied, ("xs", t)))
        for t in range(0, AT, 2):
            banks.plan(("b", t), (tok_copied, ("b", t)))
        for n in range(2):
            banks.plan(("kT", n), (kz_ready, n))
        for j in range(4):
            banks.plan(("q2T", j), (q2_ready, j))
        for what, i in weave:
            if what == "win":
                if i < NW:
                    banks.plan(("wscore", i, 0), (wscore, i))
                    banks.plan(("wscore", i, 1), (wscore, i))
                if 1 <= i <= NW:
                    banks.plan(("wprobsT", i - 1, 0), (wpt_act, i - 1))
                    banks.plan(("wprobsT", i - 1, 1), (wpt_act, i - 1))
                if i >= 2:
                    banks.plan(("watt", i - 2), (watt, i - 2))
            elif what == "state":
                banks.plan(("state", i), (state_ready, i))
            else:
                if i < len(YS):
                    if i % 2 == 0:
                        banks.plan(("cb", i // 2), (cb_masked, i // 2))
                    banks.plan(("seg", i, 0), (seg_ready, (i, 0)))
                    banks.plan(("seg", i, 1), (seg_ready, (i, 1)))
                if i >= 1:
                    banks.plan(("yoff", i - 1), (y_read, (i - 1, "off")))
                    banks.plan(("ydiag", i - 1), (y_read, (i - 1, "diag")))
        plan_norm("mix2")
        for k in SIDES:
            banks.plan(("out2",) + k, (x3, k))
        plan_norm("norm2_2")

        def by_k(name):
            return inp[name].rearrange("(p j) n -> p j n", j=KT)

        win_v, wout_v, wup_v = by_k("w_in"), by_k("w_out"), by_k("w_up")
        wada_v = inp["w_ada_2"].rearrange("a (p j) n -> p (a j) n", j=KT)
        win2_v = inp["w_in_2"].rearrange("a (p j) n -> p (a j) n", j=KT)
        wout2_v = inp["w_out_2"].rearrange("a (p j) n -> p (a j) n", j=KT)
        wdown_v = inp["w_down"].rearrange("(f p) n -> p f n", p=P)
        UNITS = []

        def unit(key, width, parts, free):
            UNITS.append((key, width, parts, free))

        for c in range(5):
            w = min(512, W1 - c * 512)
            unit(("w_in", c), w, [(0, win_v[:, :, c * 512:c * 512 + w])], ("proj", c * TT + TT - 1))
        for m in range(12):
            unit(("w_ada", m), 512, [(0, wada_v[:, :, m * 512:m * 512 + 512])], ("modrow", m))
        for n in range(2):
            unit(("w_out", n), 512, [(0, wout_v[:, :, n * 512:n * 512 + 512])], ("out1", TT - 1, n))
        for f in range(0, FT, 2):
            unit(("w_up", f), 512, [(0, wup_v[:, :, f * P:f * P + 256]),
                                    (256, wup_v[:, :, DFF + f * P:DFF + f * P + 256])], ("up", f + 1, 1))
        for i in range(6):
            nf = min(4, FT - 4 * i)
            unit(("w_down", i), D, [(0, wdown_v[:, 4 * i:4 * i + nf, :])],
                 ("down_read", i) if i < 5 else ("down", TT - 1, 1))
        unit("w_kvd", 272, [(0, win2_v[:, :, 1536:1552]), (16, win2_v[:, :, 2064:2320])], ("kvd", AT - 1))
        for n in range(2):
            unit(("w_xbc", n), 512, [(0, win2_v[:, :, 512 + n * 512:1024 + n * 512])], ("xbc", 4 * n + 3, 1))
        unit("w_z", 512, [(0, win2_v[:, :, 0:512])], ("z", TT - 1))
        unit("w_q", 512, [(0, win2_v[:, :, 1552:2064])], ("q2", TT - 1))
        for n in range(2):
            unit(("w_out2", n), 512, [(0, wout2_v[:, :, n * 512:n * 512 + 512])], ("out2", TT - 1, n))
        UNIT_AT, count = {}, [0] * RING
        for n, (key, width, parts, _) in enumerate(UNITS):
            count[n % RING] += 16 * len(parts)
            UNIT_AT[key] = (n % RING, width, count[n % RING])
        assert UNIT_AT["w_q"][0] == 1 and UNIT_AT[("w_out2", 0)][0] == 2

        def unit_view(n, width, rows):
            return ring[:, n, 0:rows * width].rearrange("p (j n) -> p j n", n=width)

        def weights(pe, key):
            n, width, value = UNIT_AT[key]
            pe.wait_ge(unit_in[n], value)
            return unit_view(n, width, UNIT // width if width != 272 else KT)

        EXPERT_SLOTS = [ring[:, i, :] for i in range(3)] + [arena[:, i * UNIT:(i + 1) * UNIT] for i in range(3)]
        (hot_p, hot_b, lg, gl, g8, e8, el, ohot, osum, rank, quo, plc, blk, prod, wide_e, cnt, novf, start, later,
         pk, bk, gexp, gsum, wts, tval) = packed(
            [(8, P), (8, 2, NBLK), (TT, 36), (TT, 8), (TT, 8), (TT, 8), (TT, E), (TT, 2, E), (TT, E), (TT, E),
             (TT, E), (TT, E), (TT, E), (TT, 2, E), (3, E), (E,), (E,), (2, E), (NOVF, E), (8,), (8,), (TT, 4),
             (TT,), (TT, 6), (3, 2 * NBLK)], start=3 * UNIT)
        gi, ei = sb("group_index", [P, TT, 8], U32), sb("expert_index", [P, TT, 8], U32)
        gif, eif = sb("group_index_f", [P, TT]), sb("expert_index_f", [P, TT, 2])
        tok_of, row_of = sb("token_of_place", [P, NBLK], I32), sb("row_of_place", [P, NBLK], I32)
        later_cnt = sb("later_counts", [P, 16])
        ovf = sb("later_blocks", [1, NOVF + 1], I32)
        tok_at, row_at = sb("token_index", [P, 2], I32), sb("row_index", [P, 2], I32)
        xg = carve(0, 2, D, of=spare)
        xT, gu = packed([(2, KT, BLK), (2, 512)], of=hTc_flat, limit=2048)
        sg, hidE, yE = packed([(2, 4, BLK), (2, 4, BLK), (2, 512)], of=hT_flat, limit=KT * T)
        final_gain = carve(0, D, of=xn[:, 0:1, :].rearrange("p a n -> p (a n)"))
        junk3 = carve(0, D, of=xn[:, 1:2, :].rearrange("p a n -> p (a n)"))
        y01 = ring[:, 0:2, :].rearrange("p a n -> p (a n)").rearrange("p (t k n) -> p t k n", t=TT, k=2)
        expert_in = [sem(f"expert_in{i}") for i in range(6)]
        h_stored, y01_in, final_in, stored = sem("h_stored"), sem("y01_in"), sem("final_gain_in"), sem("stored")
        tokens_in = [sem("tokens_in0"), sem("tokens_in1")]
        y_stored = [sem("y_stored0"), sem("y_stored1")]
        index_ready, scattered = sem("index_ready"), sem("all_y_stored")
        xt_filled, xt_scaled, xt_ready = sem("expert_x_filled"), sem("expert_x_scaled"), sem("expert_x_ready")
        gu_filled, gu_ready = sem("gate_up_filled"), sem("gate_up_ready")
        ht_filled, silu_ready, hid_ready = sem("hiddenT_filled"), sem("expert_silu"), sem("expert_hidden")
        y_filled, y_ready = sem("expert_y_filled"), sem("expert_y_ready")
        route = steps("route", ["logits", "max", "top2", "weights", "hot", "counts", "places", "table"])
        route_act = steps("route_act", ["group_exp", "pair_exp"])
        route_pe = steps("route_pe", ["logits", "rank", "table"])
        final_x = steps("final_x", range(TT))
        final_y = steps("final_y", range(TT))

        small_loads = []

        def small(dst, src):
            small_loads.append((dst, src))

        small(const[:, :], consts_d)
        small(rope1.rearrange("p a t d -> p (a t d)"), rope1_d)
        for n, name in ((0, "norm1_g"), (2, "norm2_g")):
            small(gains[:, n, :], inp[name].rearrange("(p j) -> p j", j=KT))
        small(gains[0:64, 1, :], inp["outa_norm_g"].rearrange("(p j) -> p j", j=KT))
        small(gains[64:128, 1, :], inp["outb_norm_g"].rearrange("(p j) -> p j", j=KT))
        small(gains[:, 3, :], inp["norm1_2"].rearrange("a (p j) -> p (a j)", j=KT))
        small(gains[0:64, 4, :], inp["ssd_norm_2"].rearrange("a (p j) -> p (a j)", j=KT))
        small(gains[:, 5, :], inp["norm2_2"].rearrange("a (p j) -> p (a j)", j=KT))
        for n, name in enumerate(("qa_norm_g", "ka_norm_g", "qb_norm_g", "kb_norm_g")):
            small(head_gain[:, n, :], inp[name].partition_broadcast(P))
        small(conv_rows[0:88, 0, :], inp["conv_w"][0:2, :].rearrange("k (f p) -> (k f) p", p=P))
        small(conv_rows[0:44, 1, :], inp["conv_w"][2, :].rearrange("(f p) -> f p", p=P))
        small(conv_rows[44:88, 1, :], inp["conv_b"].rearrange("(f p) -> f p", p=P))
        small(conv_rows[0:40, 2, :], inp["conv_w_2"].rearrange("a k (f p) -> (a k f) p", p=P))
        small(conv_rows[40:48, 2, :], inp["conv_b_2"].rearrange("a (f p) -> (a f) p", p=P))
        small(ada_bias[:, :, :], inp["b_ada_2"].rearrange("a (s p j) -> p (a s) j", s=6, j=KT))
        small(cvec[:, 0, :], inp["c_2"].rearrange("a (p j) -> p (a j)", j=KT))
        small(cvec[:, 1, :], inp["c_ctx_2"].rearrange("(p j) -> p j", j=KT))
        small(gates[:, 0, :], inp["b_ada_2"][0, 2 * D:3 * D].partition_broadcast(P))
        small(gates[:, 1, :], inp["b_ada_2"][0, 5 * D:6 * D].partition_broadcast(P))
        small(dt_bias[:, :], inp["dt_bias_2"].rearrange("a d h -> (a d h)").partition_broadcast(P))
        small(a_log[:, :], inp["a_log_2"].rearrange("a d h -> (a d h)").partition_broadcast(P))
        small(d_skip[:, :], inp["d_skip_2"].rearrange("a h -> (a h)").partition_broadcast(P))
        small(sinks[:, :], inp["attn_sinks_2"].rearrange("a h -> (a h)").partition_broadcast(P))
        small(route_bias[:, 0:4], inp["b_group_2"].rearrange("a h -> (a h)").partition_broadcast(P))
        small(route_bias[:, 4:36], inp["b_expert_2"].rearrange("a h -> (a h)").partition_broadcast(P))
        small(route_w[:, :, 0:4], inp["w_group_2"].rearrange("a (p j) n -> p (a j) n", j=KT))
        small(route_w[:, :, 4:36], inp["w_expert_2"].rearrange("a (p j) n -> p (a j) n", j=KT))
        CONST_ALL = 16 * len(small_loads)
        block = ctx.enter_context(nc.Block())

        def held(eng, value):
            return value if isinstance(value, int) else eng.to_reg(value)

        def load_expert(sp, e, par, kpar, reuse):
            for i, (name, pat) in enumerate((("w_gate_2", "a e (p j) f -> (a e) p (j f)"),
                                             ("w_up_2", "a e (p j) f -> (a e) p (j f)"),
                                             ("w_down_2", "a e (p f) d -> (a e) p (f d)"))):
                kw = {"f": 4} if i == 2 else {"j": KT}
                if reuse is not None:
                    sp.wait_ge(gu_filled if i < 2 else y_filled, reuse)
                sp.dma_start(EXPERT_SLOTS[3 * par + i], inp[name].rearrange(pat, **kw)[e]).then_inc(
                    expert_in[3 * par + i], 16)

        @block.sync
        def _(sp):
            sp.dma_start(x[:, :, :], inp["x"].rearrange("a (t p) n -> p (a t) n", p=P)).then_inc(x_in, 16)
            for n, (key, width, parts, _) in enumerate(UNITS):
                if key == "w_kvd":
                    squared.wait(sp, ("norm2", TT - 1, 0))
                    sp.dma_start(xn[:, TT:AT, :], inp["ctx_2"].rearrange("a (t p) n -> p (a t) n", p=P)).then_inc(
                        ctx_in, 16)
                if n >= RING:
                    free = UNITS[n - RING][3]
                    if free[0] == "down_read":
                        down_read.wait(sp, free[1])
                    else:
                        banks.filled(sp, free)
                for c, src in parts:
                    rows, w = src.shape[1], src.shape[2]
                    sp.dma_start(unit_view(n % RING, width, rows)[:, :, c:c + w], src).then_inc(unit_in[n % RING], 16)
            banks.filled(sp, ("out2", TT - 1, 1))
            load_expert(sp, 0, 0, 0, None)
            x3.wait(sp, SIDES[-1])
            load_expert(sp, 1, 1, 0, None)
            normed.wait(sp, ("norm2_2", TT - 1, 0))
            sp.dma_start(h_d.rearrange("(t p) n -> p t n", p=P), xn[:, 0:TT, :]).then_inc(h_stored, 16)
            with sp.Fori(1, E // 2) as it:
                for par in range(2):
                    load_expert(sp, 2 * it + par, par, it, 2 * it + par - 1)
            route.wait(sp, "table")
            later_n = sp.value_load(ovf[0:1, NOVF:NOVF + 1], min_val=0, max_val=NOVF)
            with sp.If(later_n > 0):
                with sp.Fori(0, later_n) as i:
                    e = sp.value_load(ovf[0:1, bass.ds(i, 1)], min_val=0, max_val=E - 1)
                    load_expert(sp, e, 0, i + E // 2, i + E)
            sp.wait_ge(h_stored, 16)
            sp.dma_start(final_gain, inp["norm_final_2"].partition_broadcast(P)).then_inc(final_in, 16)
            sp.wait_ge(scattered, 1)
            sp.dma_start(y01[:, :, :, :].rearrange("p t k n -> p t (k n)"),
                         y_d.rearrange("(t p r) n -> p t (r n)", p=P, r=4)).then_inc(y01_in, 16)
            for t in range(TT):
                final_y.wait(sp, t)
                sp.dma_start(out[0, t * P:(t + 1) * P, :], y01[:, t, 0, :]).then_inc(stored, 16)
            sp.wait_ge(stored, 16 * TT)

        @block.gpsimd
        def _(pool):
            g = nc.gpsimd
            for h in range(H):
                if h >= 2:
                    score_min.wait(pool, (H + h - 1) * TT - 1)
                pool.dma_start(dist[:, h % 2, :], dist_d[h]).then_inc(dist_in[h % 2], 16)
            pool.wait_ge(const_in, CONST_ALL)
            banks.filled(pool, ("q2", 0))

            def rope(dst, src, heads, t):
                a, b = (rope_q[:, i, 0:heads * HD] for i in range(2))
                cos, sin = (C(n).rearrange("p (t d) -> p t d", t=TT)[:, t, :] for n in ("cos2", "sin2"))
                s3 = src.rearrange("p (h d) -> p h d", d=HD)
                a3, b3 = (v.rearrange("p (h d) -> p h d", d=HD) for v in (a, b))
                g.tensor_tensor(a3, s3, cos.unsqueeze(1).broadcast_to([P, heads, HD]), ALU.mult)
                for half in range(2):
                    lo, other = half * 32, 32 - half * 32
                    last = g.tensor_tensor(b3[:, :, lo:lo + 32], s3[:, :, other:other + 32],
                                           sin[:, lo:lo + 32].unsqueeze(1).broadcast_to([P, heads, 32]), ALU.mult)
                pool_chain.link(pool, last)
                return a, b

            for t in range(TT):
                kvd_copied.wait(pool, t)
                k = kvd[:, t, 16:144]
                a, b = rope(k, k, 2, t)
                ins = g.tensor_tensor(k, a, b, ALU.add)
                roped.tick(ins, ("k", t))
                roped.wait(pool, ("k", t))
            for t in range(TT):
                q_copied.wait(pool, t)
                a, b = rope(q2[:, t, :], q2[:, t, :], H, t)
                dst = q2[:, t, :].rearrange("p (j half d) -> p half j d", j=4, half=2)
                ins = g.tensor_tensor(dst, a.rearrange("p (half j d) -> p half j d", j=4, half=2),
                                      b.rearrange("p (half j d) -> p half j d", j=4, half=2), ALU.add)
                roped.tick(ins, ("q", t))
                roped.wait(pool, ("q", t))
            sw_ready.wait(pool, 0)
            u_ready.wait(pool, KT - 1)
            for what, k in weave:
                if what == "state":
                    d, i = STATES[k]
                    t = TILE_AT[d][i]
                    tok_copied.wait(pool, ("xs", t))
                    if k >= 2:
                        banks.filled(pool, ("state", k - 2))
                    ins = g.tensor_tensor(dtxw[:, k % 2, :].rearrange("p (h d) -> p h d", d=HD),
                                          xs_tok[:, t, :].rearrange("p (h d) -> p h d", d=HD),
                                          wide(sm[:, 9, t * 16 + d * 8:t * 16 + d * 8 + 8], HD), ALU.mult)
                    dtxw_ready.tick(ins, k)
                elif what == "y" and k < len(YS):
                    t, d = YS[k]
                    if k >= 2:
                        banks.filled(pool, ("ydiag", k - 2))
                    ins = g.tensor_tensor(dtx[:, k % 2, :].rearrange("p (h d) -> p h d", d=HD),
                                          xs_tok[:, t, :].rearrange("p (h d) -> p h d", d=HD),
                                          wide(sm[:, 5, t * 16 + d * 8:t * 16 + d * 8 + 8], HD), ALU.mult)
                    dtx_ready.tick(ins, k)
            x3.wait(pool, SIDES[-1])
            pool_chain.link(pool, g.memset(xg, 0.0))
            route.wait(pool, "table")
            pool.wait_ge(h_stored, 16)

            def gather(n, e, par, reuse):
                if reuse is not None:
                    pool.wait_ge(xt_filled, reuse)
                g.tensor_copy(tok_at[:, par:par + 1], tok_of[:, bass.ds(e, 1)]).then_inc(index_ready, 1)
                after = held(pool, n + 1)
                pool.wait_ge(const_in, CONST_ALL)
                pool.wait_ge(index_ready, after)
                g.indirect_dma_start(xg[0:BLK, par, :], None, h_d, bass.IndirectOffsetOnAxis(
                    ap=tok_at[0:BLK, par:par + 1], axis=0), bounds_check=T - 1, oob_is_err=False).then_inc(
                        tokens_in[par], 16)

            def scatter(n, e, par, stored_before):
                if stored_before is not None:
                    pool.wait_ge(y_stored[par], stored_before)
                g.tensor_copy(row_at[:, par:par + 1], row_of[:, bass.ds(e, 1)]).then_inc(row_ready, 1)
                after = held(pool, n + 1)
                pool.wait_ge(const_in, CONST_ALL)
                pool.wait_ge(row_ready, after)
                pool.wait_ge(y_ready, after)
                g.indirect_dma_start(y_d, bass.IndirectOffsetOnAxis(ap=row_at[:, par:par + 1], axis=0),
                                     yE[:, par, :], None, bounds_check=4 * T - 1, oob_is_err=False).then_inc(
                                         y_stored[par], 16)

            gather(0, 0, 0, None)
            gather(1, 1, 1, None)
            scatter(0, 0, 0, None)
            with pool.Fori(1, E // 2) as it:
                gather(2 * it, 2 * it, 0, 2 * it - 1)
                pool.wait_ge(y_stored[0], 16 * it)
                scatter(2 * it - 1, 2 * it - 1, 1, None)
                gather(2 * it + 1, 2 * it + 1, 1, 2 * it)
                pool.wait_ge(y_stored[1], 16 * it)
                scatter(2 * it, 2 * it, 0, None)
            scatter(E - 1, E - 1, 1, 16 * (E // 2 - 1))
            pool.wait_ge(y_stored[0], 16 * (E // 2))
            pool.wait_ge(y_stored[1], 16 * (E // 2))
            later_n = pool.value_load(ovf[0:1, NOVF:NOVF + 1], min_val=0, max_val=NOVF)
            with pool.If(later_n > 0):
                with pool.Fori(0, later_n) as i:
                    gather(i + E, i + E, 0, i + E)
                    scatter(i + E, i + E, 0, None)
                    pool.wait_ge(y_stored[0], 16 * i + 16 * (E // 2 + 1))
            g.memset(tok_at[:, 0:1], 0).then_inc(scattered, 1)

        @block.scalar
        def _(act):
            s = nc.scalar
            for dst, src in small_loads:
                act.dma_start(dst, src).then_inc(const_in, 16)
            act.wait_ge(const_in, CONST_ALL)
            eps = C("eps")

            def root(dst, src, width):
                return s.activation(dst, src, ACT.Sqrt, scale=1.0 / width, bias=eps)

            def norm(name, before=None):
                src, n, parts, junk, gain = NORMS[name]
                i = 0
                for t in range(n):
                    if before is not None:
                        before(t)
                    for a, b in parts:
                        if i:
                            squared.wait(act, last)
                        last = (name, t, a)
                        squared.tick(s.activation(junk[:, 0:b - a], src(t)[:, a:b], ACT.Square,
                                                  accum_out=sums[:, i:i + 1]), (name, t, a))
                        i += 1
                squared.wait(act, (name, n - 1, parts[-1][0]))
                rooted.tick(root(roots[:, 0:i], sums[:, 0:i], parts[0][1] - parts[0][0]), name)
                for k in halves(name):
                    if k[1] % 2 == 0:
                        _, j, c = k
                        bank = banks.filled(act, ("hT",) + k)
                        dst = hTc[:, j, :] if c else hT[:, j, :]
                        sc, sh = gain(j, c)
                        hT_act.tick(s.activation(dst, bank[:, 0:dst.shape[1]], ACT.Identity, scale=sc, bias=sh), k)

            csilu_cleared.wait(act, 0)
            s.activation(csilu[:, :, 0], cvec[:, 0, :], ACT.Silu)
            mod_silu.tick(s.activation(csilu[:, :, 1], cvec[:, 1, :], ACT.Silu), "c")
            act.wait_ge(x_in, 16)
            norm("norm1")
            low, high = C("low"), C("high")
            for n in range(18):
                if n < 16:
                    c, t = PROJ[n]
                    bank = banks.filled(act, ("proj", n))
                    if n >= 3:
                        banks.filled(act, ("qkT", n - 3))
                    if n >= 2:
                        head_summed.wait(act, n - 2)
                    if c == 1:
                        s.activation(vA[:, t, :], bank[:, 128:256], ACT.Copy)
                    if c == 3:
                        s.activation(vB[:, t, 0:256], bank[:, 256:512], ACT.Copy)
                    s.activation(pj[:, n % 3, :], bank[:, :], ACT.Copy)
                    pj_ready.tick(s.activation(sq[:, n % 2, :], bank[:, :], ACT.Square), n)
                    head_summed.wait(act, n)
                    head_rooted.tick(root(head_root[:, n % 2, :], head_sum[:, n % 2, :], HD), n)
                if n >= 2:
                    m = n - 2
                    c, t = PROJ[m]
                    bank = banks.filled(act, ("qkT", m))
                    b3 = bank[:, :].rearrange("p (j n) -> p j n", j=4)
                    at = slice(t * P, t * P + P)
                    if c == 0:
                        ins = s.activation(qaT[:, :, at], b3, ACT.Copy)
                    if c == 1:
                        s.activation(qbT[:, 0:2, at], b3[:, 2:4, :], ACT.Copy)
                        s.activation(kzA[:, 0, at], b3[:, 0, :], ACT.Copy, scale=low)
                        ins = s.activation(kzA[:, 1, at], b3[:, 0, :], ACT.Copy, scale=high)
                    if c == 2:
                        s.activation(qbT[:, 2:4, at], b3[:, 0:2, :], ACT.Copy)
                    if c >= 2:
                        keys = b3[:, 2:4, :] if c == 2 else b3[:, 0:2, :]
                        dst = kzB[:, 4 * (c - 2):4 * (c - 1), at].rearrange("p (j two) n -> p two j n", two=2)
                        s.activation(dst[:, 0, :, :], keys, ACT.Copy, scale=low)
                        ins = s.activation(dst[:, 1, :, :], keys, ACT.Copy, scale=high)
                    qk_drained.tick(ins, m)
            for i in range(NU + 2):
                if i < NU:
                    score_min.wait(act, i)
                    if i >= 2:
                        banks.filled(act, ("probsT", i - 2))
                    src = banks.filled(act, ("score", i))[:, :] if i < NU // 2 else probs[:, i % 2, :]
                    prob.tick(s.activation(probs[:, i % 2, :], src, ACT.Exp, scale=-1.0, bias=nmin[:, i:i + 1],
                                           accum_out=psums[:, i:i + 1]), i)
                if 1 <= i <= NU and (i - 1) % 2 == 0:
                    bank = banks.filled(act, ("probsT", i - 1))
                    if i >= 3:
                        banks.filled(act, ("att", i - 3))
                    pt_act.tick(s.activation(probsT[:, (i - 1) % 2, :], bank[:, :], ACT.Copy), i - 1)
                if i % 5 == 2 and i // 5 < 12:
                    m = i // 5
                    bank = banks.filled(act, ("modrow", m))
                    if m >= 2:
                        mod_done.wait(act, m - 2)
                    mod_copied.tick(s.activation(modrow[:, m % 2, :], bank[:, :], ACT.Copy), m)
            norm("mix1", lambda t: att.wait(act, NU - 1))
            norm("norm2", lambda t: x1.wait(act, (t, 1)))
            for f in range(FT + 1):
                if f < FT:
                    for gv in range(2):
                        bank = banks.filled(act, ("up", f, gv))
                        if f >= 2:
                            hidden.wait(act, f - 2)
                        ch = gv * FT + f
                        tap_mid.tick(s.activation((conv_g, conv_v)[gv][:, f % 2, :], bank[:, :], ACT.Identity,
                                                  scale=convw[:, 44 + ch:45 + ch], bias=convw[:, 132 + ch:133 + ch]),
                                     (f, gv))
                if f >= 1:
                    tapped.wait(act, (f - 1, 1))
                    y = conv_g[:, (f - 1) % 2, :]
                    gelued.tick(s.activation(y, y, ACT.Gelu_apprx_tanh), f - 1)

            def source2(t):
                if t < TT:
                    x2.wait(act, (t, 1))
                elif t == TT:
                    act.wait_ge(ctx_in, 16)

            mod_done.wait(act, "gains")
            norm("norm1_2", source2)
            for m in range(KT + 1):
                if m < KT:
                    for c in range(2):
                        bank = banks.filled(act, ("xbc", m, c))
                        n, o = (CTX, T) if c else (T, 0)
                        if m >= 2:
                            u_ready.wait(act, m - 2)
                        mid2.tick(s.activation(conv2[:, m % 2, o:o + n], bank[:, 0:n], ACT.Identity,
                                               scale=convw[:, 192 + m:193 + m], bias=convw[:, 216 + m:217 + m]), (m, c))
                if m >= 1:
                    tapped2.wait(act, (m - 1, 1))
                    u_ready.tick(s.activation(u[:, m - 1, :], conv2[:, (m - 1) % 2, :], ACT.Silu), m - 1)
            for t in range(TT):
                bank = banks.filled(act, ("z", t))
                z_ready.tick(s.activation(zs[:, t, :], bank[:, :], ACT.Silu), t)
            for t in range(TT):
                bank = banks.filled(act, ("q2", t))
                q_copied.tick(s.activation(q2[:, t, :], bank[:, :], ACT.Copy, scale=-HD ** -0.5), t)
            dt_abs.wait(act, 0)
            dt_exp.tick(s.activation(sm[:, 1, :], sm[:, 4, :], ACT.Exp, scale=-1.0), 0)
            a_exp.tick(s.activation(a_log[:, :], a_log[:, :], ACT.Exp), 0)
            dt_abs.wait(act, 1)
            dt_log.tick(s.activation(sm[:, 3, :], sm[:, 2, :], ACT.Ln), 0)
            cs_copied.wait(act, 0)
            s.activation(sm[:, 0, :], sm[:, 7, :], ACT.Exp)
            s.activation(sm[:, 1, :], sm[:, 1, :], ACT.Exp)
            cs_exp.tick(s.activation(sm[:, 8, :], sm[:, 2, :], ACT.Exp), 0)
            for t in range(AT):
                bank = banks.filled(act, ("xs", t))
                tok_copied.tick(s.activation(xs_tok[:, t, :], bank[:, :], ACT.Copy), ("xs", t))
            for t in range(0, AT, 2):
                bank = banks.filled(act, ("b", t))
                tok_copied.tick(s.activation(b_tok[:, t:t + 2, :], bank[:, :].rearrange("p (t n) -> p t n", t=2),
                                             ACT.Copy), ("b", t))
            for n in range(2):
                bank = banks.filled(act, ("kT", n))
                w, o = (CTX, T) if n else (T, 0)
                s.activation(kz2[:, 0, o:o + w], bank[:, 0:w], ACT.Copy, scale=low)
                kz_ready.tick(s.activation(kz2[:, 1, o:o + w], bank[:, 0:w], ACT.Copy, scale=high), n)
            for j in range(4):
                bank = banks.filled(act, ("q2T", j))
                q2_ready.tick(s.activation(q2T[:, j, :], bank[:, :], ACT.Copy), j)
            for what, i in weave:
                if what == "win":
                    if i < NW:
                        h, t = divmod(i, TT)
                        lo, hi = near(t)
                        n = (hi - lo + 1) * P + CTX
                        wscore.wait(act, i)
                        row = wprobs[:, i % 2, 0:n]
                        s.activation(row, row, ACT.Exp, scale=-1.0, bias=nmin[:, i:i + 1], accum_out=psums[:, i:i + 1])
                        wprob.tick(s.activation(sink_exp[:, i:i + 1], sinks[:, h:h + 1], ACT.Exp,
                                                bias=nmin[:, i:i + 1]), i)
                    if 1 <= i <= NW:
                        m = i - 1
                        lo, hi = near(m % TT)
                        n = (hi - lo + 1) * P
                        near_b, far_b = (banks.filled(act, ("wprobsT", m, k)) for k in range(2))
                        if m >= 2:
                            banks.filled(act, ("watt", m - 2))
                        s.activation(wprobsT[:, m % 2, 0:n], near_b[:, 0:n], ACT.Copy)
                        wpt_act.tick(s.activation(wprobsT[:, m % 2, n:n + CTX], far_b[:, 0:CTX], ACT.Copy), m)
                elif what == "y" and i < len(YS):
                    seg_ready.wait(act, (i, 1))
                    decayed.tick(s.activation(decay[:, i % 2, :, :], decay[:, i % 2, :, :], ACT.Exp), i)

            def mixed2(t):
                y_done.wait(act, t)
                watt.wait(act, NW - 1)

            norm("mix2", mixed2)
            norm("norm2_2", lambda t: x3.wait(act, (t, 1)))
            route.wait(act, "max")
            for t in range(TT):
                last = s.activation(gexp[:, t, :], gl[:, t, 0:4], ACT.Exp, bias=g8[:, t, 0:1],
                                    accum_out=gsum[:, t:t + 1])
            route_act.tick(last, "group_exp")
            route.wait(act, "top2")
            route_act.tick(s.activation(wts[:, :, 3], wts[:, :, 2], ACT.Exp), "pair_exp")

            def expert(n, par, kpar, reuse):
                gate_up, hiddenT, y = ps[2 + par], ps[4 + par], ps[6 + par]
                act.wait_ge(gu_filled, n + 1)
                if reuse is not None:
                    act.wait_ge(ht_filled, reuse)
                s.activation(gu[:, par, :], gate_up[:, :], ACT.Copy).then_inc(gu_ready, 1)
                act.wait_ge(ht_filled, n + 1)
                if reuse is not None:
                    act.wait_ge(hid_ready, reuse)
                s.activation(sg[:, par, :, :], hiddenT[:, :].rearrange("p (f n) -> p f n", f=4)[:, :, 0:BLK],
                             ACT.Silu).then_inc(silu_ready, 1)
                act.wait_ge(y_filled, n + 1)
                if reuse is not None:
                    act.wait_ge(y_stored[par], 16 * kpar)
                s.activation(yE[:, par, :], y[:, :], ACT.Copy).then_inc(y_ready, 1)

            expert(0, 0, 0, None)
            expert(1, 1, 0, None)
            with act.Fori(1, E // 2) as it:
                for par in range(2):
                    expert(2 * it + par, par, it, 2 * it + par - 1)
            later_n = act.value_load(ovf[0:1, NOVF:NOVF + 1], min_val=0, max_val=NOVF)
            with act.If(later_n > 0):
                with act.Fori(0, later_n) as i:
                    expert(i + E, 0, i + E // 2, i + E)
            for t in range(TT):
                final_x.wait(act, t)
                if t:
                    squared.wait(act, ("final", t - 1, 0))
                squared.tick(s.activation(junk3, x[:, t, :], ACT.Square, accum_out=sums[:, t:t + 1]), ("final", t, 0))
            squared.wait(act, ("final", TT - 1, 0))
            rooted.tick(root(roots[:, 0:TT], sums[:, 0:TT], D), "final")

        @block.tensor
        def _(pe):
            def mm(o, lhsT, rhs, start, stop):
                return nc.tensor.matmul(o, lhsT, rhs, start=start, stop=stop)

            def tr(o, i, n=P):
                return nc.tensor.transpose(o, i, ident[0:n, 0:n])

            def norm(name, unscaled=None):
                _, n, parts, _, _ = NORMS[name]
                normed.wait(pe, (name, n - 1, parts[-1][0]))
                for k in halves(name):
                    _, j, c = k
                    bank = banks.open(pe, ("hT",) + k)
                    first, many = (TT, CT) if c else (0, TT)
                    for i in range(many):
                        last = tr(bank[:, i * P:(i + 1) * P],
                                  xn[:, first + i, :].rearrange("p (q j) -> p j q", j=KT)[:, j, :])
                    banks.close(last, ("hT",) + k)

            def hT_ready(name):
                hT_act.wait(pe, halves(name)[-2 if name != "norm1_2" else -3])
                hT_dve.wait(pe, halves(name)[-1])

            def project(key, lhs_of, w, a, n, first=0):
                bank = banks.open(pe, key)
                for j in range(KT):
                    last = mm(bank[:, 0:n], lhs_of(j), w[:, j, a:a + n], j == 0, j == KT - 1)
                banks.close(last, key)

            pe.wait_ge(const_in, CONST_ALL)
            bank = banks.open(pe, "conv_weights")
            tr(bank[:, 0:88], conv_rows[0:88, 0, :], 88)
            tr(bank[:, 88:176], conv_rows[0:88, 1, :], 88)
            banks.close(tr(bank[:, 176:224], conv_rows[0:48, 2, :], 48), "conv_weights")
            norm("norm1")
            hT_ready("norm1")
            for n in range(len(PROJ) + 2):
                if n < len(PROJ):
                    c, t = PROJ[n]
                    w = weights(pe, ("w_in", c))
                    project(("proj", n), lambda j: hT[:, j, t * P:(t + 1) * P], w, 0, w.shape[2])
                if 2 <= n < 18:
                    bank = banks.open(pe, ("qkT", n - 2))
                    qk_ready.wait(pe, n - 2)
                    for j in range(4):
                        last = tr(bank[:, j * P:(j + 1) * P], pj[:, (n - 2) % 3, j * P:(j + 1) * P])
                    banks.close(last, ("qkT", n - 2))
            qk_drained.wait(pe, 15)
            v_tail.wait(pe, TT - 1)
            mod_silu.wait(pe, "c")
            for i in range(NU + 2):
                if i < NU:
                    m, h, t = i // (H * TT), i // TT % H, i % TT
                    bank = banks.open(pe, ("score", i))
                    at = slice(t * P, t * P + P)
                    q, k = (qbT[:, h // 2, at], kzB[:, h, :]) if m else (qaT[:, h % 4, at], kzA[:, h // 4, :])
                    banks.close(mm(bank[:, :], q, k, True, True), ("score", i))
                if 1 <= i <= NU:
                    bank = banks.open(pe, ("probsT", i - 1))
                    prob.wait(pe, i - 1)
                    for k in range(TT):
                        last = tr(bank[:, k * P:(k + 1) * P], probs[:, (i - 1) % 2, k * P:(k + 1) * P])
                    banks.close(last, ("probsT", i - 1))
                if i >= 2:
                    n = i - 2
                    m, h = n // (H * TT), n // TT % H
                    bank = banks.open(pe, ("att", n))
                    pt_step(n).wait(pe, n)
                    for k in range(TT):
                        v = vB[:, k, h * HD:(h + 1) * HD] if m else vA[:, k, (h // 4) * HD:(h // 4 + 1) * HD]
                        last = mm(bank[:, 0:HD], probsT[:, n % 2, k * P:(k + 1) * P], v, k == 0, k == TT - 1)
                    banks.close(last, ("att", n))
                if i % 5 == 2 and i // 5 < 12:
                    m = i // 5
                    w = weights(pe, ("w_ada", m))
                    bank = banks.open(pe, ("modrow", m))
                    for j in range(KT):
                        quarter = bank[32 * (j % 4):32 * (j % 4) + 32, :]
                        last = mm(quarter, csilu[:, j, :], w[:, j, :], j < 4, j >= 4)
                    banks.close(last, ("modrow", m))
                if i % 5 == 4 and i // 5 < 12:
                    m = i // 5
                    mod_copied.wait(pe, m)
                    bank = banks.open(pe, ("mod", m))
                    if m // 2 in (2, 5):
                        last = mm(bank[:, :], C("sum_two")[:, 0:1].broadcast_to([P, P]), modrow[:, m % 2, :], True, True)
                    else:
                        for j in range(KT):
                            last = mm(bank[64 * (m % 2):64 * (m % 2) + 64, 2 * j:2 * j + 2],
                                      modrow[:, m % 2, :].rearrange("p (q j) -> p j q", j=KT)[:, j, :], C("sum_two"),
                                      True, True)
                    banks.close(last, ("mod", m))

            def out_projection(key, name):
                for n in range(2):
                    w = weights(pe, (name, n))
                    for t in range(TT):
                        yield t, n, w

            norm("mix1")
            hT_ready("mix1")
            for t, n in SIDES:
                w = weights(pe, ("w_out", n))
                project(("out1", t, n), lambda j: hT[:, j, t * P:(t + 1) * P], w, 0, 512)
            norm("norm2")
            hT_ready("norm2")
            for f in range(FT):
                w = weights(pe, ("w_up", f - f % 2))
                for gv in range(2):
                    bank = banks.open(pe, ("up", f, gv))
                    a = gv * 256 + (f % 2) * P
                    for j in range(KT):
                        last = mm(bank[:, :], w[:, j, a:a + P], hT[:, j, :], j == 0, j == KT - 1)
                    banks.close(last, ("up", f, gv))
            down_banks = [banks.open(pe, ("down",) + k) for k in SIDES]
            for i in range(6):
                w = weights(pe, ("w_down", i))
                fs = range(4 * i, min(4 * i + 4, FT))
                hidden.wait(pe, fs[-1])
                for k, (t, n) in enumerate(SIDES):
                    for f in fs:
                        last = mm(down_banks[k][:, :], hid[:, f, t * P:(t + 1) * P],
                                  w[:, f - 4 * i, n * 512:(n + 1) * 512], f == 0, f == FT - 1)
                    if i == 5:
                        banks.close(last, ("down", t, n))
                if i < 5:
                    down_read.tick(last, i)
            norm("norm1_2")
            hT_ready("norm1_2")

            def tokens(t):
                return (lambda j: hT[:, j, t * P:(t + 1) * P]) if t < TT else (
                    lambda j: hTc[:, j, (t - TT) * P:(t - TT + 1) * P])

            w = weights(pe, "w_kvd")
            for t in range(AT):
                project(("kvd", t), tokens(t), w, 0, 272)
            for m, c in XBC:
                w = weights(pe, ("w_xbc", m // 4))
                bank = banks.open(pe, ("xbc", m, c))
                src, n = (hTc, CTX) if c else (hT, T)
                for j in range(KT):
                    last = mm(bank[:, 0:n], w[:, j, (m % 4) * P:(m % 4 + 1) * P], src[:, j, :], j == 0, j == KT - 1)
                banks.close(last, ("xbc", m, c))
            w = weights(pe, "w_z")
            for t in range(TT):
                project(("z", t), tokens(t), w, 0, 512)
            w = weights(pe, "w_q")
            for t in range(TT):
                project(("q2", t), tokens(t), w, 0, 512)
            dta_ready.wait(pe, 0)
            bank = banks.open(pe, "cumsum")
            dta = sm[:, 6, :].rearrange("p (t d h) -> p t d h", t=AT, d=2)
            b4 = bank[:, 0:96].rearrange("p (t d h) -> p t d h", t=AT, d=2)
            mm(b4[:, :, 0, :], C("upto"), dta[:, :, 0, :], True, True)
            mm(b4[:, :, 1, :], C("from"), dta[:, :, 1, :], True, True)
            banks.close(mm(bank[:, 96:192], C("one").broadcast_to([P, P]), sm[:, 6, :], True, True), "cumsum")
            u_ready.wait(pe, KT - 1)
            for t in range(AT):
                bank = banks.open(pe, ("xs", t))
                for m in range(4):
                    last = tr(bank[:, m * P:(m + 1) * P], u[:, m, t * P:(t + 1) * P])
                banks.close(last, ("xs", t))
            for t in range(0, AT, 2):
                bank = banks.open(pe, ("b", t))
                for i in range(2):
                    for m in range(2):
                        o = i * 256 + m * P
                        last = tr(bank[:, o:o + P], u[:, 4 + m, (t + i) * P:(t + i + 1) * P])
                banks.close(last, ("b", t))
            for n in range(2):
                bank = banks.open(pe, ("kT", n))
                if n == 0:
                    roped.wait(pe, ("k", TT - 1))
                else:
                    kvd_copied.wait(pe, AT - 1)
                for i in range(CT if n else TT):
                    last = tr(bank[:, i * P:(i + 1) * P], kvd[:, n * TT + i, 16:144])
                banks.close(last, ("kT", n))
            for j in range(4):
                bank = banks.open(pe, ("q2T", j))
                roped.wait(pe, ("q", TT - 1))
                for t in range(TT):
                    last = tr(bank[:, t * P:(t + 1) * P], q2[:, t, j * P:(j + 1) * P])
                banks.close(last, ("q2T", j))
            tok_copied.wait(pe, ("b", AT - 2))
            kz_ready.wait(pe, 1)
            q2_ready.wait(pe, 3)
            for what, i in weave:
                if what == "win":
                    if i < NW:
                        h, t = divmod(i, TT)
                        lo, hi = near(t)
                        q = q2T[:, h % 4, t * P:(t + 1) * P]
                        k = kz2[:, h // 4, :]
                        bank = banks.open(pe, ("wscore", i, 0))
                        banks.close(mm(bank[:, 0:(hi - lo + 1) * P], q, k[:, lo * P:(hi + 1) * P], True, True),
                                    ("wscore", i, 0))
                        bank = banks.open(pe, ("wscore", i, 1))
                        banks.close(mm(bank[:, 0:CTX], q, k[:, T:T + CTX], True, True), ("wscore", i, 1))
                    if 1 <= i <= NW:
                        m = i - 1
                        lo, hi = near(m % TT)
                        n = hi - lo + 1
                        wprob.wait(pe, m)
                        for part, (a, many) in enumerate(((0, n), (n, CT))):
                            bank = banks.open(pe, ("wprobsT", m, part))
                            for k in range(many):
                                last = tr(bank[:, k * P:(k + 1) * P], wprobs[:, m % 2, (a + k) * P:(a + k + 1) * P])
                            banks.close(last, ("wprobsT", m, part))
                    if i >= 2:
                        m = i - 2
                        h, t = divmod(m, TT)
                        lo, hi = near(t)
                        seen = list(range(lo, hi + 1)) + list(range(TT, AT))
                        bank = banks.open(pe, ("watt", m))
                        wpt_act.wait(pe, m)
                        for n, kt in enumerate(seen):
                            v = kvd[:, kt, 144 + (h // 4) * HD:144 + (h // 4 + 1) * HD]
                            last = mm(bank[:, 0:HD], wprobsT[:, m % 2, n * P:(n + 1) * P], v, n == 0,
                                      n == len(seen) - 1)
                        banks.close(last, ("watt", m))
                elif what == "state":
                    d, pos = STATES[i]
                    t = TILE_AT[d][pos]
                    bank = banks.open(pe, ("state", i))
                    dtxw_ready.wait(pe, i)
                    for g in range(2):
                        last = mm(bank[:, g * 256:(g + 1) * 256], b_tok[:, t, g * P:(g + 1) * P],
                                  dtxw[:, i % 2, g * 256:(g + 1) * 256], True, True)
                    banks.close(last, ("state", i))
                else:
                    if i < len(YS):
                        t, d = YS[i]
                        if d == 0:
                            bank = banks.open(pe, ("cb", t))
                            for g in range(2):
                                last = mm(bank[:, g * P:(g + 1) * P], u[:, 4 + g, t * P:(t + 1) * P],
                                          u[:, 6 + g, t * P:(t + 1) * P], True, True)
                            banks.close(last, ("cb", t))
                        for g in range(2):
                            bank = banks.open(pe, ("seg", i, g))
                            for h in range(4):
                                a = t * 16 + d * 8 + g * 4 + h
                                last = mm(bank[:, h * P:(h + 1) * P], sm[:, 6, a:a + 1].broadcast_to([P, P]),
                                          C("from" if d else "upto"), True, True)
                            banks.close(last, ("seg", i, g))
                    if i >= 1:
                        t, d = YS[i - 1]
                        pos = TILE_AT[d].index(t) - 1
                        bank = banks.open(pe, ("yoff", i - 1))
                        state_ready.wait(pe, STATES.index((d, pos)))
                        for g in range(2):
                            last = mm(bank[:, g * 256:(g + 1) * 256], u[:, 6 + g, t * P:(t + 1) * P],
                                      state[:, d, pos - 1, g * 256:(g + 1) * 256], True, True)
                        banks.close(last, ("yoff", i - 1))
                        bank = banks.open(pe, ("ydiag", i - 1))
                        m_ready.wait(pe, i - 1)
                        dtx_ready.wait(pe, i - 1)
                        for h in range(H):
                            last = mm(bank[:, h * HD:(h + 1) * HD], decay[:, (i - 1) % 2, h, :],
                                      dtx[:, (i - 1) % 2, h * HD:(h + 1) * HD], True, True)
                        banks.close(last, ("ydiag", i - 1))
            norm("mix2")
            hT_ready("mix2")
            for t, n in SIDES:
                w = weights(pe, ("w_out2", n))
                project(("out2", t, n), lambda j: hT[:, j, t * P:(t + 1) * P], w, 0, 512)
            norm("norm2_2")
            hT_ready("norm2_2")
            for n, (steps_, step) in enumerate(g_[1] for g_ in banks.order[-8:]):
                steps_.wait(pe, step)
            for t in range(TT):
                for j in range(KT):
                    last = mm(ps[0][:, t * 36:(t + 1) * 36], hT[:, j, t * P:(t + 1) * P], route_w[:, j, :], j == 0,
                              j == KT - 1)
            route_pe.tick(last, "logits")
            route.wait(pe, "hot")
            for t in range(TT):
                for b in range(t):
                    mm(ps[1][:, t * E:(t + 1) * E], C("one").broadcast_to([P, P]), osum[:, b, :], b == 0, False)
                mm(ps[1][:, t * E:(t + 1) * E], C("before"), osum[:, t, :], t == 0, True)
            for t in range(TT):
                last = mm(ps[1][:, TT * E:(TT + 1) * E], C("one").broadcast_to([P, P]), osum[:, t, :], t == 0, t == TT - 1)
            route_pe.tick(last, "rank")
            route.wait(pe, "places")
            for n in range(8):
                last = mm(ps[2][:, 0:2 * NBLK], hot_p[:, n, :], hot_b[:, n, :, :].rearrange("p a b -> p (a b)"), n == 0,
                          n == 7)
            route_pe.tick(last, "table")
            route.wait(pe, "table")

            def expert(n, par, kpar, reuse):
                xt, gate_up, hiddenT, y = ps[par], ps[2 + par], ps[4 + par], ps[6 + par]
                gate_w, up_w, down_w = (EXPERT_SLOTS[3 * par + i] for i in range(3))
                loads, free = held(pe, 16 * kpar + 16), held(pe, reuse) if reuse is not None else None
                pe.wait_ge(const_in, CONST_ALL)
                pe.wait_ge(tokens_in[par], loads)
                if reuse is not None:
                    pe.wait_ge(xt_ready, free)
                for j in range(KT):
                    last = tr(xt[:, j * BLK:(j + 1) * BLK],
                              xg[0:BLK, par, :].rearrange("p (q j) -> p j q", j=KT)[:, j, :], BLK)
                last.then_inc(xt_filled, 1)
                pe.wait_ge(xt_ready, n + 1)
                pe.wait_ge(expert_in[3 * par], 16 * kpar + 16)
                pe.wait_ge(expert_in[3 * par + 1], 16 * kpar + 16)
                if reuse is not None:
                    pe.wait_ge(gu_ready, reuse)
                for j in range(KT):
                    for half, w in enumerate((gate_w, up_w)):
                        last = mm(gate_up[half * BLK:(half + 1) * BLK, :], xT[:, par, j, :], w[:, j * EF:(j + 1) * EF],
                                  j == 0, j == KT - 1)
                last.then_inc(gu_filled, 1)
                pe.wait_ge(gu_ready, n + 1)
                if reuse is not None:
                    pe.wait_ge(hid_ready, reuse)
                for f in range(4):
                    last = tr(hiddenT[:, f * P:(f + 1) * P], gu[:, par, :].rearrange("p (q f) -> p f q", f=4)[:, f, :])
                last.then_inc(ht_filled, 1)
                pe.wait_ge(hid_ready, n + 1)
                pe.wait_ge(expert_in[3 * par + 2], 16 * kpar + 16)
                if reuse is not None:
                    pe.wait_ge(y_ready, reuse)
                for f in range(4):
                    for half in range(2):
                        last = mm(y[half * BLK:(half + 1) * BLK, :], hidE[:, par, f, :],
                                  down_w[:, f * D + half * 512:f * D + half * 512 + 512], f == 0, f == 3)
                last.then_inc(y_filled, 1)

            expert(0, 0, 0, None)
            expert(1, 1, 0, None)
            with pe.Fori(1, E // 2) as it:
                for par in range(2):
                    expert(2 * it + par, par, it, 2 * it + par - 1)
            later_n = pe.value_load(ovf[0:1, NOVF:NOVF + 1], min_val=0, max_val=NOVF)
            with pe.If(later_n > 0):
                with pe.Fori(0, later_n) as i:
                    expert(i + E, 0, i + E // 2, i + E)

        @block.vector
        def _(dve):
            v = nc.vector

            def link(ins):
                dve_chain.link(dve, ins)

            def norm(name):
                src, n, parts, _, gain = NORMS[name]
                i = n * len(parts)
                rooted.wait(dve, name)
                link(v.reciprocal(rstd[:, 0:i], roots[:, 0:i]))
                i = 0
                for t in range(n):
                    for a, b in parts:
                        normed.tick(v.tensor_scalar(xn[:, t, a:b], src(t)[:, a:b], rstd[:, i:i + 1], None, ALU.mult),
                                    (name, t, a))
                        i += 1
                for k in halves(name):
                    if k[1] % 2 == 1:
                        _, j, c = k
                        bank = banks.filled(dve, ("hT",) + k)
                        dst = hTc[:, j, :] if c else hT[:, j, :]
                        sc, sh = gain(j, c)
                        hT_dve.tick(v.tensor_scalar(dst, bank[:, 0:dst.shape[1]], sc, sh, ALU.mult, ALU.add), k)

            csilu_cleared.tick(v.memset(csilu[:, :, :], 0.0), 0)
            dve.wait_ge(const_in, CONST_ALL)
            v.memset(gains[64:128, 4, :], 1.0)
            bank = banks.filled(dve, "conv_weights")
            conv_ready.tick(v.tensor_copy(convw[:, :], bank[:, 0:224]), "taps")
            for n in (0, 2):
                link(v.tensor_scalar(head_gain[:, n, :], head_gain[:, n, :], -HD ** -0.5, None, ALU.mult))
            norm("norm1")
            for n in range(20):
                if n >= 16:
                    bank = banks.filled(dve, ("proj", n))
                    v_tail.tick(v.tensor_copy(vB[:, n - 16, 256:512], bank[:, 0:256]), n - 16)
                    continue
                c, t = PROJ[n]
                pj_ready.wait(dve, n)
                if n >= 2:
                    head_rooted.wait(dve, n - 2)
                head_summed.tick(v.tensor_reduce(head_sum[:, n % 2, :], sq[:, n % 2, :].rearrange(
                    "p (h d) -> p h d", d=HD), AXX, ALU.add), n)
                head_rooted.wait(dve, n)
                link(v.reciprocal(head_sum[:, n % 2, :], head_root[:, n % 2, :]))
                row = pj[:, n % 3, :].rearrange("p (h d) -> p h d", d=HD)
                for a, many, gain in HEADS_OF[c]:
                    seg = row[:, a:a + many, :]
                    last = v.tensor_tensor(seg, seg, wide(head_sum[:, n % 2, a:a + many], HD), ALU.mult)
                link(last)
                for a, many, gain in HEADS_OF[c]:
                    seg = row[:, a:a + many, :]
                    last = v.tensor_tensor(seg, seg, head_gain[:, gain, :].unsqueeze(1).broadcast_to([P, many, HD]),
                                           ALU.mult)
                if c >= 2:
                    qk_ready.tick(last, n)
                    continue
                link(last)
                heads = 8 if c == 0 else 2
                cos, sin = rope1[:, 0, t, :], rope1[:, 1, t, :]
                a3, b3 = (rope_t[:, i, 0:heads * HD] for i in range(2))
                src = row[:, 0:heads, :]
                v.tensor_tensor(a3.rearrange("p (h d) -> p h d", d=HD), src,
                                cos.unsqueeze(1).broadcast_to([P, heads, HD]), ALU.mult)
                split = "p h (a b d) -> p h a b d"
                s5 = src.rearrange(split, a=2, b=2)
                b5 = b3.rearrange("p (h a b d) -> p h a b d", h=heads, a=2, b=2)
                sin4 = sin.rearrange("p (a b d) -> p a b d", a=2, b=2)
                for half in range(2):
                    last = v.tensor_tensor(b5[:, :, :, half, :], s5[:, :, :, 1 - half, :],
                                           sin4[:, :, half, :].unsqueeze(1).broadcast_to([P, heads, 2, 16]), ALU.mult)
                link(last)
                if c == 0:
                    dst = pj[:, n % 3, :].rearrange("p (j half d) -> p half j d", j=4, half=2)
                    order = "p (half j d) -> p half j d"
                    ins = v.tensor_tensor(dst, a3.rearrange(order, j=4, half=2), b3.rearrange(order, j=4, half=2),
                                          ALU.add)
                else:
                    ins = v.tensor_tensor(pj[:, n % 3, 0:128], a3, b3, ALU.add)
                qk_ready.tick(ins, n)
            for i in range(NU + 2):
                if i < NU:
                    bank = banks.filled(dve, ("score", i))
                    if i < NU // 2:
                        score_min.tick(v.tensor_reduce(nmin[:, i:i + 1], bank[:, :], AXX, ALU.min), i)
                    else:
                        h, t = i // TT % H, i % TT
                        dve.wait_ge(dist_in[h % 2], 16 * (h // 2 + 1))
                        banks.filled(dve, ("probsT", i - 2))
                        a = (TT - 1 - t) * P
                        score_min.tick(v.tensor_tensor_reduce(probs[:, i % 2, :], bank[:, :], dist[:, h % 2, a:a + T],
                                                              1.0, 3e38, ALU.add, ALU.min, nmin[:, i:i + 1]), i)
                if 1 <= i <= NU and (i - 1) % 2 == 1:
                    bank = banks.filled(dve, ("probsT", i - 1))
                    if i >= 3:
                        banks.filled(dve, ("att", i - 3))
                    pt_dve.tick(v.tensor_copy(probsT[:, (i - 1) % 2, :], bank[:, :]), i - 1)
                if i >= 2:
                    n = i - 2
                    m, h, t = n // (H * TT), n // TT % H, n % TT
                    bank = banks.filled(dve, ("att", n))
                    link(v.reciprocal(rsums[:, n:n + 1], psums[:, n:n + 1]))
                    att.tick(v.tensor_scalar(xn[:, t, m * 512 + h * HD:m * 512 + (h + 1) * HD], bank[:, 0:HD],
                                             rsums[:, n:n + 1], None, ALU.mult), n)
                if i % 5 == 4 and i // 5 < 12:
                    m = i // 5
                    bank = banks.filled(dve, ("mod", m))
                    if m // 2 in (2, 5):
                        row = gates[:, m // 6, (m % 2) * 512:(m % 2) * 512 + 512]
                        ins = v.tensor_tensor(row, bank[:, :], row, ALU.add)
                    else:
                        q = slice(64 * (m % 2), 64 * (m % 2) + 64)
                        ins = v.tensor_tensor(mod[q, m // 2, :, :], bank[q, 0:16].rearrange("p (j c) -> p j c", c=2),
                                              wide(ada_bias[q, m // 2, :], 2), ALU.add)
                    mod_done.tick(ins, m)
            mod_done.wait(dve, 11)
            v.scalar_tensor_tensor(mod_gain[:, 0, :], mod[:, 1, :, 0], 1.0, gains[:, 3, :], ALU.add, ALU.mult)
            v.scalar_tensor_tensor(mod_gain[:, 1, :], mod[:, 1, :, 1], 1.0, gains[:, 3, :], ALU.add, ALU.mult)
            mod_done.tick(v.scalar_tensor_tensor(mod_gain[:, 2, :], mod[:, 4, :, 0], 1.0, gains[:, 5, :], ALU.add,
                                                 ALU.mult), "gains")
            norm("mix1")
            for t, n in SIDES:
                bank = banks.filled(dve, ("out1", t, n))
                side = x[:, t, n * 512:(n + 1) * 512]
                x1.tick(v.tensor_tensor(side, bank[:, :], side, ALU.add), (t, n))
            norm("norm2")
            for f in range(FT + 1):
                if f < FT:
                    for gv in range(2):
                        bank = banks.filled(dve, ("up", f, gv))
                        tap_mid.wait(dve, (f, gv))
                        y = (conv_g, conv_v)[gv][:, f % 2, :]
                        ch = gv * FT + f
                        link(v.scalar_tensor_tensor(y[:, 1:T], bank[:, 0:T - 1], convw[:, ch:ch + 1], y[:, 1:T],
                                                    ALU.mult, ALU.add))
                        tapped.tick(v.scalar_tensor_tensor(y[:, 0:T - 1], bank[:, 1:T], convw[:, 88 + ch:89 + ch],
                                                           y[:, 0:T - 1], ALU.mult, ALU.add), (f, gv))
                if f >= 1:
                    gelued.wait(dve, f - 1)
                    hidden.tick(v.tensor_tensor(hid[:, f - 1, :], conv_g[:, (f - 1) % 2, :], conv_v[:, (f - 1) % 2, :],
                                                ALU.mult), f - 1)
            for t, n in SIDES:
                bank = banks.filled(dve, ("down", t, n))
                side = x[:, t, n * 512:(n + 1) * 512]
                x2.tick(v.tensor_tensor(side, bank[:, :], side, ALU.add), (t, n))
            norm("norm1_2")
            for t in range(AT):
                bank = banks.filled(dve, ("kvd", t))
                kvd_copied.tick(v.tensor_copy(kvd[:, t, :], bank[:, 0:272]), t)
            kvd_copied.wait(dve, AT - 1)
            raw = sm[:, 0, :].rearrange("p (t k) -> p t k", t=AT)
            link(v.tensor_tensor(raw, kvd[:, :, 0:16], dt_bias[:, :].unsqueeze(1).broadcast_to([P, AT, 16]), ALU.add))
            dt_abs.tick(v.scalar_tensor_tensor(sm[:, 4, :], sm[:, 0, :], -1.0, sm[:, 0, :], ALU.mult, ALU.max), 0)
            for m, c in XBC:
                bank = banks.filled(dve, ("xbc", m, c))
                mid2.wait(dve, (m, c))
                n, o = (CTX, T) if c else (T, 0)
                y = conv2[:, m % 2, o:o + n]
                for k, off in ((0, -2), (1, -1), (3, 1), (4, 2)):
                    a, b = max(0, -off), min(n, n - off)
                    w = convw[:, 176 + 8 * k + m:177 + 8 * k + m]
                    ins = v.scalar_tensor_tensor(y[:, a:b], bank[:, a + off:b + off], w, y[:, a:b], ALU.mult, ALU.add)
                    if k < 4:
                        link(ins)
                tapped2.tick(ins, (m, c))
            dt_exp.wait(dve, 0)
            dt_abs.tick(v.tensor_scalar(sm[:, 2, :], sm[:, 1, :], 1.0, None, ALU.add), 1)
            dt_abs.wait(dve, 1)
            link(v.tensor_scalar(sm[:, 4, :], sm[:, 2, :], -1.0, None, ALU.add))
            link(v.tensor_scalar(sm[:, 5, :], sm[:, 4, :], 0.0, None, ALU.is_equal))
            link(v.tensor_tensor(sm[:, 4, :], sm[:, 4, :], sm[:, 5, :], ALU.add))
            link(v.reciprocal(sm[:, 4, :], sm[:, 4, :]))
            link(v.tensor_tensor(sm[:, 4, :], sm[:, 4, :], sm[:, 1, :], ALU.mult))
            dt_log.wait(dve, 0)
            link(v.tensor_tensor(sm[:, 4, :], sm[:, 4, :], sm[:, 3, :], ALU.mult))
            link(v.tensor_tensor(sm[:, 5, :], sm[:, 5, :], sm[:, 1, :], ALU.mult))
            link(v.tensor_tensor(sm[:, 4, :], sm[:, 4, :], sm[:, 5, :], ALU.add))
            link(v.scalar_tensor_tensor(sm[:, 5, :], sm[:, 0, :], 0.0, sm[:, 4, :], ALU.max, ALU.add))
            a_exp.wait(dve, 0)
            dta_ready.tick(v.scalar_tensor_tensor(
                sm[:, 6, :].rearrange("p (t k) -> p t k", t=AT), sm[:, 5, :].rearrange("p (t k) -> p t k", t=AT), -1.0,
                a_log[:, :].unsqueeze(1).broadcast_to([P, AT, 16]), ALU.mult, ALU.mult), 0)
            bank = banks.filled(dve, "cumsum")
            v.tensor_copy(sm[:, 7, :], bank[:, 0:96])
            link(v.tensor_copy(sm[:, 2, :], bank[:, 96:192]))
            cs_copied.tick(v.tensor_tensor(sm[:, 1, :], sm[:, 2, :], sm[:, 7, :], ALU.subtract), 0)
            cs_exp.wait(dve, 0)
            sw_ready.tick(v.tensor_tensor(sm[:, 9, :], sm[:, 1, :], sm[:, 5, :], ALU.mult), 0)
            link(v.tensor_scalar(win_min[:, 64:72], sinks[:, :], -1.0, None, ALU.mult))

            def y_rows(k, parts):
                t, d = YS[k]
                row = cat[:, t, 0:512]
                row3 = row.rearrange("p (h d) -> p h d", d=HD)
                off = banks.filled(dve, ("yoff", k))
                ea = wide(sm[:, 0, t * 16 + d * 8:t * 16 + d * 8 + 8], HD)
                ins = v.tensor_tensor(ytmp.rearrange("p (h d) -> p h d", d=HD),
                                      off[:, :].rearrange("p (h d) -> p h d", d=HD), ea, ALU.mult)
                y_read.tick(ins, (k, "off"))
                y_read.wait(dve, (k, "off"))
                diag = banks.filled(dve, ("ydiag", k))
                if d == 0:
                    y_read.tick(v.tensor_tensor(row, diag[:, :], ytmp, ALU.add), (k, "diag"))
                    y_read.wait(dve, (k, "diag"))
                    return
                link(v.tensor_tensor(row, row, ytmp, ALU.add))
                y_read.tick(v.tensor_tensor(row, diag[:, :], row, ALU.add), (k, "diag"))
                y_read.wait(dve, (k, "diag"))
                link(v.tensor_tensor(ytmp.rearrange("p (h d) -> p h d", d=HD),
                                     xs_tok[:, t, :].rearrange("p (h d) -> p h d", d=HD), wide(d_skip[:, :], HD),
                                     ALU.mult))
                link(v.tensor_tensor(row, row, ytmp, ALU.add))
                y_done.tick(v.tensor_tensor(row, row, zs[:, t, :], ALU.mult), t)

            for what, i in weave:
                if what == "win":
                    if i < NW:
                        h, t = divmod(i, TT)
                        lo, hi = near(t)
                        n = (hi - lo + 1) * P
                        if i >= 2:
                            banks.filled(dve, ("wprobsT", i - 2, 1))
                        mask = C("window")
                        a = (lo - t + 1) * P
                        near_b, far_b = (banks.filled(dve, ("wscore", i, k)) for k in range(2))
                        v.tensor_tensor_reduce(wprobs[:, i % 2, 0:n], near_b[:, 0:n], mask[:, a:a + n], 1.0, 3e38,
                                               ALU.add, ALU.min, win_min[:, 2 * i:2 * i + 1])
                        link(v.tensor_tensor_reduce(wprobs[:, i % 2, n:n + CTX], far_b[:, 0:CTX],
                                                    mask[:, 3 * P:3 * P + CTX], 1.0, 3e38, ALU.add, ALU.min,
                                                    win_min[:, 2 * i + 1:2 * i + 2]))
                        wscore.tick(v.tensor_scalar(nmin[:, i:i + 1], win_min[:, 2 * i:2 * i + 1], win_min[:, 2 * i + 1:2 * i + 2],
                                                    win_min[:, 64 + h:65 + h], ALU.min, ALU.min), i)
                    if i >= 2:
                        m = i - 2
                        h, t = divmod(m, TT)
                        bank = banks.filled(dve, ("watt", m))
                        link(v.tensor_tensor(rsums[:, m:m + 1], psums[:, m:m + 1], sink_exp[:, m:m + 1], ALU.add))
                        link(v.reciprocal(rsums[:, m:m + 1], rsums[:, m:m + 1]))
                        watt.tick(v.tensor_scalar(cat[:, t, 512 + h * HD:512 + (h + 1) * HD], bank[:, 0:HD],
                                                  rsums[:, m:m + 1], None, ALU.mult), m)
                elif what == "state":
                    d, pos = STATES[i]
                    t = TILE_AT[d][pos]
                    bank = banks.filled(dve, ("state", i))
                    if pos == 0:
                        ins = v.tensor_copy(state0[:, d, :], bank[:, :])
                    else:
                        old = state0[:, d, :] if pos == 1 else state[:, d, pos - 2, :]
                        state_ready.wait(dve, STATES.index((d, pos - 1)))
                        link(v.tensor_tensor(stmp.rearrange("p (h d) -> p h d", d=HD),
                                             old.rearrange("p (h d) -> p h d", d=HD),
                                             wide(sm[:, 8, t * 16 + d * 8:t * 16 + d * 8 + 8], HD), ALU.mult))
                        ins = v.tensor_tensor(state[:, d, pos - 1, :], bank[:, :], stmp, ALU.add)
                    state_ready.tick(ins, i)
                else:
                    if i < len(YS):
                        t, d = YS[i]
                        if d == 0:
                            bank = banks.filled(dve, ("cb", t))
                            b3 = bank[:, 0:256].rearrange("p (g n) -> p g n", g=2)
                            v.tensor_tensor(cbm[:, 0, :, :], b3, C("upto").unsqueeze(1).broadcast_to([P, 2, P]),
                                            ALU.mult)
                            cb_masked.tick(v.tensor_tensor(
                                cbm[:, 1, :, :], b3, C("from").unsqueeze(1).broadcast_to([P, 2, P]), ALU.mult), t)
                        if i >= 2:
                            banks.filled(dve, ("ydiag", i - 2))
                        for g in range(2):
                            bank = banks.filled(dve, ("seg", i, g))
                            for h in range(4):
                                a = t * 16 + d * 8 + g * 4 + h
                                ins = v.tensor_scalar(decay[:, i % 2, g * 4 + h, :], bank[:, h * P:(h + 1) * P],
                                                      sm[:, 7, a:a + 1], 0.0, ALU.subtract, ALU.min)
                            seg_ready.tick(ins, (i, g))
                    if i >= 1:
                        y_rows(i - 1, None)
                    if i < len(YS):
                        cb_masked.wait(dve, t)
                        decayed.wait(dve, i)
                        for g in range(2):
                            rows = decay[:, i % 2, 4 * g:4 * g + 4, :]
                            ins = v.tensor_tensor(rows, rows, cbm[:, d, g, :].unsqueeze(1).broadcast_to([P, 4, P]),
                                                  ALU.mult)
                        m_ready.tick(ins, i)
            norm("mix2")
            for t, n in SIDES:
                bank = banks.filled(dve, ("out2", t, n))
                side = x[:, t, n * 512:(n + 1) * 512]
                gated = (ytmp, stmp)[n]
                link(v.tensor_tensor(gated, bank[:, :], gates[:, 0, n * 512:(n + 1) * 512], ALU.mult))
                x3.tick(v.tensor_tensor(side, side, gated, ALU.add), (t, n))
            norm("norm2_2")
            route_pe.wait(dve, "logits")
            link(v.tensor_tensor(lg[:, :, :], ps[0][:, 0:TT * 36].rearrange("p (t n) -> p t n", t=TT),
                                 route_bias[:, :].unsqueeze(1).broadcast_to([P, TT, 36]), ALU.add))
            link(v.memset(gl[:, :, :], -3e38))
            link(v.tensor_copy(gl[:, :, 0:4], lg[:, :, 0:4]))
            for t in range(TT):
                ins = v.max(g8[:, t, :], gl[:, t, :])
            link(ins)
            for t in range(TT):
                ins = v.max_index(gi[:, t, :], g8[:, t, :], gl[:, t, :])
            route.tick(ins, "logits")
            route.wait(dve, "logits")
            link(v.tensor_copy(gif[:, :], gi[:, :, 0]))
            route.tick(v.tensor_scalar(g8[:, :, 0:1], g8[:, :, 0:1], -1.0, None, ALU.mult), "max")
            for t in range(TT):
                ins = v.tensor_scalar(el[:, t, :], C("group"), gif[:, t:t + 1], BIG, ALU.is_equal, ALU.mult)
            link(ins)
            link(v.scalar_tensor_tensor(el[:, :, :], el[:, :, :], -BIG, lg[:, :, 4:36], ALU.add, ALU.add))
            for t in range(TT):
                ins = v.max(e8[:, t, :], el[:, t, :])
            link(ins)
            for t in range(TT):
                ins = v.max_index(ei[:, t, :], e8[:, t, :], el[:, t, :])
            link(ins)
            link(v.tensor_copy(eif[:, :, :], ei[:, :, 0:2]))
            route.tick(v.tensor_tensor(wts[:, :, 2], e8[:, :, 1], e8[:, :, 0], ALU.subtract), "top2")
            route_act.wait(dve, "pair_exp")
            link(v.tensor_scalar(wts[:, :, 4], wts[:, :, 3], 1.0, None, ALU.add))
            link(v.tensor_tensor(wts[:, :, 4], wts[:, :, 4], gsum[:, :], ALU.mult))
            link(v.reciprocal(wts[:, :, 0], wts[:, :, 4]))
            route.tick(v.tensor_tensor(wts[:, :, 1], wts[:, :, 0], wts[:, :, 3], ALU.mult), "weights")
            for t in range(TT):
                for k in range(2):
                    ins = v.tensor_scalar(ohot[:, t, k, :], C("expert"), eif[:, t, k:k + 1], None, ALU.is_equal)
            link(ins)
            route.tick(v.tensor_tensor(osum[:, :, :], ohot[:, :, 0, :], ohot[:, :, 1, :], ALU.add), "hot")
            route_pe.wait(dve, "rank")
            v.tensor_copy(rank[:, :, :], ps[1][:, 0:TT * E].rearrange("p (t e) -> p t e", t=TT))
            link(v.tensor_copy(cnt, ps[1][:, TT * E:(TT + 1) * E]))
            link(v.tensor_scalar(novf, cnt, float(BLK), None, ALU.is_gt))
            for m in range(2, T // BLK):
                link(v.scalar_tensor_tensor(novf, cnt, float(m * BLK), novf, ALU.is_gt, ALU.add))
            a, b = 0, 1
            link(v.tensor_copy(start[:, 0, :], novf))
            for k in (1, 2, 4, 8, 16):
                v.tensor_copy(start[:, b, 0:k], start[:, a, 0:k])
                link(v.tensor_tensor(start[:, b, k:E], start[:, a, k:E], start[:, a, 0:E - k], ALU.add))
                a, b = b, a
            v.tensor_tensor(later, start[:, a, :].unsqueeze(1).broadcast_to([P, NOVF, E]),
                            C("block")[:, 0:NOVF].unsqueeze(2).broadcast_to([P, NOVF, E]), ALU.is_le)
            link(v.tensor_copy(ovf[0:1, NOVF:NOVF + 1], start[0:1, a, E - 1:E]))
            link(v.tensor_reduce(later_cnt[:, 0:NOVF], later, AXX, ALU.add))
            link(v.tensor_scalar(later_cnt[:, 0:NOVF], later_cnt[:, 0:NOVF], float(E - 1), None, ALU.min))
            route.tick(v.tensor_copy(ovf[0:1, 0:NOVF], later_cnt[0:1, 0:NOVF]), "counts")
            first = wide_e[:, 0, :]
            link(v.tensor_tensor(first, start[:, a, :], novf, ALU.subtract))
            link(v.tensor_tensor(first, first, C("blocks_on"), ALU.add))
            link(v.tensor_scalar(quo[:, :, :], rank[:, :, :], float(BLK), None, ALU.is_ge))
            for m in range(2, T // BLK):
                link(v.scalar_tensor_tensor(quo[:, :, :], rank[:, :, :], float(m * BLK), quo[:, :, :], ALU.is_ge, ALU.add))
            v.scalar_tensor_tensor(plc[:, :, :], quo[:, :, :], -float(BLK), rank[:, :, :], ALU.mult, ALU.add)
            link(v.tensor_tensor(blk[:, :, :], quo[:, :, :], first.unsqueeze(1).broadcast_to([P, TT, E]), ALU.add))
            link(v.scalar_tensor_tensor(blk[:, :, :], quo[:, :, :], 1.0, blk[:, :, :], ALU.is_ge, ALU.mult))
            link(v.tensor_tensor(blk[:, :, :], blk[:, :, :], C("expert").unsqueeze(1).broadcast_to([P, TT, E]), ALU.add))
            for src, dst in ((plc, pk), (blk, bk)):
                for k in range(2):
                    ins = v.tensor_tensor(prod[:, :, k, :], ohot[:, :, k, :], src[:, :, :], ALU.mult)
                link(ins)
                link(v.tensor_reduce(dst.rearrange("p (t k) -> p t k", t=TT), prod[:, :, :, :], AXX, ALU.add))
            for n in range(8):
                v.tensor_scalar(hot_p[:, n, :].rearrange("p (a b) -> p a b", a=2),
                                C("place").unsqueeze(1).broadcast_to([P, 2, BLK]), pk[:, n:n + 1], None, ALU.is_equal)
                v.tensor_scalar(hot_b[:, n, 0, :], C("block"), bk[:, n:n + 1], C("token1")[:, n // 2:n // 2 + 1],
                                ALU.is_equal, ALU.mult)
                ins = v.tensor_scalar(hot_b[:, n, 1, :], C("block"), bk[:, n:n + 1], C("choice1")[:, n:n + 1],
                                      ALU.is_equal, ALU.mult)
            route.tick(ins, "places")
            route_pe.wait(dve, "table")
            link(v.tensor_copy(tval[:, 0, :], ps[2][:, 0:2 * NBLK]))
            link(v.tensor_scalar(tval[:, 1, :], tval[:, 0, :], 0.0, 16384.0, ALU.is_equal, ALU.mult))
            link(v.tensor_scalar(tval[:, 1, NBLK:2 * NBLK], tval[:, 1, NBLK:2 * NBLK], C("half2"), None, ALU.add))
            link(v.scalar_tensor_tensor(tok_of[:, :], tval[:, 0, 0:NBLK], -1.0, tval[:, 1, 0:NBLK], ALU.add, ALU.add))
            route.tick(v.scalar_tensor_tensor(row_of[:, :], tval[:, 0, NBLK:2 * NBLK], 2.0, tval[:, 1, NBLK:2 * NBLK],
                                              ALU.mult, ALU.add), "table")

            def expert(n, par, kpar, reuse):
                xt, hiddenT = ps[par], ps[4 + par]
                dve.wait_ge(xt_filled, n + 1)
                if reuse is not None:
                    dve.wait_ge(gu_filled, reuse)
                v.tensor_tensor(xT[:, par, :, :], xt[:, :].rearrange("p (j n) -> p j n", j=KT),
                                wide(mod_gain[:, 2, :], BLK), ALU.mult).then_inc(xt_scaled, 1)
                dve.wait_ge(xt_scaled, n + 1)
                v.tensor_tensor(xT[:, par, :, :], xT[:, par, :, :], wide(mod[:, 3, :, 0], BLK), ALU.add).then_inc(
                    xt_ready, 1)
                dve.wait_ge(silu_ready, n + 1)
                if reuse is not None:
                    dve.wait_ge(y_filled, reuse)
                v.tensor_tensor(hidE[:, par, :, :], sg[:, par, :, :],
                                hiddenT[:, :].rearrange("p (f n) -> p f n", f=4)[:, :, BLK:2 * BLK],
                                ALU.mult).then_inc(hid_ready, 1)

            expert(0, 0, 0, None)
            expert(1, 1, 0, None)
            with dve.Fori(1, E // 2) as it:
                for par in range(2):
                    expert(2 * it + par, par, it, 2 * it + par - 1)
            later_n = dve.value_load(ovf[0:1, NOVF:NOVF + 1], min_val=0, max_val=NOVF)
            with dve.If(later_n > 0):
                with dve.Fori(0, later_n) as i:
                    expert(i + E, 0, i + E // 2, i + E)
            dve.wait_ge(y01_in, 16)
            for t in range(TT):
                link(v.tensor_scalar(y01[:, t, 0, :], y01[:, t, 0, :], wts[:, t, 0:1], None, ALU.mult))
                link(v.scalar_tensor_tensor(y01[:, t, 0, :], y01[:, t, 1, :], wts[:, t, 1:2], y01[:, t, 0, :], ALU.mult,
                                            ALU.add))
                link(v.tensor_tensor(y01[:, t, 0, :], y01[:, t, 0, :], gates[:, 1, :], ALU.mult))
                final_x.tick(v.tensor_tensor(x[:, t, :], x[:, t, :], y01[:, t, 0, :], ALU.add), t)
            rooted.wait(dve, "final")
            link(v.reciprocal(rstd[:, 0:TT], roots[:, 0:TT]))
            dve.wait_ge(final_in, 16)
            for t in range(TT):
                final_y.tick(v.scalar_tensor_tensor(y01[:, t, 0, :], x[:, t, :], rstd[:, t:t + 1], final_gain, ALU.mult,
                                                    ALU.mult), t)


INPUTS = ["x", "norm1_g", "w_in", "qa_norm_g", "ka_norm_g", "qb_norm_g", "kb_norm_g", "outa_norm_g", "outb_norm_g",
          "w_out", "norm2_g", "w_up", "conv_w", "conv_b", "w_down", "c_2", "ctx_2", "c_ctx_2", "w_ada_2", "b_ada_2",
          "norm1_2", "w_in_2", "conv_w_2", "conv_b_2", "dt_bias_2", "a_log_2", "d_skip_2", "ssd_norm_2",
          "attn_sinks_2", "w_out_2", "norm2_2", "w_group_2", "b_group_2", "w_expert_2", "b_expert_2", "w_gate_2",
          "w_up_2", "w_down_2", "norm_final_2"]


def kernel(**inputs):
    import concourse.bacc as bacc
    from concourse.bass_utils import run_bass_kernel_spmd

    nc = bacc.Bacc("TRN2", target_bir_lowering=False, num_devices=1)
    arrays, aps = {}, {}
    for name in INPUTS:
        a = np.ascontiguousarray(inputs[name])
        arrays[f"in_{name}"] = a
        aps[name] = nc.dram_tensor(f"in_{name}", a.shape, F32, kind="ExternalInput").ap()
    tables = {"tables": constants()[1], "rotary": constants()[2], "distances": distance_tables()}
    for name, a in tables.items():
        arrays[name] = a
    consts_d, rope1_d, dist_d = (nc.dram_tensor(n, a.shape, F32, kind="ExternalInput").ap() for n, a in tables.items())
    h_d = nc.dram_tensor("normed_tokens", (T, D), F32, kind="Internal").ap()
    y_d = nc.dram_tensor("expert_outputs", (4 * T, D // 2), F32, kind="Internal").ap()
    out = nc.dram_tensor("out", (1, T, D), F32, kind="ExternalOutput").ap()
    two_blocks(nc, consts_d, rope1_d, dist_d, h_d, y_d, aps, out)
    r = run_bass_kernel_spmd(nc, [arrays], core_ids=[0])
    return r.results[0]["out"]
```

```python
import numpy as np
import concourse.bass as bass
from concourse import mybir
from contextlib import ExitStack

F32 = mybir.dt.float32
F32R = mybir.dt.float32r
I32 = mybir.dt.int32
U32 = mybir.dt.uint32
ALU = mybir.AluOpType
ACT = mybir.ActivationFunctionType
AXX = mybir.AxisListType.X

P = 128
T, CTX, D = 512, 256, 1024
TT, CT = T // P, CTX // P
AT = TT + CT
KT = D // P
HD = 64
H = 8
W1 = 2304
DFF = 2816
FT = DFF // P
E = 32
EG = 8
EF = 512
BLK = 64
NOVF = 2 * T // BLK - 1
NBLK = E + NOVF
EPS = 1e-6
BIG = 1e30
RING = 3
UNIT = 4096
HALF = UNIT // 2
ARENA = 17760
BIASW = T + (TT - 1) * P


def constants():
    f = np.float32
    i = np.arange(P)
    col = i[:, None]
    row = i[None, :]
    t = {}
    t["ident"] = np.eye(P, dtype=f)
    t["upto"] = (col <= row).astype(f)
    t["from"] = (col >= row).astype(f)
    t["before"] = (col < row).astype(f)
    t["one"] = np.ones((P, 1), f)
    group_row = (i % 32 == 0).astype(f)[:, None]
    t["sum_two"] = np.concatenate([group_row, (i % 32 == 1).astype(f)[:, None]], axis=1)
    t["window"] = np.concatenate([np.where(row >= col, 0, BIG), np.zeros((P, P)), np.where(row <= col, 0, BIG),
                                  np.zeros((P, CTX))], axis=1).astype(f)
    tok = np.arange(T)
    r, c = (tok // 64).astype(f)[:, None], (tok % 64).astype(f)[:, None]

    def tiles(a):
        return a.reshape(TT, P, -1).transpose(1, 0, 2).reshape(P, -1).astype(f)

    inv = (f(10000.0) ** (-np.arange(0, 32, 2, dtype=f) / f(32))).astype(f)[None]
    ar, ac = r * inv, c * inv
    rope1 = tiles(np.concatenate([np.cos(ar), np.cos(ar), np.cos(ac), np.cos(ac)], 1)), tiles(np.concatenate(
        [-np.sin(ar), np.sin(ar), -np.sin(ac), np.sin(ac)], 1))
    inv = (f(10000.0) ** (-np.arange(16, dtype=f) / f(16))).astype(f)[None]
    a = np.concatenate([r * inv, c * inv], 1)
    t["cos2"] = tiles(np.concatenate([np.cos(a), np.cos(a)], 1))
    t["sin2"] = tiles(np.concatenate([-np.sin(a), np.sin(a)], 1))
    t["eps"] = np.full((P, 1), EPS, f)
    t["zero"] = np.zeros((P, 1), f)
    t["low"] = (i < 64).astype(f)[:, None]
    t["high"] = (i >= 64).astype(f)[:, None]
    e = np.arange(E)
    t["expert"] = np.tile(e, (P, 1)).astype(f)
    t["group"] = np.tile(e // EG, (P, 1)).astype(f)
    t["blocks_on"] = np.tile(E - 1 - e, (P, 1)).astype(f)
    t["block"] = np.tile(np.arange(NBLK), (P, 1)).astype(f)
    t["place"] = np.tile(np.arange(BLK), (P, 1)).astype(f)
    t["full_blocks"] = np.tile(BLK * np.arange(1, T // BLK), (P, 1)).astype(f)
    t["both_halves"] = (i[:, None] % 64 == np.arange(E + E // EG)[None]).astype(f)
    both = 2 * tok.reshape(TT, P).T[:, :, None] + np.arange(2) + 1
    t["numbers"] = np.stack([(both + 1) // 2, both], axis=-1).reshape(P, 4 * TT).astype(f)
    t["half2"] = (i // BLK - 2).astype(f)[:, None]
    at, out = {}, []
    for k, v in t.items():
        at[k] = (sum(x.shape[1] for x in out), v.shape[1])
        out.append(v.astype(f))
    return at, np.ascontiguousarray(np.concatenate(out, axis=1)), np.ascontiguousarray(np.concatenate(rope1, axis=1))


def distance_tables():
    off = np.abs(np.arange(P)[:, None] - (np.arange(BIASW)[None] - (TT - 1) * P))
    seen = (off <= 64).astype(np.int64) + ((off <= 256) & (off % 4 == 0)) + (off % 16 == 0)
    log = np.where(seen > 0, np.log(np.maximum(seen, 1)), -BIG)
    slope = 2.0 ** (-np.arange(1, H + 1))
    return (slope[:, None, None] * off[None] - log[None]).astype(np.float32)


class Steps:

    def __init__(self, sem, keys):
        self.sem, self.at, self.done = sem, {k: n + 1 for n, k in enumerate(keys)}, 0

    def tick(self, ins, key):
        self.done += 1
        assert self.at[key] == self.done, (key, self.done)
        ins.then_inc(self.sem, 1)

    def wait(self, eng, key):
        eng.wait_ge(self.sem, self.at[key])


class Chain:

    def __init__(self, sem):
        self.sem, self.n = sem, 0

    def link(self, eng, ins):
        self.n += 1
        ins.then_inc(self.sem, 1)
        eng.wait_ge(self.sem, self.n)


class Banks:

    def __init__(self, banks, sems):
        self.banks, self.sems, self.order, self.at = banks, sems, [], {}
        self.opened = 0

    def plan(self, key, freed):
        self.at[key] = len(self.order)
        self.order.append((key, freed))

    def open(self, pe, key):
        n = self.at[key]
        assert n == self.opened, (key, n, self.opened)
        self.opened += 1
        if n >= 8:
            steps, step = self.order[n - 8][1]
            steps.wait(pe, step)
        return self.banks[n % 8]

    def close(self, ins, key):
        ins.then_inc(self.sems[self.at[key] % 8], 1)

    def filled(self, eng, key):
        n = self.at[key]
        eng.wait_ge(self.sems[n % 8], n // 8 + 1)
        return self.banks[n % 8]



def two_blocks(nc, consts_d, rope1_d, dist_d, h_d, y_d, inp, out):
    ctx = ExitStack()
    with ctx:
        cols, _, _ = constants()
        ncols = sum(w for _, w in cols.values())

        def sb(name, shape, dt=F32):
            return ctx.enter_context(nc.sbuf_tensor(name, shape, dt))

        def sem(name):
            return ctx.enter_context(nc.semaphore(name))

        def steps(name, keys):
            return Steps(sem(name), list(keys))

        def wide(v, n):
            return v.unsqueeze(len(v.shape)).broadcast_to(list(v.shape) + [n])

        const = sb("const", [P, ncols])

        def C(name, parts=P):
            a, w = cols[name]
            return const[0:parts, a:a + w]

        ident = C("ident")
        x = sb("x_res", [P, TT, D])
        hT_at = nc.sbuf_base
        hT = sb("hT", [P, KT, T])
        hTc = sb("hTc", [P, KT, CTX])
        xn = sb("xn", [P, AT, D])
        ring_at = nc.sbuf_base
        ring = sb("ring", [P, RING, UNIT])
        gains = sb("gains", [P, 6, KT])
        convw = sb("convw", [P, 224])
        ada_bias = sb("ada_bias", [P, 6, KT])
        cvec = sb("cvec", [P, 2, KT])
        csilu = sb("csilu", [P, KT, 32])
        mod = sb("mod", [P, 6, KT, 2])
        mod_gain = sb("mod_gain", [P, 3, KT])
        gates = sb("gates", [P, 2, D])
        dt_bias, a_log = sb("dt_bias", [P, 16]), sb("a_log", [P, 16])
        d_skip, sinks, route_bias = sb("d_skip", [P, 8]), sb("sinks", [P, 8]), sb("route_bias", [P, 36])
        route_w = sb("route_w", [P, KT, 36])
        sums, roots, rstd = sb("sums", [P, 12]), sb("roots", [P, 12]), sb("rstd", [P, 12])
        head_sum, head_root = sb("head_sum", [P, 2, 8]), sb("head_root", [P, 2, 8])
        nmin, psums, rsums = sb("nmin", [P, 96]), sb("psums", [P, 96]), sb("rsums", [P, 96])
        win_min, sink_exp = sb("win_min", [P, 72]), sb("sink_exp", [P, 32])
        arena_at = nc.sbuf_base
        arena = sb("arena", [P, ARENA])
        LOW_AT = 13312

        def over(name, shape, column):
            return nc.alloc_sbuf_tensor_at(name, shape, F32R, offset=column)

        hT_high = over("hT_high", [P, KT, T], hT_at)
        hT_low = over("hT_low", [P, KT, T], arena_at + 4 * LOW_AT)
        w_high = over("weights_high", [P, 2, HALF], ring_at + 4 * UNIT)
        w_low = over("weights_low", [P, 2, HALF], ring_at + 8 * UNIT)
        hid_high = hT_high[:, 0:4, :].rearrange("p (b f) n -> p b f n", b=2)
        hid_low = hT_high[:, 4:8, :].rearrange("p (b f) n -> p b f n", b=2)

        def carve(start, *shape, of=arena):
            n = int(np.prod(shape))
            v = of[:, start:start + n]
            names = "abcd"[:len(shape)]
            if len(shape) > 1:
                v = v.rearrange(f"p ({' '.join(names)}) -> p {' '.join(names)}",
                                **{k: s for k, s in zip(names[1:], shape[1:])})
            return v

        def packed(size_of, start=0, of=arena, limit=ARENA):
            views = []
            for shape in size_of:
                views.append(carve(start, *shape, of=of))
                start += int(np.prod(shape))
            assert start <= limit, start
            return views

        hT_flat = hT[:, :, :].rearrange("p j n -> p (j n)")
        ring_flat = ring[:, :, :].rearrange("p a n -> p (a n)")
        hTc_flat = hTc[:, :, :].rearrange("p j n -> p (j n)")
        spare = xn[:, TT:AT, :].rearrange("p t n -> p (t n)")

        vA, vB, pj, sq, qaT, qbT, kzA, kzB, dist, rope1, head_gain = packed(
            [(TT, 128), (TT, 512), (3, 512), (2, 512), (4, T), (4, T), (2, T), (8, T), (2, BIASW), (2, TT, HD),
             (4, HD)])
        junk1, rope_t = carve(0, D, of=spare), carve(D, 2, 512, of=spare)
        probs, probsT = packed([(2, T), (2, T)], of=hTc_flat, limit=2048)
        modrow = sq
        junk_c = carve(13400, D)
        conv_rows = carve(16900, 3, P)
        hid, conv_g, conv_v = packed([(FT, T), (2, T), (2, T)])
        zs, u, kvd, q2, xs_tok, b_tok = packed(
            [(TT, 512), (KT, T + CTX), (AT, 272), (TT, 512), (AT, 512), (AT, 256)])
        junk2 = carve(0, D)
        conv2 = carve(0, 2, T + CTX, of=spare)
        u_flat = carve(TT * 512, 4 * (T + CTX))
        slot = ring[:, 1, :]
        q2T, kz2 = carve(0, 4, T, of=slot), carve(2048, 2, T + CTX, of=slot)
        rope_q = carve(0, 2, 512, of=hTc_flat)
        wprobs = carve(TT * 512 + KT * (T + CTX) + AT * 272, 2, 640)
        wprobsT = carve(16480, 2, 640)
        state = carve(0, 2, 4, 512, of=hT_flat)
        state0, dtxw = packed([(2, 512), (2, 512)], of=hTc_flat, limit=2048)
        dtx, cbm, ytmp = packed([(2, 512), (2, 2, P), (512,)], of=spare, limit=2048)
        decay = u_flat[:, 0:3072].rearrange("p (a b c) -> p a b c", a=3, b=8)
        stmp = carve(TT * 512 + KT * (T + CTX) + AT * 272 + 2 * 640, 512)
        skip_x = carve(2048 + 2 * (T + CTX), 512, of=slot)
        sm = sb("ssd_small", [P, 10, 96])
        cat = xn

        ps = [ctx.enter_context(nc.psum_tensor(f"bank{i}", [P, 512], F32)) for i in range(8)]
        banks = Banks(ps, [sem(f"bank_filled{i}") for i in range(8)])

        x_in, const_in, more_in, ctx_in = [sem(f"x_in{t}") for t in range(TT)], sem("const_in"), sem("more_in"), sem("ctx_in")
        dist_in = [sem("dist_in0"), sem("dist_in1")]
        unit_in = {p: sem(f"unit_in_{p}") for p in ("slot0", "slot1", "slot2", "half0", "half1")}
        dve_chain, act_chain, pool_chain = Chain(sem("dve_order")), Chain(sem("act_order")), Chain(sem("pool_order"))

        zero = C("zero")
        XT, XC = range(TT), range(TT, AT)
        NORMS = {
            "norm1": (lambda t: x[:, t, :], XT, [(0, D)], junk1, lambda j: (gains[:, 0, j:j + 1], zero)),
            "mix1": (lambda t: xn[:, t, :], XT, [(0, 512), (512, D)], junk1, lambda j: (gains[:, 1, j:j + 1], zero)),
            "norm2": (lambda t: x[:, t, :], XT, [(0, D)], junk1, lambda j: (gains[:, 2, j:j + 1], zero)),
            "context": (lambda t: xn[:, t, :], XC, [(0, D)], junk_c,
                        lambda j: (mod_gain[:, 1, j:j + 1], mod[:, 0, j, 1:2])),
            "norm1_2": (lambda t: x[:, t, :], XT, [(0, D)], junk2,
                        lambda j: (mod_gain[:, 0, j:j + 1], mod[:, 0, j, 0:1])),
            "mix2": (lambda t: cat[:, t, :], XT, [(0, 512)], u_flat[:, 0:D], lambda j: (gains[:, 4, j:j + 1], zero)),
            "norm2_2": (lambda t: x[:, t, :], XT, [(0, D)], hTc_flat[:, 0:D],
                        lambda j: (mod_gain[:, 2, j:j + 1], mod[:, 3, j, 0:1])),
        }
        norm_keys = [(s, t, a) for s, (_, tiles, parts, _, _) in NORMS.items() for t in tiles for a, _ in parts]
        squared = steps("norm_squared", norm_keys + [("final", t, 0) for t in range(TT)])
        rooted = steps("norm_rooted", [(s, t) for s, n in NORMS.items() for t in n[1]] + [("final", t) for t in range(TT)])
        normed = steps("normed", norm_keys)

        def halves(s):
            return [(s, j) for j in range(KT)]

        SPLIT_NORMS = ("norm2",)
        hT_act = steps("hT_by_act", [k for s in NORMS for k in halves(s) if k[1] % 2 == 0 or s in SPLIT_NORMS])
        hT_dve = steps("hT_by_dve", [k for s in NORMS for k in halves(s) if k[1] % 2 == 1 or s in SPLIT_NORMS])

        def hT_step(k):
            return hT_act if k[1] % 2 == 0 and k[0] not in SPLIT_NORMS else hT_dve

        PROJ = [(c, t) for c in range(5) for t in range(TT)]
        HEADS_OF = [[(0, 8, 0)], [(0, 2, 1), (4, 4, 2)], [(0, 4, 2), (4, 4, 3)], [(0, 4, 3)]]
        conv_ready = steps("conv_weights", ["taps"])
        pj_ready = steps("proj_copied", range(16))
        v_tail = steps("v_tail", range(TT))
        head_summed = steps("head_summed", range(16))
        head_rooted = steps("head_rooted", range(16))
        qk_ready = steps("qk_normed", range(16))
        qk_drained = steps("qk_transposed", range(16))

        NU = 2 * H * TT
        score_min = steps("score_min", range(NU))
        prob = steps("prob", range(NU))
        pt_act = steps("probsT_by_act", range(0, NU, 2))
        pt_dve = steps("probsT_by_dve", range(1, NU, 2))
        att = steps("attended", range(NU))
        mod_silu = steps("mod_silu", ["c"])
        mod_copied = steps("mod_copied", range(12))
        mod_done = steps("mod_done", list(range(12)) + ["gains"])

        def pt_step(i):
            return pt_dve if i % 2 else pt_act

        SIDES = [(t, n) for t in range(TT) for n in range(2)]
        x1 = steps("x_after_attention", SIDES)
        tap_mid = steps("conv_middle_tap", [(f, g) for f in range(FT) for g in range(2)])
        tapped = steps("conv_tapped", [(f, g) for f in range(FT) for g in range(2)])
        gelued = steps("gelued", range(FT))
        hidden = steps("hidden", range(FT))
        ND = FT // 2
        SPLITS = [("w_up", f) for f in range(FT)] + [("w_down", i) for i in range(ND)]
        high_ready = steps("weights_high_ready", range(len(SPLITS)))
        low_ready = steps("weights_low_ready", range(len(SPLITS)))
        hid_high_ready = steps("hidden_high_ready", range(ND))
        hid_low_ready = steps("hidden_low_ready", range(ND))
        down_read = steps("down_weights_read", range(ND - 1))
        x2 = steps("x_after_ffn", SIDES)

        kvd_copied = steps("kv_dt_copied", range(AT))
        XBC = [(m, c) for m in range(KT) for c in range(2)]
        mid2 = steps("conv2_middle_tap", XBC)
        tapped2 = steps("conv2_tapped", XBC)
        u_ready = steps("conv2_silu", range(KT))
        z_ready = steps("z_silu", range(TT))
        q_copied = steps("q_copied", range(TT))
        roped = steps("roped", [("k", t) for t in range(TT)] + [("q", t) for t in range(TT)])
        tok_copied = steps("tokens_first", [("xs", t) for t in range(AT)] + [("b", t) for t in range(0, AT, 2)])
        kz_ready = steps("k_transposed", range(2))
        q2_ready = steps("q_transposed", range(4))
        csilu_cleared = steps("csilu_cleared", [0])
        row_ready = sem("row_ready")
        dt_abs, dt_exp, dt_log = steps("dt_abs", [0, 1]), steps("dt_exp", [0]), steps("dt_log", [0])
        a_exp = steps("a_exp", [0])
        dta_ready = steps("dt_times_a", [0])
        cs_copied = steps("cumsums", [0])
        cs_exp = steps("cumsum_exps", [0])
        sw_ready = steps("state_weights", [0])

        TILE_AT = [[TT, TT + 1, 0, 1, 2, 3], [TT + 1, TT, 3, 2, 1, 0]]
        STATES = [(d, i) for i in range(5) for d in range(2)]
        NW = H * TT
        YS = [(t, d) for t in range(TT) for d in range(2)]
        ssd = [("state", k) for k in range(len(STATES))] + [("y", k) for k in range(len(YS) + 2)]
        weave, n = [], 0
        for i in range(NW + 2):
            weave.append(("win", i))
            while n * (NW + 2) < len(ssd) * (i + 1) and n < len(ssd):
                weave.append(ssd[n])
                n += 1
        dtxw_ready = steps("weighted_x", range(len(STATES)))
        state_ready = steps("state_ready", range(len(STATES)))
        dtx_ready = steps("dt_x", range(len(YS)))
        cb_masked = steps("cb_masked", range(TT))
        seg_ready = steps("segments", [(k, g) for k in range(len(YS)) for g in range(2)])
        decayed = steps("decay_exp", range(len(YS)))
        m_ready = steps("decay_times_cb", range(len(YS)))
        y_read = steps("y_read", [(k, w) for k in range(len(YS)) for w in ("off", "diag")] )
        y_done = steps("y_done", range(TT))
        wscore = steps("win_score", range(NW))
        wprob = steps("win_prob", range(NW))
        wpt_act = steps("win_probsT", range(NW))
        watt = steps("win_attended", range(NW))
        x3 = steps("x_after_mixers", SIDES)

        def near(t):
            return max(0, t - 1), min(TT - 1, t + 1)

        def plan_norm(s):
            for k in halves(s):
                banks.plan(("hT",) + k, (hT_step(k), k))

        plan_norm("norm1")
        for n in range(len(PROJ) + 2):
            if n < len(PROJ):
                banks.plan(("proj", n), (pj_ready, n) if n < 16 else (v_tail, n - 16))
            if 2 <= n < 18:
                banks.plan(("qkT", n - 2), (qk_drained, n - 2))
        banks.plan("conv_weights", (conv_ready, "taps"))
        for i in range(NU + 2):
            if i < NU:
                banks.plan(("score", i), (prob, i) if i < NU // 2 else (score_min, i))
            if 1 <= i <= NU:
                banks.plan(("probsT", i - 1), (pt_step(i - 1), i - 1))
            if i >= 2:
                banks.plan(("att", i - 2), (att, i - 2))
            if i % 5 == 2 and i // 5 < 12:
                banks.plan(("modrow", i // 5), (mod_copied, i // 5))
            if i % 5 == 4 and i // 5 < 12:
                banks.plan(("mod", i // 5), (mod_done, i // 5))
        plan_norm("mix1")
        for k in SIDES:
            banks.plan(("out1",) + k, (x1, k))
        plan_norm("norm2")
        for f in range(FT):
            for g in range(2):
                banks.plan(("up", f, g), (tapped, (f, g)))
        plan_norm("context")
        for k in SIDES:
            banks.plan(("down",) + k, (x2, k))
        plan_norm("norm1_2")
        for t in range(AT):
            banks.plan(("kvd", t), (kvd_copied, t))
        for k in XBC:
            banks.plan(("xbc",) + k, (tapped2, k))
        for t in range(TT):
            banks.plan(("z", t), (z_ready, t))
        for t in range(TT):
            banks.plan(("q2", t), (q_copied, t))
        banks.plan("cumsum", (cs_copied, 0))
        for t in range(AT):
            banks.plan(("xs", t), (tok_copied, ("xs", t)))
        for t in range(0, AT, 2):
            banks.plan(("b", t), (tok_copied, ("b", t)))
        for n in range(2):
            banks.plan(("kT", n), (kz_ready, n))
        for j in range(4):
            banks.plan(("q2T", j), (q2_ready, j))
        for what, i in weave:
            if what == "win":
                if i < NW:
                    banks.plan(("wscore", i, 0), (wscore, i))
                    banks.plan(("wscore", i, 1), (wscore, i))
                if 1 <= i <= NW:
                    banks.plan(("wprobsT", i - 1, 0), (wpt_act, i - 1))
                    banks.plan(("wprobsT", i - 1, 1), (wpt_act, i - 1))
                if i >= 2:
                    banks.plan(("watt", i - 2), (watt, i - 2))
            elif what == "state":
                banks.plan(("state", i), (state_ready, i))
            else:
                if i < len(YS):
                    if i % 2 == 0:
                        banks.plan(("cb", i // 2), (cb_masked, i // 2))
                    banks.plan(("seg", i, 0), (seg_ready, (i, 0)))
                    banks.plan(("seg", i, 1), (seg_ready, (i, 1)))
                if i >= 2:
                    banks.plan(("yoff", i - 2), (y_read, (i - 2, "off")))
                    banks.plan(("ydiag", i - 2), (y_read, (i - 2, "diag")))
        plan_norm("mix2")
        for k in SIDES:
            banks.plan(("out2",) + k, (x3, k))
        plan_norm("norm2_2")

        def by_k(name):
            return inp[name].rearrange("(p j) n -> p j n", j=KT)

        win_v, wout_v, wup_v = by_k("w_in"), by_k("w_out"), by_k("w_up")
        wada_v = inp["w_ada_2"].rearrange("a (p j) n -> p (a j) n", j=KT)
        win2_v = inp["w_in_2"].rearrange("a (p j) n -> p (a j) n", j=KT)
        wout2_v = inp["w_out_2"].rearrange("a (p j) n -> p (a j) n", j=KT)
        wdown_v = inp["w_down"].rearrange("(f p) n -> p f n", p=P)
        PLACES = {"slot0": (0, UNIT), "slot1": (UNIT, UNIT), "slot2": (2 * UNIT, UNIT), "half0": (0, HALF),
                  "half1": (HALF, HALF)}
        UNITS = []

        def unit(key, place, width, parts, free):
            UNITS.append((key, place, width, parts, free))

        for c in range(5):
            w = min(512, W1 - c * 512)
            unit(("w_in", c), f"slot{(c + 1) % RING}", w, [(0, win_v[:, :, c * 512:c * 512 + w])],
                 ("proj", c * TT + TT - 1))
        for m in range(12):
            unit(("w_ada", m), f"slot{m % RING}", 512, [(0, wada_v[:, :, m * 512:m * 512 + 512])], ("modrow", m))
        for n in range(2):
            unit(("w_out", n), f"slot{1 + n}", 512, [(0, wout_v[:, :, n * 512:n * 512 + 512])], ("out1", TT - 1, n))
        for f in range(FT):
            unit(("w_up", f), f"half{f % 2}", 256, [(0, wup_v[:, :, f * P:f * P + P]),
                                                    (P, wup_v[:, :, DFF + f * P:DFF + f * P + P])], ("split", f))
        for i in range(ND):
            unit(("w_down", i), f"half{i % 2}", D, [(0, wdown_v[:, 2 * i:2 * i + 2, :])], ("split", FT + i))
        unit("w_kvd", "slot0", 272, [(0, win2_v[:, :, 1536:1552]), (16, win2_v[:, :, 2064:2320])], ("kvd", AT - 1))
        for n in range(2):
            unit(("w_xbc", n), f"slot{1 + n}", 512, [(0, win2_v[:, :, 512 + n * 512:1024 + n * 512])],
                 ("xbc", 4 * n + 3, 1))
        unit("w_z", "slot0", 512, [(0, win2_v[:, :, 0:512])], ("z", TT - 1))
        unit("w_q", "slot1", 512, [(0, win2_v[:, :, 1552:2064])], ("q2", TT - 1))
        for n in range(2):
            unit(("w_out2", n), f"slot{2 - 2 * n}", 512, [(0, wout2_v[:, :, n * 512:n * 512 + 512])],
                 ("out2", TT - 1, n))
        UNIT_AT, UNIT_AFTER, count, lies = {}, {}, {p: 0 for p in PLACES}, {}
        for key, place, width, parts, free in UNITS:
            count[place] += 16 * len(parts)
            UNIT_AT[key] = (place, width, count[place])
            a, n = PLACES[place]
            gone = [p for p in lies if PLACES[p][0] < a + n and a < sum(PLACES[p])]
            UNIT_AFTER[key] = [lies.pop(p) for p in gone]
            if key[0] == "w_xbc":
                UNIT_AFTER[key] = [("down", TT - 1, 1)]
            lies[place] = free

        def unit_view(place, width, rows):
            a = PLACES[place][0]
            return ring_flat[:, a:a + rows * width].rearrange("p (j n) -> p j n", n=width)

        def weights(pe, key):
            place, width, value = UNIT_AT[key]
            pe.wait_ge(unit_in[place], value)
            return unit_view(place, width, PLACES[place][1] // width if width != 272 else KT)

        def halfway(key, part):
            return part.rearrange("p (j n) -> p j n", n=UNIT_AT[key][1])

        EXPERT_SLOTS = [ring[:, i, :] for i in range(3)] + [arena[:, i * UNIT:(i + 1) * UNIT] for i in range(3)]
        (hot_p, hot_b, lg, gl, g8, e8, el, ohot, osum, tot, rank, prod, first, novf, over_cnt, start, later,
         pk, bk, quo, over_place, gexp, gsum, wts, tval, lgT) = packed(
            [(8, P), (8, 2, NBLK), (TT, 36), (TT, 8), (TT, 8), (TT, 8), (TT, E), (TT, 2, E), (TT, E), (TT, E),
             (TT, E), (TT, 2, E), (E,), (E,), (E, T // BLK - 1), (2, E), (NOVF, E), (8,), (8,), (8,),
             (8, T // BLK - 1), (TT, 4), (TT,), (TT, 6), (3, 2 * NBLK), (T,)], start=3 * UNIT)
        gi, ei = sb("group_index", [P, TT, 8], U32), sb("expert_index", [P, TT, 8], U32)
        gif, eif = sb("group_index_f", [P, TT]), sb("expert_index_f", [P, TT, 2])
        tok_of, row_of = sb("token_of_place", [P, NBLK], I32), sb("row_of_place", [P, NBLK], I32)
        later_cnt = sb("later_counts", [P, 16])
        ovf = sb("later_blocks", [1, NOVF + 1], I32)
        tok_at, row_at = sb("token_index", [P, 2], I32), sb("row_index", [P, 2], I32)
        xg = carve(0, 2, D, of=spare)
        xT, gu = packed([(2, KT, BLK), (2, 512)], of=hTc_flat, limit=2048)
        sg, hidE, yE = packed([(2, 4, BLK), (2, 4, BLK), (2, 512)], of=hT_flat, limit=KT * T)
        final_gain = carve(0, D, of=xn[:, 0:1, :].rearrange("p a n -> p (a n)"))
        junk3 = carve(0, D, of=xn[:, 1:2, :].rearrange("p a n -> p (a n)"))
        y01 = ring[:, 0:2, :].rearrange("p a n -> p (a n)").rearrange("p (t k n) -> p t k n", t=TT, k=2)
        expert_in = [sem(f"expert_in{i}") for i in range(6)]
        h_stored, y01_in, final_in, stored = sem("h_stored"), [sem(f"y01_in{t}") for t in range(TT)], sem("final_gain_in"), sem("stored")
        tokens_in = [sem("tokens_in0"), sem("tokens_in1")]
        y_stored = [sem("y_stored0"), sem("y_stored1")]
        index_ready, scattered = sem("index_ready"), sem("all_y_stored")
        xt_filled, xt_scaled, xt_ready = sem("expert_x_filled"), sem("expert_x_scaled"), sem("expert_x_ready")
        gu_filled, gu_ready = sem("gate_up_filled"), sem("gate_up_ready")
        ht_filled, silu_ready, hid_ready = sem("hiddenT_filled"), sem("expert_silu"), sem("expert_hidden")
        y_filled, y_ready = sem("expert_y_filled"), sem("expert_y_ready")
        route = steps("route", ["cleared", "odd", "logits", "max", "top2", "hot", "weights", "places", "table"])
        route_act = steps("route_act", ["even", "group_exp", "pair_exp"])
        route_pe = steps("route_pe", ["halves", "logits", "rank", "table"])
        final_x = steps("final_x", range(TT))
        final_y = steps("final_y", range(TT))

        small_loads = []

        def small(dst, src):
            small_loads.append((dst, src))

        FIRST_LOADS = 2
        small(const[:, :], consts_d)
        small(gains[:, 0, :], inp["norm1_g"].rearrange("(p j) -> p j", j=KT))
        small(rope1.rearrange("p a t d -> p (a t d)"), rope1_d)
        small(gains[:, 2, :], inp["norm2_g"].rearrange("(p j) -> p j", j=KT))
        small(gains[0:64, 1, :], inp["outa_norm_g"].rearrange("(p j) -> p j", j=KT))
        small(gains[64:128, 1, :], inp["outb_norm_g"].rearrange("(p j) -> p j", j=KT))
        small(gains[:, 3, :], inp["norm1_2"].rearrange("a (p j) -> p (a j)", j=KT))
        small(gains[0:64, 4, :], inp["ssd_norm_2"].rearrange("a (p j) -> p (a j)", j=KT))
        small(gains[:, 5, :], inp["norm2_2"].rearrange("a (p j) -> p (a j)", j=KT))
        for n, name in enumerate(("qa_norm_g", "ka_norm_g", "qb_norm_g", "kb_norm_g")):
            small(head_gain[:, n, :], inp[name].partition_broadcast(P))
        small(conv_rows[0:88, 0, :], inp["conv_w"][0:2, :].rearrange("k (f p) -> (k f) p", p=P))
        small(conv_rows[0:44, 1, :], inp["conv_w"][2, :].rearrange("(f p) -> f p", p=P))
        small(conv_rows[44:88, 1, :], inp["conv_b"].rearrange("(f p) -> f p", p=P))
        small(conv_rows[0:40, 2, :], inp["conv_w_2"].rearrange("a k (f p) -> (a k f) p", p=P))
        small(conv_rows[40:48, 2, :], inp["conv_b_2"].rearrange("a (f p) -> (a f) p", p=P))
        small(ada_bias[:, :, :], inp["b_ada_2"].rearrange("a (s p j) -> p (a s) j", s=6, j=KT))
        small(cvec[:, 0, :], inp["c_2"].rearrange("a (p j) -> p (a j)", j=KT))
        small(cvec[:, 1, :], inp["c_ctx_2"].rearrange("(p j) -> p j", j=KT))
        small(gates[:, 0, :], inp["b_ada_2"][0, 2 * D:3 * D].partition_broadcast(P))
        small(gates[:, 1, :], inp["b_ada_2"][0, 5 * D:6 * D].partition_broadcast(P))
        small(dt_bias[:, :], inp["dt_bias_2"].rearrange("a d h -> (a d h)").partition_broadcast(P))
        small(a_log[:, :], inp["a_log_2"].rearrange("a d h -> (a d h)").partition_broadcast(P))
        small(d_skip[:, :], inp["d_skip_2"].rearrange("a h -> (a h)").partition_broadcast(P))
        small(sinks[:, :], inp["attn_sinks_2"].rearrange("a h -> (a h)").partition_broadcast(P))
        small(route_bias[:, 0:4], inp["b_group_2"].rearrange("a h -> (a h)").partition_broadcast(P))
        small(route_bias[:, 4:36], inp["b_expert_2"].rearrange("a h -> (a h)").partition_broadcast(P))
        small(route_w[:, :, 0:4], inp["w_group_2"].rearrange("a (p j) n -> p (a j) n", j=KT))
        small(route_w[:, :, 4:36], inp["w_expert_2"].rearrange("a (p j) n -> p (a j) n", j=KT))
        CONST_ALL = 16 * FIRST_LOADS
        MORE_ALL = 16 * (len(small_loads) - FIRST_LOADS)
        block = ctx.enter_context(nc.Block())

        def held(eng, value):
            return value if isinstance(value, int) else eng.to_reg(value)

        def load_expert(sp, e, par, kpar, reuse):
            for i, (name, pat) in enumerate((("w_gate_2", "a e (p j) f -> (a e) p (j f)"),
                                             ("w_up_2", "a e (p j) f -> (a e) p (j f)"),
                                             ("w_down_2", "a e (p f) d -> (a e) p (f d)"))):
                kw = {"f": 4} if i == 2 else {"j": KT}
                if reuse is not None:
                    sp.wait_ge(gu_filled if i < 2 else y_filled, reuse)
                sp.dma_start(EXPERT_SLOTS[3 * par + i], inp[name].rearrange(pat, **kw)[e]).then_inc(
                    expert_in[3 * par + i], 16)

        @block.sync
        def _(sp):
            for t in range(TT):
                sp.dma_start(x[:, t, :], inp["x"][0, t * P:(t + 1) * P, :]).then_inc(x_in[t], 16)
            for key, place, width, parts, _ in UNITS:
                if key == ("w_up", 4):
                    squared.wait(sp, ("norm2", TT - 1, 0))
                    sp.dma_start(xn[:, TT:AT, :], inp["ctx_2"].rearrange("a (t p) n -> p (a t) n", p=P)).then_inc(
                        ctx_in, 16)
                for free in UNIT_AFTER[key]:
                    if free[0] == "split":
                        low_ready.wait(sp, free[1])
                    else:
                        banks.filled(sp, free)
                for c, src in parts:
                    rows, w = src.shape[1], src.shape[2]
                    sp.dma_start(unit_view(place, width, rows)[:, :, c:c + w], src).then_inc(unit_in[place], 16)
            banks.filled(sp, ("out2", TT - 1, 1))
            load_expert(sp, 0, 0, 0, None)
            normed.wait(sp, ("norm2_2", TT - 1, 0))
            sp.dma_start(h_d.rearrange("(t p) n -> p t n", p=P), xn[:, 0:TT, :]).then_inc(h_stored, 16)
            load_expert(sp, 1, 1, 0, None)
            with sp.Fori(1, E // 2) as it:
                for par in range(2):
                    load_expert(sp, 2 * it + par, par, it, 2 * it + par - 1)
            route.wait(sp, "table")
            later_n = sp.value_load(ovf[0:1, NOVF:NOVF + 1], min_val=0, max_val=NOVF)
            with sp.If(later_n > 0):
                with sp.Fori(0, later_n) as i:
                    e = sp.value_load(ovf[0:1, bass.ds(i, 1)], min_val=0, max_val=E - 1)
                    load_expert(sp, e, 0, i + E // 2, i + E)
            sp.wait_ge(h_stored, 16)
            sp.dma_start(final_gain, inp["norm_final_2"].partition_broadcast(P)).then_inc(final_in, 16)
            sp.wait_ge(scattered, 1)
            for t in range(TT):
                sp.dma_start(y01[:, t, :, :].rearrange("p k n -> p (k n)"),
                             y_d[4 * t * P:4 * (t + 1) * P, :].rearrange("(p r) n -> p (r n)", r=4)).then_inc(
                                 y01_in[t], 16)
            for t in range(TT):
                final_y.wait(sp, t)
                sp.dma_start(out[0, t * P:(t + 1) * P, :], y01[:, t, 0, :]).then_inc(stored, 16)
            sp.wait_ge(stored, 16 * TT)

        @block.gpsimd
        def _(pool):
            g = nc.gpsimd
            for h in range(H):
                if h >= 2:
                    score_min.wait(pool, (H + h - 1) * TT - 1)
                pool.dma_start(dist[:, h % 2, :], dist_d[h]).then_inc(dist_in[h % 2], 16)
            pool.wait_ge(const_in, CONST_ALL)
            banks.filled(pool, ("q2", 0))

            def rope(dst, src, heads, t):
                a, b = (rope_q[:, i, 0:heads * HD] for i in range(2))
                cos, sin = (C(n).rearrange("p (t d) -> p t d", t=TT)[:, t, :] for n in ("cos2", "sin2"))
                s3 = src.rearrange("p (h d) -> p h d", d=HD)
                a3, b3 = (v.rearrange("p (h d) -> p h d", d=HD) for v in (a, b))
                g.tensor_tensor(a3, s3, cos.unsqueeze(1).broadcast_to([P, heads, HD]), ALU.mult)
                for half in range(2):
                    lo, other = half * 32, 32 - half * 32
                    last = g.tensor_tensor(b3[:, :, lo:lo + 32], s3[:, :, other:other + 32],
                                           sin[:, lo:lo + 32].unsqueeze(1).broadcast_to([P, heads, 32]), ALU.mult)
                pool_chain.link(pool, last)
                return a, b

            for t in range(TT):
                kvd_copied.wait(pool, t)
                k = kvd[:, t, 16:144]
                a, b = rope(k, k, 2, t)
                ins = g.tensor_tensor(k, a, b, ALU.add)
                roped.tick(ins, ("k", t))
                roped.wait(pool, ("k", t))
            for t in range(TT):
                q_copied.wait(pool, t)
                a, b = rope(q2[:, t, :], q2[:, t, :], H, t)
                dst = q2[:, t, :].rearrange("p (j half d) -> p half j d", j=4, half=2)
                ins = g.tensor_tensor(dst, a.rearrange("p (half j d) -> p half j d", j=4, half=2),
                                      b.rearrange("p (half j d) -> p half j d", j=4, half=2), ALU.add)
                roped.tick(ins, ("q", t))
                roped.wait(pool, ("q", t))
            sw_ready.wait(pool, 0)
            u_ready.wait(pool, KT - 1)
            for what, k in weave:
                if what == "state":
                    d, i = STATES[k]
                    t = TILE_AT[d][i]
                    tok_copied.wait(pool, ("xs", t))
                    if k >= 2:
                        banks.filled(pool, ("state", k - 2))
                    ins = g.tensor_tensor(dtxw[:, k % 2, :].rearrange("p (h d) -> p h d", d=HD),
                                          xs_tok[:, t, :].rearrange("p (h d) -> p h d", d=HD),
                                          wide(sm[:, 9, t * 16 + d * 8:t * 16 + d * 8 + 8], HD), ALU.mult)
                    dtxw_ready.tick(ins, k)
                elif what == "y":
                    if k >= 2:
                        banks.filled(pool, ("ydiag", k - 2))
                    if k < len(YS):
                        t, d = YS[k]
                        ins = g.tensor_tensor(dtx[:, k % 2, :].rearrange("p (h d) -> p h d", d=HD),
                                              xs_tok[:, t, :].rearrange("p (h d) -> p h d", d=HD),
                                              wide(sm[:, 5, t * 16 + d * 8:t * 16 + d * 8 + 8], HD), ALU.mult)
                        dtx_ready.tick(ins, k)
                    if k >= 2 and YS[k - 2][1] == 1:
                        t, row = YS[k - 2][0], cat[:, YS[k - 2][0], 0:512]
                        pool_chain.link(pool, g.tensor_tensor(
                            skip_x.rearrange("p (h d) -> p h d", d=HD), xs_tok[:, t, :].rearrange("p (h d) -> p h d", d=HD),
                            wide(d_skip[:, :], HD), ALU.mult))
                        y_read.wait(pool, (k - 2, "diag"))
                        pool_chain.link(pool, g.tensor_tensor(row, row, skip_x, ALU.add))
                        y_done.tick(g.tensor_tensor(row, row, zs[:, t, :], ALU.mult), t)
            x3.wait(pool, SIDES[-1])
            pool_chain.link(pool, g.memset(xg, 0.0))
            route.wait(pool, "table")
            pool.wait_ge(h_stored, 16)

            def gather(n, e, par, reuse):
                if reuse is not None:
                    pool.wait_ge(xt_filled, reuse)
                g.tensor_copy(tok_at[:, par:par + 1], tok_of[:, bass.ds(e, 1)]).then_inc(index_ready, 1)
                after = held(pool, n + 1)
                pool.wait_ge(const_in, CONST_ALL)
                pool.wait_ge(index_ready, after)
                g.indirect_dma_start(xg[0:BLK, par, :], None, h_d, bass.IndirectOffsetOnAxis(
                    ap=tok_at[0:BLK, par:par + 1], axis=0), bounds_check=T - 1, oob_is_err=False).then_inc(
                        tokens_in[par], 16)

            def scatter(n, e, par, stored_before):
                if stored_before is not None:
                    pool.wait_ge(y_stored[par], stored_before)
                g.tensor_copy(row_at[:, par:par + 1], row_of[:, bass.ds(e, 1)]).then_inc(row_ready, 1)
                after = held(pool, n + 1)
                pool.wait_ge(const_in, CONST_ALL)
                pool.wait_ge(row_ready, after)
                pool.wait_ge(y_ready, after)
                g.indirect_dma_start(y_d, bass.IndirectOffsetOnAxis(ap=row_at[:, par:par + 1], axis=0),
                                     yE[:, par, :], None, bounds_check=4 * T - 1, oob_is_err=False).then_inc(
                                         y_stored[par], 16)

            gather(0, 0, 0, None)
            gather(1, 1, 1, None)
            scatter(0, 0, 0, None)
            with pool.Fori(1, E // 2) as it:
                gather(2 * it, 2 * it, 0, 2 * it - 1)
                pool.wait_ge(y_stored[0], 16 * it)
                scatter(2 * it - 1, 2 * it - 1, 1, None)
                gather(2 * it + 1, 2 * it + 1, 1, 2 * it)
                pool.wait_ge(y_stored[1], 16 * it)
                scatter(2 * it, 2 * it, 0, None)
            scatter(E - 1, E - 1, 1, 16 * (E // 2 - 1))
            pool.wait_ge(y_stored[0], 16 * (E // 2))
            pool.wait_ge(y_stored[1], 16 * (E // 2))
            later_n = pool.value_load(ovf[0:1, NOVF:NOVF + 1], min_val=0, max_val=NOVF)
            with pool.If(later_n > 0):
                with pool.Fori(0, later_n) as i:
                    gather(i + E, i + E, 0, i + E)
                    scatter(i + E, i + E, 0, None)
                    pool.wait_ge(y_stored[0], 16 * i + 16 * (E // 2 + 1))
            g.memset(tok_at[:, 0:1], 0).then_inc(scattered, 1)

        @block.scalar
        def _(act):
            s = nc.scalar
            for dst, src in small_loads[:FIRST_LOADS]:
                act.dma_start(dst, src).then_inc(const_in, 16)
            act.wait_ge(const_in, CONST_ALL)
            eps = C("eps")

            def root(dst, src, width):
                return s.activation(dst, src, ACT.Sqrt, scale=1.0 / width, bias=eps)

            def high_part(k):
                place, width, value = UNIT_AT[SPLITS[k]]
                act.wait_ge(unit_in[place], value)
                if k >= 2 + FT:
                    down_read.wait(act, k - 2 - FT)
                else:
                    banks.filled(act, ("up", k - 2, 1) if k >= 2 else ("out1", TT - 1, 1))
                a = PLACES[place][0]
                high_ready.tick(s.activation(w_high[:, k % 2, :], ring_flat[:, a:a + HALF], ACT.Copy), k)

            def hidden_high(i):
                hidden.wait(act, 2 * i + 1)
                if i >= 2:
                    down_read.wait(act, i - 2)
                else:
                    banks.filled(act, ("up", FT - 1, 1))
                hid_high_ready.tick(s.activation(hid_high[:, i % 2, :, :], hid[:, 2 * i:2 * i + 2, :], ACT.Copy), i)

            def norm(name, before=None, between=None):
                src, tiles, parts, junk, gain = NORMS[name]
                n = len(parts)
                for t in tiles:
                    if before is not None:
                        before(t)
                    for i, (a, b) in enumerate(parts):
                        squared.tick(s.activation(junk[:, a:b], src(t)[:, a:b], ACT.Square,
                                                  accum_out=sums[:, t * n + i:t * n + i + 1]), (name, t, a))
                    squared.wait(act, (name, t, parts[-1][0]))
                    rooted.tick(root(roots[:, t * n:t * n + n], sums[:, t * n:t * n + n], parts[0][1] - parts[0][0]),
                                (name, t))
                if between is not None:
                    between()
                for k in halves(name):
                    if k[1] % 2 == 0 or name in SPLIT_NORMS:
                        j = k[1]
                        bank = banks.filled(act, ("hT",) + k)
                        dst = hTc[:, j, :] if name == "context" else (hT_high if name in SPLIT_NORMS else hT)[:, j, :]
                        sc, sh = gain(j)
                        hT_act.tick(s.activation(dst, bank[:, 0:dst.shape[1]], ACT.Identity, scale=sc, bias=sh), k)

            norm("norm1", lambda t: act.wait_ge(x_in[t], 16))
            for dst, src in small_loads[FIRST_LOADS:]:
                act.dma_start(dst, src).then_inc(more_in, 16)
            low, high = C("low"), C("high")
            for n in range(18):
                if n < 16:
                    c, t = PROJ[n]
                    bank = banks.filled(act, ("proj", n))
                    if n >= 3:
                        banks.filled(act, ("qkT", n - 3))
                    if n >= 2:
                        head_summed.wait(act, n - 2)
                    if c == 1:
                        s.activation(vA[:, t, :], bank[:, 128:256], ACT.Copy)
                    if c == 3:
                        s.activation(vB[:, t, 0:256], bank[:, 256:512], ACT.Copy)
                    s.activation(pj[:, n % 3, :], bank[:, :], ACT.Copy)
                    pj_ready.tick(s.activation(sq[:, n % 2, :], bank[:, :], ACT.Square), n)
                    head_summed.wait(act, n)
                    head_rooted.tick(root(head_root[:, n % 2, :], head_sum[:, n % 2, :], HD), n)
                if n >= 2:
                    m = n - 2
                    c, t = PROJ[m]
                    bank = banks.filled(act, ("qkT", m))
                    b3 = bank[:, :].rearrange("p (j n) -> p j n", j=4)
                    at = slice(t * P, t * P + P)
                    if c == 0:
                        ins = s.activation(qaT[:, :, at], b3, ACT.Copy)
                    if c == 1:
                        s.activation(qbT[:, 0:2, at], b3[:, 2:4, :], ACT.Copy)
                        s.activation(kzA[:, 0, at], b3[:, 0, :], ACT.Copy, scale=low)
                        ins = s.activation(kzA[:, 1, at], b3[:, 0, :], ACT.Copy, scale=high)
                    if c == 2:
                        s.activation(qbT[:, 2:4, at], b3[:, 0:2, :], ACT.Copy)
                    if c >= 2:
                        keys = b3[:, 2:4, :] if c == 2 else b3[:, 0:2, :]
                        dst = kzB[:, 4 * (c - 2):4 * (c - 1), at].rearrange("p (j two) n -> p two j n", two=2)
                        s.activation(dst[:, 0, :, :], keys, ACT.Copy, scale=low)
                        ins = s.activation(dst[:, 1, :, :], keys, ACT.Copy, scale=high)
                    qk_drained.tick(ins, m)
            act.wait_ge(more_in, MORE_ALL)
            csilu_cleared.wait(act, 0)
            s.activation(csilu[:, :, 0], cvec[:, 0, :], ACT.Silu)
            mod_silu.tick(s.activation(csilu[:, :, 1], cvec[:, 1, :], ACT.Silu), "c")
            for i in range(NU + 2):
                if i < NU:
                    score_min.wait(act, i)
                    if i >= 2:
                        banks.filled(act, ("probsT", i - 2))
                    src = banks.filled(act, ("score", i))[:, :] if i < NU // 2 else probs[:, i % 2, :]
                    prob.tick(s.activation(probs[:, i % 2, :], src, ACT.Exp, scale=-1.0, bias=nmin[:, i:i + 1],
                                           accum_out=psums[:, i:i + 1]), i)
                if 1 <= i <= NU and (i - 1) % 2 == 0:
                    bank = banks.filled(act, ("probsT", i - 1))
                    if i >= 3:
                        banks.filled(act, ("att", i - 3))
                    pt_act.tick(s.activation(probsT[:, (i - 1) % 2, :], bank[:, :], ACT.Copy), i - 1)
                if i % 5 == 2 and i // 5 < 12:
                    m = i // 5
                    bank = banks.filled(act, ("modrow", m))
                    if m >= 2:
                        mod_done.wait(act, m - 2)
                    mod_copied.tick(s.activation(modrow[:, m % 2, :], bank[:, :], ACT.Copy), m)
            norm("mix1", lambda t: att.wait(act, NU - 1))
            norm("norm2", lambda t: x1.wait(act, (t, 1)), lambda: high_part(0))
            for f in range(FT + 1):
                if f < FT:
                    high_part(f + 1)
                    for gv in range(2):
                        bank = banks.filled(act, ("up", f, gv))
                        if f >= 2:
                            hidden.wait(act, f - 2)
                        ch = gv * FT + f
                        tap_mid.tick(s.activation((conv_g, conv_v)[gv][:, f % 2, :], bank[:, :], ACT.Identity,
                                                  scale=convw[:, 44 + ch:45 + ch], bias=convw[:, 132 + ch:133 + ch]),
                                     (f, gv))
                if f >= 1:
                    tapped.wait(act, (f - 1, 1))
                    y = conv_g[:, (f - 1) % 2, :]
                    gelued.tick(s.activation(y, y, ACT.Gelu_apprx_tanh), f - 1)
            hidden_high(0)
            high_part(FT + 1)
            hidden_high(1)
            mod_done.wait(act, "gains")
            norm("context", lambda t: act.wait_ge(ctx_in, 16))
            for i in range(2, ND):
                high_part(FT + i)
                hidden_high(i)
            norm("norm1_2", lambda t: x2.wait(act, (t, 1)))
            for m in range(KT + 1):
                if m < KT:
                    for c in range(2):
                        bank = banks.filled(act, ("xbc", m, c))
                        n, o = (CTX, T) if c else (T, 0)
                        if m >= 2:
                            u_ready.wait(act, m - 2)
                        mid2.tick(s.activation(conv2[:, m % 2, o:o + n], bank[:, 0:n], ACT.Identity,
                                               scale=convw[:, 192 + m:193 + m], bias=convw[:, 216 + m:217 + m]), (m, c))
                if m >= 1:
                    tapped2.wait(act, (m - 1, 1))
                    u_ready.tick(s.activation(u[:, m - 1, :], conv2[:, (m - 1) % 2, :], ACT.Silu), m - 1)
            for t in range(TT):
                bank = banks.filled(act, ("z", t))
                z_ready.tick(s.activation(zs[:, t, :], bank[:, :], ACT.Silu), t)
            for t in range(TT):
                bank = banks.filled(act, ("q2", t))
                q_copied.tick(s.activation(q2[:, t, :], bank[:, :], ACT.Copy, scale=-HD ** -0.5), t)
            dt_abs.wait(act, 0)
            dt_exp.tick(s.activation(sm[:, 1, :], sm[:, 4, :], ACT.Exp, scale=-1.0), 0)
            a_exp.tick(s.activation(a_log[:, :], a_log[:, :], ACT.Exp), 0)
            dt_abs.wait(act, 1)
            dt_log.tick(s.activation(sm[:, 3, :], sm[:, 2, :], ACT.Ln), 0)
            cs_copied.wait(act, 0)
            s.activation(sm[:, 0, :], sm[:, 7, :], ACT.Exp)
            s.activation(sm[:, 1, :], sm[:, 1, :], ACT.Exp)
            cs_exp.tick(s.activation(sm[:, 8, :], sm[:, 2, :], ACT.Exp), 0)
            for t in range(AT):
                bank = banks.filled(act, ("xs", t))
                tok_copied.tick(s.activation(xs_tok[:, t, :], bank[:, :], ACT.Copy), ("xs", t))
            for t in range(0, AT, 2):
                bank = banks.filled(act, ("b", t))
                tok_copied.tick(s.activation(b_tok[:, t:t + 2, :], bank[:, :].rearrange("p (t n) -> p t n", t=2),
                                             ACT.Copy), ("b", t))
            for n in range(2):
                bank = banks.filled(act, ("kT", n))
                w, o = (CTX, T) if n else (T, 0)
                s.activation(kz2[:, 0, o:o + w], bank[:, 0:w], ACT.Copy, scale=low)
                kz_ready.tick(s.activation(kz2[:, 1, o:o + w], bank[:, 0:w], ACT.Copy, scale=high), n)
            for j in range(4):
                bank = banks.filled(act, ("q2T", j))
                q2_ready.tick(s.activation(q2T[:, j, :], bank[:, :], ACT.Copy), j)
            segments = []
            for what, i in weave:
                if what == "win":
                    if i < NW:
                        h, t = divmod(i, TT)
                        lo, hi = near(t)
                        n = (hi - lo + 1) * P + CTX
                        wscore.wait(act, i)
                        row = wprobs[:, i % 2, 0:n]
                        s.activation(row, row, ACT.Exp, scale=-1.0, bias=nmin[:, i:i + 1], accum_out=psums[:, i:i + 1])
                        wprob.tick(s.activation(sink_exp[:, i:i + 1], sinks[:, h:h + 1], ACT.Exp,
                                                bias=nmin[:, i:i + 1]), i)
                    if 1 <= i <= NW:
                        m = i - 1
                        lo, hi = near(m % TT)
                        n = (hi - lo + 1) * P
                        near_b, far_b = (banks.filled(act, ("wprobsT", m, k)) for k in range(2))
                        if m >= 2:
                            banks.filled(act, ("watt", m - 2))
                        s.activation(wprobsT[:, m % 2, 0:n], near_b[:, 0:n], ACT.Copy)
                        wpt_act.tick(s.activation(wprobsT[:, m % 2, n:n + CTX], far_b[:, 0:CTX], ACT.Copy), m)
                    for k in segments:
                        seg_ready.wait(act, (k, 1))
                        decayed.tick(s.activation(decay[:, k % 3, :, :], decay[:, k % 3, :, :], ACT.Exp), k)
                    segments = []
                elif what == "y" and i < len(YS):
                    segments.append(i)

            def mixed2(t):
                y_done.wait(act, t)
                watt.wait(act, NW - 1)

            norm("mix2", mixed2)
            norm("norm2_2", lambda t: x3.wait(act, (t, 1)))
            route_pe.wait(act, "halves")
            route.wait(act, "cleared")
            route_act.tick(s.activation(lgT[0:36, :], ps[0][0:36, :], ACT.Copy), "even")
            route.wait(act, "max")
            for t in range(TT):
                last = s.activation(gexp[:, t, :], gl[:, t, 0:4], ACT.Exp, bias=g8[:, t, 0:1],
                                    accum_out=gsum[:, t:t + 1])
            route_act.tick(last, "group_exp")
            route.wait(act, "top2")
            route_act.tick(s.activation(wts[:, :, 3], wts[:, :, 2], ACT.Exp), "pair_exp")
            s.activation(wts[:, :, 5], wts[:, :, 2], ACT.Silu)

            def expert(n, par, kpar, reuse):
                gate_up, hiddenT, y = ps[2 + par], ps[4 + par], ps[6 + par]
                act.wait_ge(gu_filled, n + 1)
                if reuse is not None:
                    act.wait_ge(ht_filled, reuse)
                s.activation(gu[:, par, :], gate_up[:, :], ACT.Copy).then_inc(gu_ready, 1)
                act.wait_ge(ht_filled, n + 1)
                if reuse is not None:
                    act.wait_ge(hid_ready, reuse)
                s.activation(sg[:, par, :, :], hiddenT[:, :].rearrange("p (f n) -> p f n", f=4)[:, :, 0:BLK],
                             ACT.Silu).then_inc(silu_ready, 1)
                act.wait_ge(y_filled, n + 1)
                if reuse is not None:
                    act.wait_ge(y_stored[par], 16 * kpar)
                s.activation(yE[:, par, :], y[:, :], ACT.Copy).then_inc(y_ready, 1)

            expert(0, 0, 0, None)
            expert(1, 1, 0, None)
            with act.Fori(1, E // 2) as it:
                for par in range(2):
                    expert(2 * it + par, par, it, 2 * it + par - 1)
            later_n = act.value_load(ovf[0:1, NOVF:NOVF + 1], min_val=0, max_val=NOVF)
            with act.If(later_n > 0):
                with act.Fori(0, later_n) as i:
                    expert(i + E, 0, i + E // 2, i + E)
            for t in range(TT):
                final_x.wait(act, t)
                squared.tick(s.activation(junk3, x[:, t, :], ACT.Square, accum_out=sums[:, t:t + 1]), ("final", t, 0))
                squared.wait(act, ("final", t, 0))
                rooted.tick(root(roots[:, t:t + 1], sums[:, t:t + 1], D), ("final", t))

        @block.tensor
        def _(pe):
            def mm(o, lhsT, rhs, start, stop):
                return nc.tensor.matmul(o, lhsT, rhs, start=start, stop=stop)

            def tr(o, i, n=P):
                return nc.tensor.transpose(o, i, ident[0:n, 0:n])

            def norm(name):
                _, tiles, parts, _, _ = NORMS[name]
                opened = [banks.open(pe, ("hT",) + k) for k in halves(name)]
                for i, t in enumerate(tiles):
                    normed.wait(pe, (name, t, parts[-1][0]))
                    for k in halves(name):
                        j = k[1]
                        last = tr(opened[j][:, i * P:(i + 1) * P],
                                  xn[:, t, :].rearrange("p (q j) -> p j q", j=KT)[:, j, :])
                        if t == tiles[-1]:
                            banks.close(last, ("hT",) + k)

            def hT_ready(name):
                hT_act.wait(pe, halves(name)[-1 if name in SPLIT_NORMS else -2])
                hT_dve.wait(pe, halves(name)[-1])

            def project(key, lhs_of, w, a, n, first=0):
                bank = banks.open(pe, key)
                for j in range(KT):
                    last = mm(bank[:, 0:n], lhs_of(j), w[:, j, a:a + n], j == 0, j == KT - 1)
                banks.close(last, key)

            pe.wait_ge(const_in, CONST_ALL)
            norm("norm1")
            hT_ready("norm1")
            for n in range(len(PROJ) + 2):
                if n < len(PROJ):
                    c, t = PROJ[n]
                    w = weights(pe, ("w_in", c))
                    project(("proj", n), lambda j: hT[:, j, t * P:(t + 1) * P], w, 0, w.shape[2])
                if 2 <= n < 18:
                    bank = banks.open(pe, ("qkT", n - 2))
                    qk_ready.wait(pe, n - 2)
                    for j in range(4):
                        last = tr(bank[:, j * P:(j + 1) * P], pj[:, (n - 2) % 3, j * P:(j + 1) * P])
                    banks.close(last, ("qkT", n - 2))
            pe.wait_ge(more_in, MORE_ALL)
            bank = banks.open(pe, "conv_weights")
            tr(bank[:, 0:88], conv_rows[0:88, 0, :], 88)
            tr(bank[:, 88:176], conv_rows[0:88, 1, :], 88)
            banks.close(tr(bank[:, 176:224], conv_rows[0:48, 2, :], 48), "conv_weights")
            qk_drained.wait(pe, 15)
            v_tail.wait(pe, TT - 1)
            mod_silu.wait(pe, "c")
            for i in range(NU + 2):
                if i < NU:
                    m, h, t = i // (H * TT), i // TT % H, i % TT
                    bank = banks.open(pe, ("score", i))
                    at = slice(t * P, t * P + P)
                    q, k = (qbT[:, h // 2, at], kzB[:, h, :]) if m else (qaT[:, h % 4, at], kzA[:, h // 4, :])
                    banks.close(mm(bank[:, :], q, k, True, True), ("score", i))
                if 1 <= i <= NU:
                    bank = banks.open(pe, ("probsT", i - 1))
                    prob.wait(pe, i - 1)
                    for k in range(TT):
                        last = tr(bank[:, k * P:(k + 1) * P], probs[:, (i - 1) % 2, k * P:(k + 1) * P])
                    banks.close(last, ("probsT", i - 1))
                if i >= 2:
                    n = i - 2
                    m, h = n // (H * TT), n // TT % H
                    bank = banks.open(pe, ("att", n))
                    pt_step(n).wait(pe, n)
                    for k in range(TT):
                        v = vB[:, k, h * HD:(h + 1) * HD] if m else vA[:, k, (h // 4) * HD:(h // 4 + 1) * HD]
                        last = mm(bank[:, 0:HD], probsT[:, n % 2, k * P:(k + 1) * P], v, k == 0, k == TT - 1)
                    banks.close(last, ("att", n))
                if i % 5 == 2 and i // 5 < 12:
                    m = i // 5
                    w = weights(pe, ("w_ada", m))
                    bank = banks.open(pe, ("modrow", m))
                    for j in range(KT):
                        quarter = bank[32 * (j % 4):32 * (j % 4) + 32, :]
                        last = mm(quarter, csilu[:, j, :], w[:, j, :], j < 4, j >= 4)
                    banks.close(last, ("modrow", m))
                if i % 5 == 4 and i // 5 < 12:
                    m = i // 5
                    mod_copied.wait(pe, m)
                    bank = banks.open(pe, ("mod", m))
                    if m // 2 in (2, 5):
                        last = mm(bank[:, :], C("sum_two")[:, 0:1].broadcast_to([P, P]), modrow[:, m % 2, :], True, True)
                    else:
                        for j in range(KT):
                            last = mm(bank[64 * (m % 2):64 * (m % 2) + 64, 2 * j:2 * j + 2],
                                      modrow[:, m % 2, :].rearrange("p (q j) -> p j q", j=KT)[:, j, :], C("sum_two"),
                                      True, True)
                    banks.close(last, ("mod", m))

            def out_projection(key, name):
                for n in range(2):
                    w = weights(pe, (name, n))
                    for t in range(TT):
                        yield t, n, w

            norm("mix1")
            hT_ready("mix1")
            for t, n in SIDES:
                w = weights(pe, ("w_out", n))
                project(("out1", t, n), lambda j: hT[:, j, t * P:(t + 1) * P], w, 0, 512)
            norm("norm2")
            hT_ready("norm2")
            def pairs(a_high, a_low, b_high, b_low):
                return (a_high, b_high), (a_high, b_low), (a_low, b_high)

            for f in range(FT):
                low_ready.wait(pe, f)
                wh, wl = (halfway(("w_up", f), part[:, f % 2, :]) for part in (w_high, w_low))
                for gv in range(2):
                    bank = banks.open(pe, ("up", f, gv))
                    cs = slice(gv * P, gv * P + P)
                    for j in range(KT):
                        for n, (a, b) in enumerate(pairs(wh[:, j, cs], wl[:, j, cs], hT_high[:, j, :], hT_low[:, j, :])):
                            last = mm(bank[:, :], a, b, j == n == 0, j == KT - 1 and n == 2)
                    banks.close(last, ("up", f, gv))
            norm("context")
            down_banks = [banks.open(pe, ("down",) + k) for k in SIDES]
            for i in range(ND):
                low_ready.wait(pe, FT + i)
                hid_low_ready.wait(pe, i)
                wh, wl = (halfway(("w_down", i), part[:, (FT + i) % 2, :]) for part in (w_high, w_low))
                for k, (t, n) in enumerate(SIDES):
                    ts, cs = slice(t * P, t * P + P), slice(n * 512, n * 512 + 512)
                    for f in range(2):
                        for m, (a, b) in enumerate(pairs(hid_high[:, i % 2, f, ts], hid_low[:, i % 2, f, ts], wh[:, f, cs],
                                                         wl[:, f, cs])):
                            last = mm(down_banks[k][:, :], a, b, i == f == m == 0, i == ND - 1 and f == 1 and m == 2)
                    if i == ND - 1:
                        banks.close(last, ("down", t, n))
                if i < ND - 1:
                    down_read.tick(last, i)
            norm("norm1_2")
            hT_ready("norm1_2")

            def tokens(t):
                return (lambda j: hT[:, j, t * P:(t + 1) * P]) if t < TT else (
                    lambda j: hTc[:, j, (t - TT) * P:(t - TT + 1) * P])

            w = weights(pe, "w_kvd")
            for t in range(AT):
                project(("kvd", t), tokens(t), w, 0, 272)
            for m, c in XBC:
                w = weights(pe, ("w_xbc", m // 4))
                bank = banks.open(pe, ("xbc", m, c))
                src, n = (hTc, CTX) if c else (hT, T)
                for j in range(KT):
                    last = mm(bank[:, 0:n], w[:, j, (m % 4) * P:(m % 4 + 1) * P], src[:, j, :], j == 0, j == KT - 1)
                banks.close(last, ("xbc", m, c))
            w = weights(pe, "w_z")
            for t in range(TT):
                project(("z", t), tokens(t), w, 0, 512)
            w = weights(pe, "w_q")
            for t in range(TT):
                project(("q2", t), tokens(t), w, 0, 512)
            dta_ready.wait(pe, 0)
            bank = banks.open(pe, "cumsum")
            dta = sm[:, 6, :].rearrange("p (t d h) -> p t d h", t=AT, d=2)
            b4 = bank[:, 0:96].rearrange("p (t d h) -> p t d h", t=AT, d=2)
            mm(b4[:, :, 0, :], C("upto"), dta[:, :, 0, :], True, True)
            mm(b4[:, :, 1, :], C("from"), dta[:, :, 1, :], True, True)
            banks.close(mm(bank[:, 96:192], C("one").broadcast_to([P, P]), sm[:, 6, :], True, True), "cumsum")
            u_ready.wait(pe, KT - 1)
            for t in range(AT):
                bank = banks.open(pe, ("xs", t))
                for m in range(4):
                    last = tr(bank[:, m * P:(m + 1) * P], u[:, m, t * P:(t + 1) * P])
                banks.close(last, ("xs", t))
            for t in range(0, AT, 2):
                bank = banks.open(pe, ("b", t))
                for i in range(2):
                    for m in range(2):
                        o = i * 256 + m * P
                        last = tr(bank[:, o:o + P], u[:, 4 + m, (t + i) * P:(t + i + 1) * P])
                banks.close(last, ("b", t))
            for n in range(2):
                bank = banks.open(pe, ("kT", n))
                if n == 0:
                    roped.wait(pe, ("k", TT - 1))
                else:
                    kvd_copied.wait(pe, AT - 1)
                for i in range(CT if n else TT):
                    last = tr(bank[:, i * P:(i + 1) * P], kvd[:, n * TT + i, 16:144])
                banks.close(last, ("kT", n))
            for j in range(4):
                bank = banks.open(pe, ("q2T", j))
                roped.wait(pe, ("q", TT - 1))
                for t in range(TT):
                    last = tr(bank[:, t * P:(t + 1) * P], q2[:, t, j * P:(j + 1) * P])
                banks.close(last, ("q2T", j))
            tok_copied.wait(pe, ("b", AT - 2))
            kz_ready.wait(pe, 1)
            q2_ready.wait(pe, 3)
            for what, i in weave:
                if what == "win":
                    if i < NW:
                        h, t = divmod(i, TT)
                        lo, hi = near(t)
                        q = q2T[:, h % 4, t * P:(t + 1) * P]
                        k = kz2[:, h // 4, :]
                        bank = banks.open(pe, ("wscore", i, 0))
                        banks.close(mm(bank[:, 0:(hi - lo + 1) * P], q, k[:, lo * P:(hi + 1) * P], True, True),
                                    ("wscore", i, 0))
                        bank = banks.open(pe, ("wscore", i, 1))
                        banks.close(mm(bank[:, 0:CTX], q, k[:, T:T + CTX], True, True), ("wscore", i, 1))
                    if 1 <= i <= NW:
                        m = i - 1
                        lo, hi = near(m % TT)
                        n = hi - lo + 1
                        wprob.wait(pe, m)
                        for part, (a, many) in enumerate(((0, n), (n, CT))):
                            bank = banks.open(pe, ("wprobsT", m, part))
                            for k in range(many):
                                last = tr(bank[:, k * P:(k + 1) * P], wprobs[:, m % 2, (a + k) * P:(a + k + 1) * P])
                            banks.close(last, ("wprobsT", m, part))
                    if i >= 2:
                        m = i - 2
                        h, t = divmod(m, TT)
                        lo, hi = near(t)
                        seen = list(range(lo, hi + 1)) + list(range(TT, AT))
                        bank = banks.open(pe, ("watt", m))
                        wpt_act.wait(pe, m)
                        for n, kt in enumerate(seen):
                            v = kvd[:, kt, 144 + (h // 4) * HD:144 + (h // 4 + 1) * HD]
                            last = mm(bank[:, 0:HD], wprobsT[:, m % 2, n * P:(n + 1) * P], v, n == 0,
                                      n == len(seen) - 1)
                        banks.close(last, ("watt", m))
                elif what == "state":
                    d, pos = STATES[i]
                    t = TILE_AT[d][pos]
                    bank = banks.open(pe, ("state", i))
                    dtxw_ready.wait(pe, i)
                    for g in range(2):
                        last = mm(bank[:, g * 256:(g + 1) * 256], b_tok[:, t, g * P:(g + 1) * P],
                                  dtxw[:, i % 2, g * 256:(g + 1) * 256], True, True)
                    banks.close(last, ("state", i))
                else:
                    if i < len(YS):
                        t, d = YS[i]
                        if d == 0:
                            bank = banks.open(pe, ("cb", t))
                            for g in range(2):
                                last = mm(bank[:, g * P:(g + 1) * P], u[:, 4 + g, t * P:(t + 1) * P],
                                          u[:, 6 + g, t * P:(t + 1) * P], True, True)
                            banks.close(last, ("cb", t))
                        for g in range(2):
                            bank = banks.open(pe, ("seg", i, g))
                            for h in range(4):
                                a = t * 16 + d * 8 + g * 4 + h
                                last = mm(bank[:, h * P:(h + 1) * P], sm[:, 6, a:a + 1].broadcast_to([P, P]),
                                          C("from" if d else "upto"), True, True)
                            banks.close(last, ("seg", i, g))
                    if i >= 2:
                        k = i - 2
                        t, d = YS[k]
                        pos = TILE_AT[d].index(t) - 1
                        bank = banks.open(pe, ("yoff", k))
                        state_ready.wait(pe, STATES.index((d, pos)))
                        for g in range(2):
                            last = mm(bank[:, g * 256:(g + 1) * 256], u[:, 6 + g, t * P:(t + 1) * P],
                                      state[:, d, pos - 1, g * 256:(g + 1) * 256], True, True)
                        banks.close(last, ("yoff", k))
                        bank = banks.open(pe, ("ydiag", k))
                        m_ready.wait(pe, k)
                        dtx_ready.wait(pe, k)
                        for h in range(H):
                            last = mm(bank[:, h * HD:(h + 1) * HD], decay[:, k % 3, h, :],
                                      dtx[:, k % 2, h * HD:(h + 1) * HD], True, True)
                        banks.close(last, ("ydiag", k))
            norm("mix2")
            hT_ready("mix2")
            for t, n in SIDES:
                w = weights(pe, ("w_out2", n))
                project(("out2", t, n), lambda j: hT[:, j, t * P:(t + 1) * P], w, 0, 512)
            norm("norm2_2")
            hT_ready("norm2_2")
            for n, (steps_, step) in enumerate(g_[1] for g_ in banks.order[-8:]):
                steps_.wait(pe, step)
            for j in range(KT):
                row = 64 * (j % 2)
                last = mm(ps[0][row:row + 36, :], route_w[:, j, :], hT[:, j, :], j < 2, j >= KT - 2)
            route_pe.tick(last, "halves")
            route_act.wait(pe, "even")
            route.wait(pe, "odd")
            for t in range(TT):
                last = mm(ps[1][:, t * 36:(t + 1) * 36], lgT[:, t * P:(t + 1) * P], C("both_halves"), True, True)
            route_pe.tick(last, "logits")
            route.wait(pe, "hot")
            hot = osum.rearrange("p t e -> p (t e)")
            mm(ps[2][:, 0:TT * E], C("before"), hot, True, True)
            route_pe.tick(mm(ps[2][:, TT * E:2 * TT * E], C("one").broadcast_to([P, P]), hot, True, True), "rank")
            route.wait(pe, "places")
            for n in range(8):
                last = mm(ps[3][:, 0:2 * NBLK], hot_p[:, n, :], hot_b[:, n, :, :].rearrange("p a b -> p (a b)"), n == 0,
                          n == 7)
            route_pe.tick(last, "table")
            route.wait(pe, "table")

            def expert(n, par, kpar, reuse):
                xt, gate_up, hiddenT, y = ps[par], ps[2 + par], ps[4 + par], ps[6 + par]
                gate_w, up_w, down_w = (EXPERT_SLOTS[3 * par + i] for i in range(3))
                loads, free = held(pe, 16 * kpar + 16), held(pe, reuse) if reuse is not None else None
                pe.wait_ge(const_in, CONST_ALL)
                pe.wait_ge(tokens_in[par], loads)
                if reuse is not None:
                    pe.wait_ge(xt_ready, free)
                for j in range(KT):
                    last = tr(xt[:, j * BLK:(j + 1) * BLK],
                              xg[0:BLK, par, :].rearrange("p (q j) -> p j q", j=KT)[:, j, :], BLK)
                last.then_inc(xt_filled, 1)
                pe.wait_ge(xt_ready, n + 1)
                pe.wait_ge(expert_in[3 * par], 16 * kpar + 16)
                pe.wait_ge(expert_in[3 * par + 1], 16 * kpar + 16)
                if reuse is not None:
                    pe.wait_ge(gu_ready, reuse)
                for j in range(KT):
                    for half, w in enumerate((gate_w, up_w)):
                        last = mm(gate_up[half * BLK:(half + 1) * BLK, :], xT[:, par, j, :], w[:, j * EF:(j + 1) * EF],
                                  j == 0, j == KT - 1)
                last.then_inc(gu_filled, 1)
                pe.wait_ge(gu_ready, n + 1)
                if reuse is not None:
                    pe.wait_ge(hid_ready, reuse)
                for f in range(4):
                    last = tr(hiddenT[:, f * P:(f + 1) * P], gu[:, par, :].rearrange("p (q f) -> p f q", f=4)[:, f, :])
                last.then_inc(ht_filled, 1)
                pe.wait_ge(hid_ready, n + 1)
                pe.wait_ge(expert_in[3 * par + 2], 16 * kpar + 16)
                if reuse is not None:
                    pe.wait_ge(y_ready, reuse)
                for f in range(4):
                    for half in range(2):
                        last = mm(y[half * BLK:(half + 1) * BLK, :], hidE[:, par, f, :],
                                  down_w[:, f * D + half * 512:f * D + half * 512 + 512], f == 0, f == 3)
                last.then_inc(y_filled, 1)

            expert(0, 0, 0, None)
            expert(1, 1, 0, None)
            with pe.Fori(1, E // 2) as it:
                for par in range(2):
                    expert(2 * it + par, par, it, 2 * it + par - 1)
            later_n = pe.value_load(ovf[0:1, NOVF:NOVF + 1], min_val=0, max_val=NOVF)
            with pe.If(later_n > 0):
                with pe.Fori(0, later_n) as i:
                    expert(i + E, 0, i + E // 2, i + E)

        @block.vector
        def _(dve):
            v = nc.vector

            def link(ins):
                dve_chain.link(dve, ins)

            def low_part(k):
                high_ready.wait(dve, k)
                a = PLACES[UNIT_AT[SPLITS[k]][0]][0]
                low_ready.tick(v.tensor_tensor(w_low[:, k % 2, :], ring_flat[:, a:a + HALF], w_high[:, k % 2, :],
                                               ALU.subtract), k)

            def hidden_low(i):
                hid_high_ready.wait(dve, i)
                hid_low_ready.tick(v.tensor_tensor(hid_low[:, i % 2, :, :], hid[:, 2 * i:2 * i + 2, :],
                                                   hid_high[:, i % 2, :, :], ALU.subtract), i)

            def norm(name, between=None):
                src, tiles, parts, _, gain = NORMS[name]
                n = len(parts)
                for t in tiles:
                    rooted.wait(dve, (name, t))
                    link(v.reciprocal(rstd[:, t * n:t * n + n], roots[:, t * n:t * n + n]))
                    for i, (a, b) in enumerate(parts):
                        normed.tick(v.tensor_scalar(xn[:, t, a:b], src(t)[:, a:b], rstd[:, t * n + i:t * n + i + 1], None,
                                                    ALU.mult), (name, t, a))
                if between is not None:
                    between()
                for k in halves(name):
                    if name in SPLIT_NORMS:
                        j = k[1]
                        bank = banks.filled(dve, ("hT",) + k)
                        hT_act.wait(dve, k)
                        hT_dve.tick(v.scalar_tensor_tensor(hT_low[:, j, :], bank[:, :], gain(j)[0], hT_high[:, j, :],
                                                           ALU.mult, ALU.subtract), k)
                    elif k[1] % 2 == 1:
                        j = k[1]
                        bank = banks.filled(dve, ("hT",) + k)
                        dst = hTc[:, j, :] if name == "context" else hT[:, j, :]
                        sc, sh = gain(j)
                        hT_dve.tick(v.tensor_scalar(dst, bank[:, 0:dst.shape[1]], sc, sh, ALU.mult, ALU.add), k)

            csilu_cleared.tick(v.memset(csilu[:, :, :], 0.0), 0)
            dve.wait_ge(const_in, CONST_ALL)
            v.memset(gains[64:128, 4, :], 1.0)
            norm("norm1")
            dve.wait_ge(more_in, MORE_ALL)
            for n in (0, 2):
                link(v.tensor_scalar(head_gain[:, n, :], head_gain[:, n, :], -HD ** -0.5, None, ALU.mult))
            for n in range(20):
                if n >= 16:
                    bank = banks.filled(dve, ("proj", n))
                    v_tail.tick(v.tensor_copy(vB[:, n - 16, 256:512], bank[:, 0:256]), n - 16)
                    continue
                c, t = PROJ[n]
                pj_ready.wait(dve, n)
                if n >= 2:
                    head_rooted.wait(dve, n - 2)
                head_summed.tick(v.tensor_reduce(head_sum[:, n % 2, :], sq[:, n % 2, :].rearrange(
                    "p (h d) -> p h d", d=HD), AXX, ALU.add), n)
                head_rooted.wait(dve, n)
                link(v.reciprocal(head_sum[:, n % 2, :], head_root[:, n % 2, :]))
                row = pj[:, n % 3, :].rearrange("p (h d) -> p h d", d=HD)
                for a, many, gain in HEADS_OF[c]:
                    seg = row[:, a:a + many, :]
                    last = v.tensor_tensor(seg, seg, wide(head_sum[:, n % 2, a:a + many], HD), ALU.mult)
                link(last)
                for a, many, gain in HEADS_OF[c]:
                    seg = row[:, a:a + many, :]
                    last = v.tensor_tensor(seg, seg, head_gain[:, gain, :].unsqueeze(1).broadcast_to([P, many, HD]),
                                           ALU.mult)
                if c >= 2:
                    qk_ready.tick(last, n)
                    continue
                link(last)
                heads = 8 if c == 0 else 2
                cos, sin = rope1[:, 0, t, :], rope1[:, 1, t, :]
                a3, b3 = (rope_t[:, i, 0:heads * HD] for i in range(2))
                src = row[:, 0:heads, :]
                v.tensor_tensor(a3.rearrange("p (h d) -> p h d", d=HD), src,
                                cos.unsqueeze(1).broadcast_to([P, heads, HD]), ALU.mult)
                split = "p h (a b d) -> p h a b d"
                s5 = src.rearrange(split, a=2, b=2)
                b5 = b3.rearrange("p (h a b d) -> p h a b d", h=heads, a=2, b=2)
                sin4 = sin.rearrange("p (a b d) -> p a b d", a=2, b=2)
                for half in range(2):
                    last = v.tensor_tensor(b5[:, :, :, half, :], s5[:, :, :, 1 - half, :],
                                           sin4[:, :, half, :].unsqueeze(1).broadcast_to([P, heads, 2, 16]), ALU.mult)
                link(last)
                if c == 0:
                    dst = pj[:, n % 3, :].rearrange("p (j half d) -> p half j d", j=4, half=2)
                    order = "p (half j d) -> p half j d"
                    ins = v.tensor_tensor(dst, a3.rearrange(order, j=4, half=2), b3.rearrange(order, j=4, half=2),
                                          ALU.add)
                else:
                    ins = v.tensor_tensor(pj[:, n % 3, 0:128], a3, b3, ALU.add)
                qk_ready.tick(ins, n)
            bank = banks.filled(dve, "conv_weights")
            conv_ready.tick(v.tensor_copy(convw[:, :], bank[:, 0:224]), "taps")
            for i in range(NU + 2):
                if i < NU:
                    bank = banks.filled(dve, ("score", i))
                    if i < NU // 2:
                        score_min.tick(v.tensor_reduce(nmin[:, i:i + 1], bank[:, :], AXX, ALU.min), i)
                    else:
                        h, t = i // TT % H, i % TT
                        dve.wait_ge(dist_in[h % 2], 16 * (h // 2 + 1))
                        banks.filled(dve, ("probsT", i - 2))
                        a = (TT - 1 - t) * P
                        score_min.tick(v.tensor_tensor_reduce(probs[:, i % 2, :], bank[:, :], dist[:, h % 2, a:a + T],
                                                              1.0, 3e38, ALU.add, ALU.min, nmin[:, i:i + 1]), i)
                if 1 <= i <= NU and (i - 1) % 2 == 1:
                    bank = banks.filled(dve, ("probsT", i - 1))
                    if i >= 3:
                        banks.filled(dve, ("att", i - 3))
                    pt_dve.tick(v.tensor_copy(probsT[:, (i - 1) % 2, :], bank[:, :]), i - 1)
                if i >= 2:
                    n = i - 2
                    m, h, t = n // (H * TT), n // TT % H, n % TT
                    bank = banks.filled(dve, ("att", n))
                    link(v.reciprocal(rsums[:, n:n + 1], psums[:, n:n + 1]))
                    att.tick(v.tensor_scalar(xn[:, t, m * 512 + h * HD:m * 512 + (h + 1) * HD], bank[:, 0:HD],
                                             rsums[:, n:n + 1], None, ALU.mult), n)
                if i % 5 == 4 and i // 5 < 12:
                    m = i // 5
                    bank = banks.filled(dve, ("mod", m))
                    if m // 2 in (2, 5):
                        row = gates[:, m // 6, (m % 2) * 512:(m % 2) * 512 + 512]
                        ins = v.tensor_tensor(row, bank[:, :], row, ALU.add)
                    else:
                        q = slice(64 * (m % 2), 64 * (m % 2) + 64)
                        ins = v.tensor_tensor(mod[q, m // 2, :, :], bank[q, 0:16].rearrange("p (j c) -> p j c", c=2),
                                              wide(ada_bias[q, m // 2, :], 2), ALU.add)
                    mod_done.tick(ins, m)
            mod_done.wait(dve, 11)
            v.scalar_tensor_tensor(mod_gain[:, 0, :], mod[:, 1, :, 0], 1.0, gains[:, 3, :], ALU.add, ALU.mult)
            v.scalar_tensor_tensor(mod_gain[:, 1, :], mod[:, 1, :, 1], 1.0, gains[:, 3, :], ALU.add, ALU.mult)
            mod_done.tick(v.scalar_tensor_tensor(mod_gain[:, 2, :], mod[:, 4, :, 0], 1.0, gains[:, 5, :], ALU.add,
                                                 ALU.mult), "gains")
            norm("mix1")
            for t, n in SIDES:
                bank = banks.filled(dve, ("out1", t, n))
                side = x[:, t, n * 512:(n + 1) * 512]
                x1.tick(v.tensor_tensor(side, bank[:, :], side, ALU.add), (t, n))
            norm("norm2", lambda: low_part(0))
            for f in range(FT + 1):
                if f < FT:
                    low_part(f + 1)
                    for gv in range(2):
                        bank = banks.filled(dve, ("up", f, gv))
                        tap_mid.wait(dve, (f, gv))
                        y = (conv_g, conv_v)[gv][:, f % 2, :]
                        ch = gv * FT + f
                        link(v.scalar_tensor_tensor(y[:, 1:T], bank[:, 0:T - 1], convw[:, ch:ch + 1], y[:, 1:T],
                                                    ALU.mult, ALU.add))
                        tapped.tick(v.scalar_tensor_tensor(y[:, 0:T - 1], bank[:, 1:T], convw[:, 88 + ch:89 + ch],
                                                           y[:, 0:T - 1], ALU.mult, ALU.add), (f, gv))
                if f >= 1:
                    gelued.wait(dve, f - 1)
                    hidden.tick(v.tensor_tensor(hid[:, f - 1, :], conv_g[:, (f - 1) % 2, :], conv_v[:, (f - 1) % 2, :],
                                                ALU.mult), f - 1)
            hidden_low(0)
            low_part(FT + 1)
            hidden_low(1)
            norm("context")
            for i in range(2, ND):
                low_part(FT + i)
                hidden_low(i)
            for t, n in SIDES:
                bank = banks.filled(dve, ("down", t, n))
                side = x[:, t, n * 512:(n + 1) * 512]
                x2.tick(v.tensor_tensor(side, bank[:, :], side, ALU.add), (t, n))
            norm("norm1_2")
            for t in range(AT):
                bank = banks.filled(dve, ("kvd", t))
                kvd_copied.tick(v.tensor_copy(kvd[:, t, :], bank[:, 0:272]), t)
            kvd_copied.wait(dve, AT - 1)
            raw = sm[:, 0, :].rearrange("p (t k) -> p t k", t=AT)
            link(v.tensor_tensor(raw, kvd[:, :, 0:16], dt_bias[:, :].unsqueeze(1).broadcast_to([P, AT, 16]), ALU.add))
            dt_abs.tick(v.scalar_tensor_tensor(sm[:, 4, :], sm[:, 0, :], -1.0, sm[:, 0, :], ALU.mult, ALU.max), 0)
            for m, c in XBC:
                bank = banks.filled(dve, ("xbc", m, c))
                mid2.wait(dve, (m, c))
                n, o = (CTX, T) if c else (T, 0)
                y = conv2[:, m % 2, o:o + n]
                for k, off in ((0, -2), (1, -1), (3, 1), (4, 2)):
                    a, b = max(0, -off), min(n, n - off)
                    w = convw[:, 176 + 8 * k + m:177 + 8 * k + m]
                    ins = v.scalar_tensor_tensor(y[:, a:b], bank[:, a + off:b + off], w, y[:, a:b], ALU.mult, ALU.add)
                    if k < 4:
                        link(ins)
                tapped2.tick(ins, (m, c))
            dt_exp.wait(dve, 0)
            dt_abs.tick(v.tensor_scalar(sm[:, 2, :], sm[:, 1, :], 1.0, None, ALU.add), 1)
            dt_abs.wait(dve, 1)
            link(v.tensor_scalar(sm[:, 4, :], sm[:, 2, :], -1.0, None, ALU.add))
            link(v.tensor_scalar(sm[:, 5, :], sm[:, 4, :], 0.0, None, ALU.is_equal))
            link(v.tensor_tensor(sm[:, 4, :], sm[:, 4, :], sm[:, 5, :], ALU.add))
            link(v.reciprocal(sm[:, 4, :], sm[:, 4, :]))
            link(v.tensor_tensor(sm[:, 4, :], sm[:, 4, :], sm[:, 1, :], ALU.mult))
            dt_log.wait(dve, 0)
            link(v.tensor_tensor(sm[:, 4, :], sm[:, 4, :], sm[:, 3, :], ALU.mult))
            link(v.tensor_tensor(sm[:, 5, :], sm[:, 5, :], sm[:, 1, :], ALU.mult))
            link(v.tensor_tensor(sm[:, 4, :], sm[:, 4, :], sm[:, 5, :], ALU.add))
            link(v.scalar_tensor_tensor(sm[:, 5, :], sm[:, 0, :], 0.0, sm[:, 4, :], ALU.max, ALU.add))
            a_exp.wait(dve, 0)
            dta_ready.tick(v.scalar_tensor_tensor(
                sm[:, 6, :].rearrange("p (t k) -> p t k", t=AT), sm[:, 5, :].rearrange("p (t k) -> p t k", t=AT), -1.0,
                a_log[:, :].unsqueeze(1).broadcast_to([P, AT, 16]), ALU.mult, ALU.mult), 0)
            bank = banks.filled(dve, "cumsum")
            v.tensor_copy(sm[:, 7, :], bank[:, 0:96])
            link(v.tensor_copy(sm[:, 2, :], bank[:, 96:192]))
            cs_copied.tick(v.tensor_tensor(sm[:, 1, :], sm[:, 2, :], sm[:, 7, :], ALU.subtract), 0)
            cs_exp.wait(dve, 0)
            sw_ready.tick(v.tensor_tensor(sm[:, 9, :], sm[:, 1, :], sm[:, 5, :], ALU.mult), 0)
            link(v.tensor_scalar(win_min[:, 64:72], sinks[:, :], -1.0, None, ALU.mult))

            def y_rows(k):
                t, d = YS[k]
                row = cat[:, t, 0:512]
                off = banks.filled(dve, ("yoff", k))
                ea = wide(sm[:, 0, t * 16 + d * 8:t * 16 + d * 8 + 8], HD)
                ins = v.tensor_tensor(ytmp.rearrange("p (h d) -> p h d", d=HD),
                                      off[:, :].rearrange("p (h d) -> p h d", d=HD), ea, ALU.mult)
                y_read.tick(ins, (k, "off"))
                y_read.wait(dve, (k, "off"))
                diag = banks.filled(dve, ("ydiag", k))
                if d == 0:
                    y_read.tick(v.tensor_tensor(row, diag[:, :], ytmp, ALU.add), (k, "diag"))
                    y_read.wait(dve, (k, "diag"))
                    return
                link(v.tensor_tensor(row, row, ytmp, ALU.add))
                y_read.tick(v.tensor_tensor(row, diag[:, :], row, ALU.add), (k, "diag"))
                y_read.wait(dve, (k, "diag"))

            for what, i in weave:
                if what == "win":
                    if i < NW:
                        h, t = divmod(i, TT)
                        lo, hi = near(t)
                        n = (hi - lo + 1) * P
                        if i >= 2:
                            banks.filled(dve, ("wprobsT", i - 2, 1))
                        mask = C("window")
                        a = (lo - t + 1) * P
                        near_b, far_b = (banks.filled(dve, ("wscore", i, k)) for k in range(2))
                        v.tensor_tensor_reduce(wprobs[:, i % 2, 0:n], near_b[:, 0:n], mask[:, a:a + n], 1.0, 3e38,
                                               ALU.add, ALU.min, win_min[:, 2 * i:2 * i + 1])
                        link(v.tensor_tensor_reduce(wprobs[:, i % 2, n:n + CTX], far_b[:, 0:CTX],
                                                    mask[:, 3 * P:3 * P + CTX], 1.0, 3e38, ALU.add, ALU.min,
                                                    win_min[:, 2 * i + 1:2 * i + 2]))
                        wscore.tick(v.tensor_scalar(nmin[:, i:i + 1], win_min[:, 2 * i:2 * i + 1], win_min[:, 2 * i + 1:2 * i + 2],
                                                    win_min[:, 64 + h:65 + h], ALU.min, ALU.min), i)
                    if i >= 2:
                        m = i - 2
                        h, t = divmod(m, TT)
                        bank = banks.filled(dve, ("watt", m))
                        link(v.tensor_tensor(rsums[:, m:m + 1], psums[:, m:m + 1], sink_exp[:, m:m + 1], ALU.add))
                        link(v.reciprocal(rsums[:, m:m + 1], rsums[:, m:m + 1]))
                        watt.tick(v.tensor_scalar(cat[:, t, 512 + h * HD:512 + (h + 1) * HD], bank[:, 0:HD],
                                                  rsums[:, m:m + 1], None, ALU.mult), m)
                elif what == "state":
                    d, pos = STATES[i]
                    t = TILE_AT[d][pos]
                    bank = banks.filled(dve, ("state", i))
                    if pos == 0:
                        ins = v.tensor_copy(state0[:, d, :], bank[:, :])
                    else:
                        old = state0[:, d, :] if pos == 1 else state[:, d, pos - 2, :]
                        state_ready.wait(dve, STATES.index((d, pos - 1)))
                        link(v.tensor_tensor(stmp.rearrange("p (h d) -> p h d", d=HD),
                                             old.rearrange("p (h d) -> p h d", d=HD),
                                             wide(sm[:, 8, t * 16 + d * 8:t * 16 + d * 8 + 8], HD), ALU.mult))
                        ins = v.tensor_tensor(state[:, d, pos - 1, :], bank[:, :], stmp, ALU.add)
                    state_ready.tick(ins, i)
                else:
                    if 1 <= i <= len(YS):
                        k = i - 1
                        if k % 2 == 0:
                            cb_masked.wait(dve, k // 2)
                        decayed.wait(dve, k)
                        for g in range(2):
                            rows = decay[:, k % 3, 4 * g:4 * g + 4, :]
                            ins = v.tensor_tensor(rows, rows, cbm[:, YS[k][1], g, :].unsqueeze(1).broadcast_to([P, 4, P]),
                                                  ALU.mult)
                        m_ready.tick(ins, k)
                    if i < len(YS):
                        t, d = YS[i]
                        if d == 0:
                            if i:
                                m_ready.wait(dve, i - 1)
                            bank = banks.filled(dve, ("cb", t))
                            b3 = bank[:, 0:256].rearrange("p (g n) -> p g n", g=2)
                            v.tensor_tensor(cbm[:, 0, :, :], b3, C("upto").unsqueeze(1).broadcast_to([P, 2, P]),
                                            ALU.mult)
                            cb_masked.tick(v.tensor_tensor(
                                cbm[:, 1, :, :], b3, C("from").unsqueeze(1).broadcast_to([P, 2, P]), ALU.mult), t)
                        if i >= 3:
                            banks.filled(dve, ("ydiag", i - 3))
                        for g in range(2):
                            bank = banks.filled(dve, ("seg", i, g))
                            for h in range(4):
                                a = t * 16 + d * 8 + g * 4 + h
                                ins = v.tensor_scalar(decay[:, i % 3, g * 4 + h, :], bank[:, h * P:(h + 1) * P],
                                                      sm[:, 7, a:a + 1], 0.0, ALU.subtract, ALU.min)
                            seg_ready.tick(ins, (i, g))
                    if i >= 2:
                        y_rows(i - 2)
            norm("mix2")
            for t, n in SIDES:
                bank = banks.filled(dve, ("out2", t, n))
                side = x[:, t, n * 512:(n + 1) * 512]
                gated = (ytmp, stmp)[n]
                link(v.tensor_tensor(gated, bank[:, :], gates[:, 0, n * 512:(n + 1) * 512], ALU.mult))
                x3.tick(v.tensor_tensor(side, side, gated, ALU.add), (t, n))
            v.memset(gl[:, :, :], -3e38)
            route.tick(v.memset(lgT, 0.0), "cleared")
            norm("norm2_2")
            route_pe.wait(dve, "halves")
            route.wait(dve, "cleared")
            route.tick(v.tensor_copy(lgT[64:100, :], ps[0][64:100, :]), "odd")
            route_pe.wait(dve, "logits")
            link(v.tensor_tensor(lg[:, :, :], ps[1][:, 0:TT * 36].rearrange("p (t n) -> p t n", t=TT),
                                 route_bias[:, :].unsqueeze(1).broadcast_to([P, TT, 36]), ALU.add))
            link(v.tensor_copy(gl[:, :, 0:4], lg[:, :, 0:4]))
            for t in range(TT):
                ins = v.max(g8[:, t, :], gl[:, t, :])
            link(ins)
            for t in range(TT):
                ins = v.max_index(gi[:, t, :], g8[:, t, :], gl[:, t, :])
            route.tick(ins, "logits")
            route.wait(dve, "logits")
            link(v.tensor_copy(gif[:, :], gi[:, :, 0]))
            route.tick(v.tensor_scalar(g8[:, :, 0:1], g8[:, :, 0:1], -1.0, None, ALU.mult), "max")
            for t in range(TT):
                ins = v.tensor_scalar(el[:, t, :], C("group"), gif[:, t:t + 1], BIG, ALU.is_equal, ALU.mult)
            link(ins)
            link(v.scalar_tensor_tensor(el[:, :, :], el[:, :, :], -BIG, lg[:, :, 4:36], ALU.add, ALU.add))
            for t in range(TT):
                ins = v.max(e8[:, t, :], el[:, t, :])
            link(ins)
            for t in range(TT):
                ins = v.max_index(ei[:, t, :], e8[:, t, :], el[:, t, :])
            link(ins)
            link(v.tensor_copy(eif[:, :, :], ei[:, :, 0:2]))
            route.tick(v.tensor_tensor(wts[:, :, 2], e8[:, :, 1], e8[:, :, 0], ALU.subtract), "top2")
            pairs = [P, TT, 2, E]
            link(v.tensor_tensor(ohot[:, :, :, :], C("expert").unsqueeze(1).unsqueeze(1).broadcast_to(pairs), wide(eif[:, :, :], E),
                                 ALU.is_equal))
            route.tick(v.tensor_tensor(osum[:, :, :], ohot[:, :, 0, :], ohot[:, :, 1, :], ALU.add), "hot")
            route_act.wait(dve, "pair_exp")
            link(v.tensor_scalar(wts[:, :, 4], wts[:, :, 3], 1.0, None, ALU.add))
            link(v.tensor_tensor(wts[:, :, 4], wts[:, :, 4], gsum[:, :], ALU.mult))
            link(v.reciprocal(wts[:, :, 0], wts[:, :, 4]))
            route.tick(v.tensor_tensor(wts[:, :, 1], wts[:, :, 0], wts[:, :, 3], ALU.mult), "weights")
            route_pe.wait(dve, "rank")
            v.tensor_copy(rank[:, 0, :], ps[2][:, 0:E])
            link(v.tensor_copy(tot[:, :, :], ps[2][:, TT * E:2 * TT * E].rearrange("p (t e) -> p t e", t=TT)))
            for t in range(1, TT):
                ins = v.tensor_tensor(rank[:, t, :], ps[2][:, t * E:(t + 1) * E], tot[:, t - 1, :], ALU.add)
                link(v.tensor_tensor(tot[:, t, :], tot[:, t, :], tot[:, t - 1, :], ALU.add))
            cnt = tot[:, TT - 1, :]
            link(v.tensor_tensor(over_cnt, wide(cnt, T // BLK - 1), C("full_blocks").unsqueeze(1).broadcast_to(
                [P, E, T // BLK - 1]), ALU.is_gt))
            link(v.tensor_reduce(novf, over_cnt, AXX, ALU.add))
            a, b = 0, 1
            v.tensor_tensor(prod, ohot[:, :, :, :], rank[:, :, :].unsqueeze(2).broadcast_to(pairs), ALU.mult)
            link(v.tensor_copy(start[:, 0, :], novf))
            for k in (1, 2, 4, 8, 16):
                v.tensor_copy(start[:, b, 0:k], start[:, a, 0:k])
                link(v.tensor_tensor(start[:, b, k:E], start[:, a, k:E], start[:, a, 0:E - k], ALU.add))
                a, b = b, a
            v.tensor_reduce(pk.rearrange("p (t k) -> p t k", t=TT), prod, AXX, ALU.add)
            link(v.tensor_tensor(first, start[:, a, :], novf, ALU.subtract))
            link(v.tensor_tensor(first, first, C("blocks_on"), ALU.add))
            v.tensor_tensor(over_place, wide(pk, T // BLK - 1), C("full_blocks").unsqueeze(1).broadcast_to(
                [P, 8, T // BLK - 1]), ALU.is_ge)
            link(v.tensor_tensor(prod, ohot[:, :, :, :], first.unsqueeze(1).unsqueeze(1).broadcast_to(pairs), ALU.mult))
            v.tensor_reduce(quo, over_place, AXX, ALU.add)
            link(v.tensor_reduce(bk.rearrange("p (t k) -> p t k", t=TT), prod, AXX, ALU.add))
            v.scalar_tensor_tensor(pk, quo, -float(BLK), pk, ALU.mult, ALU.add)
            link(v.tensor_tensor(bk, bk, quo, ALU.add))
            link(v.scalar_tensor_tensor(bk, quo, 1.0, bk, ALU.is_ge, ALU.mult))
            link(v.tensor_tensor(bk, bk, eif[:, :, :].rearrange("p t k -> p (t k)"), ALU.add))
            by_block = [P, 8, 2, NBLK]
            link(v.tensor_tensor(hot_b[:, :, :, :], C("block").unsqueeze(1).unsqueeze(1).broadcast_to(by_block),
                                 wide(wide(bk, 2), NBLK), ALU.is_equal))
            v.tensor_tensor(hot_p.rearrange("p n (a b) -> p n a b", a=2),
                            C("place").unsqueeze(1).unsqueeze(1).broadcast_to([P, 8, 2, BLK]), wide(wide(pk, 2), BLK),
                            ALU.is_equal)
            route.tick(v.tensor_tensor(hot_b[:, :, :, :], hot_b[:, :, :, :], wide(C("numbers").rearrange(
                "p (n k) -> p n k", k=2), NBLK), ALU.mult), "places")
            v.tensor_tensor(later, start[:, a, :].unsqueeze(1).broadcast_to([P, NOVF, E]),
                            C("block")[:, 0:NOVF].unsqueeze(2).broadcast_to([P, NOVF, E]), ALU.is_le)
            link(v.tensor_copy(ovf[0:1, NOVF:NOVF + 1], start[0:1, a, E - 1:E]))
            link(v.tensor_reduce(later_cnt[:, 0:NOVF], later, AXX, ALU.add))
            link(v.tensor_scalar(later_cnt[:, 0:NOVF], later_cnt[:, 0:NOVF], float(E - 1), None, ALU.min))
            link(v.tensor_copy(ovf[0:1, 0:NOVF], later_cnt[0:1, 0:NOVF]))
            route_pe.wait(dve, "table")
            link(v.tensor_copy(tval[:, 0, :], ps[3][:, 0:2 * NBLK]))
            link(v.tensor_scalar(tval[:, 1, :], tval[:, 0, :], 0.0, 16384.0, ALU.is_equal, ALU.mult))
            link(v.tensor_scalar(tval[:, 1, NBLK:2 * NBLK], tval[:, 1, NBLK:2 * NBLK], C("half2"), None, ALU.add))
            link(v.scalar_tensor_tensor(tok_of[:, :], tval[:, 0, 0:NBLK], -1.0, tval[:, 1, 0:NBLK], ALU.add, ALU.add))
            route.tick(v.scalar_tensor_tensor(row_of[:, :], tval[:, 0, NBLK:2 * NBLK], 2.0, tval[:, 1, NBLK:2 * NBLK],
                                              ALU.mult, ALU.add), "table")

            def expert(n, par, kpar, reuse):
                xt, hiddenT = ps[par], ps[4 + par]
                dve.wait_ge(xt_filled, n + 1)
                if reuse is not None:
                    dve.wait_ge(gu_filled, reuse)
                v.tensor_tensor(xT[:, par, :, :], xt[:, :].rearrange("p (j n) -> p j n", j=KT),
                                wide(mod_gain[:, 2, :], BLK), ALU.mult).then_inc(xt_scaled, 1)
                dve.wait_ge(xt_scaled, n + 1)
                v.tensor_tensor(xT[:, par, :, :], xT[:, par, :, :], wide(mod[:, 3, :, 0], BLK), ALU.add).then_inc(
                    xt_ready, 1)
                dve.wait_ge(silu_ready, n + 1)
                if reuse is not None:
                    dve.wait_ge(y_filled, reuse)
                v.tensor_tensor(hidE[:, par, :, :], sg[:, par, :, :],
                                hiddenT[:, :].rearrange("p (f n) -> p f n", f=4)[:, :, BLK:2 * BLK],
                                ALU.mult).then_inc(hid_ready, 1)

            expert(0, 0, 0, None)
            expert(1, 1, 0, None)
            with dve.Fori(1, E // 2) as it:
                for par in range(2):
                    expert(2 * it + par, par, it, 2 * it + par - 1)
            later_n = dve.value_load(ovf[0:1, NOVF:NOVF + 1], min_val=0, max_val=NOVF)
            with dve.If(later_n > 0):
                with dve.Fori(0, later_n) as i:
                    expert(i + E, 0, i + E // 2, i + E)
            dve.wait_ge(final_in, 16)
            for t in range(TT + 1):
                if t < TT:
                    dve.wait_ge(y01_in[t], 16)
                    link(v.tensor_scalar(y01[:, t, 0, :], y01[:, t, 0, :], wts[:, t, 0:1], None, ALU.mult))
                    link(v.scalar_tensor_tensor(y01[:, t, 0, :], y01[:, t, 1, :], wts[:, t, 1:2], y01[:, t, 0, :],
                                                ALU.mult, ALU.add))
                    link(v.tensor_tensor(y01[:, t, 0, :], y01[:, t, 0, :], gates[:, 1, :], ALU.mult))
                    final_x.tick(v.tensor_tensor(x[:, t, :], x[:, t, :], y01[:, t, 0, :], ALU.add), t)
                if t >= 1:
                    rooted.wait(dve, ("final", t - 1))
                    link(v.reciprocal(rstd[:, t - 1:t], roots[:, t - 1:t]))
                    final_y.tick(v.scalar_tensor_tensor(y01[:, t - 1, 0, :], x[:, t - 1, :], rstd[:, t - 1:t], final_gain,
                                                        ALU.mult, ALU.mult), t - 1)


INPUTS = ["x", "norm1_g", "w_in", "qa_norm_g", "ka_norm_g", "qb_norm_g", "kb_norm_g", "outa_norm_g", "outb_norm_g",
          "w_out", "norm2_g", "w_up", "conv_w", "conv_b", "w_down", "c_2", "ctx_2", "c_ctx_2", "w_ada_2", "b_ada_2",
          "norm1_2", "w_in_2", "conv_w_2", "conv_b_2", "dt_bias_2", "a_log_2", "d_skip_2", "ssd_norm_2",
          "attn_sinks_2", "w_out_2", "norm2_2", "w_group_2", "b_group_2", "w_expert_2", "b_expert_2", "w_gate_2",
          "w_up_2", "w_down_2", "norm_final_2"]


def kernel(**inputs):
    import concourse.bacc as bacc
    from concourse.bass_utils import run_bass_kernel_spmd

    nc = bacc.Bacc("TRN2", target_bir_lowering=False, num_devices=1)
    arrays, aps = {}, {}
    for name in INPUTS:
        a = np.ascontiguousarray(inputs[name])
        arrays[f"in_{name}"] = a
        aps[name] = nc.dram_tensor(f"in_{name}", a.shape, F32, kind="ExternalInput").ap()
    tables = {"tables": constants()[1], "rotary": constants()[2], "distances": distance_tables()}
    for name, a in tables.items():
        arrays[name] = a
    consts_d, rope1_d, dist_d = (nc.dram_tensor(n, a.shape, F32, kind="ExternalInput").ap() for n, a in tables.items())
    h_d = nc.dram_tensor("normed_tokens", (T, D), F32, kind="Internal").ap()
    y_d = nc.dram_tensor("expert_outputs", (4 * T, D // 2), F32, kind="Internal").ap()
    out = nc.dram_tensor("out", (1, T, D), F32, kind="ExternalOutput").ap()
    two_blocks(nc, consts_d, rope1_d, dist_d, h_d, y_d, aps, out)
    r = run_bass_kernel_spmd(nc, [arrays], core_ids=[0])
    return r.results[0]["out"]
```

```python
import numpy as np
import concourse.bass as bass
from concourse import mybir
from contextlib import ExitStack

F32 = mybir.dt.float32
F32R = mybir.dt.float32r
I32 = mybir.dt.int32
U32 = mybir.dt.uint32
ALU = mybir.AluOpType
ACT = mybir.ActivationFunctionType
AXX = mybir.AxisListType.X

P = 128
T, CTX, D = 512, 256, 1024
TT, CT = T // P, CTX // P
AT = TT + CT
KT = D // P
HD = 64
H = 8
W1 = 2304
DFF = 2816
FT = DFF // P
E = 32
EG = 8
EF = 512
BLK = 64
NOVF = 2 * T // BLK - 1
NBLK = E + NOVF
EPS = 1e-6
BIG = 1e30
RING = 3
UNIT = 4096
HALF = UNIT // 2
ARENA = 17760
BIASW = T + (TT - 1) * P


def constants():
    f = np.float32
    i = np.arange(P)
    col = i[:, None]
    row = i[None, :]
    t = {}
    t["ident"] = np.eye(P, dtype=f)
    t["eps"] = np.full((P, 1), EPS, f)
    t["zero"] = np.zeros((P, 1), f)
    t["upto"] = (col <= row).astype(f)
    t["from"] = (col >= row).astype(f)
    t["before"] = (col < row).astype(f)
    t["one"] = np.ones((P, 1), f)
    group_row = (i % 32 == 0).astype(f)[:, None]
    t["sum_two"] = np.concatenate([group_row, (i % 32 == 1).astype(f)[:, None]], axis=1)
    t["window"] = np.concatenate([np.where(row >= col, 0, BIG), np.zeros((P, P)), np.where(row <= col, 0, BIG),
                                  np.zeros((P, CTX))], axis=1).astype(f)
    tok = np.arange(T)
    r, c = (tok // 64).astype(f)[:, None], (tok % 64).astype(f)[:, None]

    def tiles(a):
        return a.reshape(TT, P, -1).transpose(1, 0, 2).reshape(P, -1).astype(f)

    inv = (f(10000.0) ** (-np.arange(0, 32, 2, dtype=f) / f(32))).astype(f)[None]
    ar, ac = r * inv, c * inv
    rope1 = tiles(np.concatenate([np.cos(ar), np.cos(ar), np.cos(ac), np.cos(ac)], 1)), tiles(np.concatenate(
        [-np.sin(ar), np.sin(ar), -np.sin(ac), np.sin(ac)], 1))
    inv = (f(10000.0) ** (-np.arange(16, dtype=f) / f(16))).astype(f)[None]
    a = np.concatenate([r * inv, c * inv], 1)
    t["cos2"] = tiles(np.concatenate([np.cos(a), np.cos(a)], 1))
    t["sin2"] = tiles(np.concatenate([-np.sin(a), np.sin(a)], 1))
    t["low"] = (i < 64).astype(f)[:, None]
    t["high"] = (i >= 64).astype(f)[:, None]
    e = np.arange(E)
    t["expert"] = np.tile(e, (P, 1)).astype(f)
    t["group"] = np.tile(e // EG, (P, 1)).astype(f)
    t["blocks_on"] = np.tile(E - 1 - e, (P, 1)).astype(f)
    t["block"] = np.tile(np.arange(NBLK), (P, 1)).astype(f)
    t["place"] = np.tile(np.arange(BLK), (P, 1)).astype(f)
    t["full_blocks"] = np.tile(BLK * np.arange(1, T // BLK), (P, 1)).astype(f)
    t["both_halves"] = (i[:, None] % 64 == np.arange(E + E // EG)[None]).astype(f)
    both = 2 * tok.reshape(TT, P).T[:, :, None] + np.arange(2) + 1
    t["numbers"] = np.stack([(both + 1) // 2, both], axis=-1).reshape(P, 4 * TT).astype(f)
    t["half2"] = (i // BLK - 2).astype(f)[:, None]
    at, out = {}, []
    for k, v in t.items():
        at[k] = (sum(x.shape[1] for x in out), v.shape[1])
        out.append(v.astype(f))
    return at, np.ascontiguousarray(np.concatenate(out, axis=1)), np.ascontiguousarray(np.concatenate(rope1, axis=1))


def distance_tables():
    off = np.abs(np.arange(P)[:, None] - (np.arange(BIASW)[None] - (TT - 1) * P))
    seen = (off <= 64).astype(np.int64) + ((off <= 256) & (off % 4 == 0)) + (off % 16 == 0)
    log = np.where(seen > 0, np.log(np.maximum(seen, 1)), -BIG)
    slope = 2.0 ** (-np.arange(1, H + 1))
    return (slope[:, None, None] * off[None] - log[None]).astype(np.float32)


class Steps:

    def __init__(self, sem, keys):
        self.sem, self.at, self.done = sem, {k: n + 1 for n, k in enumerate(keys)}, 0

    def tick(self, ins, key):
        self.done += 1
        assert self.at[key] == self.done, (key, self.done)
        ins.then_inc(self.sem, 1)

    def wait(self, eng, key):
        eng.wait_ge(self.sem, self.at[key])


class Chain:

    def __init__(self, sem):
        self.sem, self.n = sem, 0

    def link(self, eng, ins):
        self.n += 1
        ins.then_inc(self.sem, 1)
        eng.wait_ge(self.sem, self.n)


class Banks:

    def __init__(self, banks, sems):
        self.banks, self.sems, self.order, self.at = banks, sems, [], {}
        self.opened = 0

    def plan(self, key, freed):
        self.at[key] = len(self.order)
        self.order.append((key, freed))

    def open(self, pe, key):
        n = self.at[key]
        assert n == self.opened, (key, n, self.opened)
        self.opened += 1
        if n >= 8:
            steps, step = self.order[n - 8][1]
            steps.wait(pe, step)
        return self.banks[n % 8]

    def close(self, ins, key):
        ins.then_inc(self.sems[self.at[key] % 8], 1)

    def filled(self, eng, key):
        n = self.at[key]
        eng.wait_ge(self.sems[n % 8], n // 8 + 1)
        return self.banks[n % 8]



def two_blocks(nc, consts_d, rope1_d, dist_d, h_d, y_d, inp, out):
    ctx = ExitStack()
    with ctx:
        cols, _, _ = constants()
        ncols = sum(w for _, w in cols.values())

        def sb(name, shape, dt=F32):
            return ctx.enter_context(nc.sbuf_tensor(name, shape, dt))

        def sem(name):
            return ctx.enter_context(nc.semaphore(name))

        def steps(name, keys):
            return Steps(sem(name), list(keys))

        def wide(v, n):
            return v.unsqueeze(len(v.shape)).broadcast_to(list(v.shape) + [n])

        const = sb("const", [P, ncols])

        def C(name, parts=P):
            a, w = cols[name]
            return const[0:parts, a:a + w]

        ident = C("ident")
        x = sb("x_res", [P, TT, D])
        hT_at = nc.sbuf_base
        hT = sb("hT", [P, KT, T])
        hTc_at = nc.sbuf_base
        hTc = sb("hTc", [P, KT, CTX])
        xn_at = nc.sbuf_base
        xn = sb("xn", [P, AT, D])
        ring_at = nc.sbuf_base
        ring = sb("ring", [P, RING, UNIT])
        gains = sb("gains", [P, 6, KT])
        convw = sb("convw", [P, 224])
        ada_bias = sb("ada_bias", [P, 6, KT])
        cvec = sb("cvec", [P, 2, KT])
        csilu = sb("csilu", [P, KT, 32])
        mod = sb("mod", [P, 6, KT, 2])
        mod_gain = sb("mod_gain", [P, 3, KT])
        gates = sb("gates", [P, 2, D])
        dt_bias, a_log = sb("dt_bias", [P, 16]), sb("a_log", [P, 16])
        d_skip, sinks, route_bias = sb("d_skip", [P, 8]), sb("sinks", [P, 8]), sb("route_bias", [P, 36])
        route_w = sb("route_w", [P, KT, 36])
        sums, roots, rstd = sb("sums", [P, 12]), sb("roots", [P, 12]), sb("rstd", [P, 12])
        warm = sb("warm", [P, 8])
        head_sum, head_root = sb("head_sum", [P, 2, 8]), sb("head_root", [P, 2, 8])
        nmin, psums, rsums = sb("nmin", [P, 96]), sb("psums", [P, 96]), sb("rsums", [P, 96])
        win_min, sink_exp = sb("win_min", [P, 72]), sb("sink_exp", [P, 32])
        arena_at = nc.sbuf_base
        arena = sb("arena", [P, ARENA])
        LOW_AT = 13312
        DIST_AT = 14336

        def over(name, shape, column):
            return nc.alloc_sbuf_tensor_at(name, shape, F32R, offset=column)

        hT_high = over("hT_high", [P, KT, T], hT_at)
        hT_low = over("hT_low", [P, KT, T], arena_at + 4 * LOW_AT)
        low1 = [over("hT_low_a", [P, 4, T], hTc_at), over("hT_low_b", [P, 3, T], arena_at + 4 * DIST_AT),
                over("hT_low_c", [P, 1, T], xn_at + 4 * TT * D)]

        def low_row(name, j):
            return low1[j // 4 + j // 7][:, j % 7 % 4, :] if name == "norm1" else hT_low[:, j, :]

        w_high = over("weights_high", [P, 2, HALF], ring_at + 4 * UNIT)
        w_low = over("weights_low", [P, 2, HALF], ring_at + 8 * UNIT)
        hid_high = hT_high[:, 0:4, :].rearrange("p (b f) n -> p b f n", b=2)
        hid_low = hT_high[:, 4:8, :].rearrange("p (b f) n -> p b f n", b=2)

        def carve(start, *shape, of=arena):
            n = int(np.prod(shape))
            v = of[:, start:start + n]
            names = "abcd"[:len(shape)]
            if len(shape) > 1:
                v = v.rearrange(f"p ({' '.join(names)}) -> p {' '.join(names)}",
                                **{k: s for k, s in zip(names[1:], shape[1:])})
            return v

        def packed(size_of, start=0, of=arena, limit=ARENA):
            views = []
            for shape in size_of:
                views.append(carve(start, *shape, of=of))
                start += int(np.prod(shape))
            assert start <= limit, start
            return views

        hT_flat = hT[:, :, :].rearrange("p j n -> p (j n)")
        ring_flat = ring[:, :, :].rearrange("p a n -> p (a n)")
        hTc_flat = hTc[:, :, :].rearrange("p j n -> p (j n)")
        spare = xn[:, TT:AT, :].rearrange("p t n -> p (t n)")

        vA, vB, pj, sq, qaT, qbT, kzA, kzB, dist, rope1, head_gain = packed(
            [(TT, 128), (TT, 512), (3, 512), (2, 512), (4, T), (4, T), (2, T), (8, T), (2, BIASW), (2, TT, HD),
             (4, HD)])
        assert DIST_AT == TT * 640 + 5 * 512 + 10 * T + 8 * T
        junk1, rope_t = carve(0, D, of=spare), carve(D, 2, 512, of=spare)
        probs, probsT, attT = pj, carve(0, 4, T, of=hTc_flat), carve(17300, 2, P)
        dists = [dist[:, 0, :], dist[:, 1, :], carve(0, BIASW, of=spare), carve(BIASW, BIASW, of=spare)]
        modrow = sq
        junk_c = hTc_flat[:, 0:D]
        conv_rows = carve(16900, 3, P)
        hid, conv_g, conv_v = packed([(FT, T), (2, T), (2, T)])
        zs, u, kvd, q2, xs_tok, b_tok = packed(
            [(TT, 512), (KT, T + CTX), (AT, 272), (TT, 512), (AT, 512), (AT, 256)])
        junk2 = carve(0, D)
        conv2 = carve(0, 2, T + CTX, of=spare)
        u_flat = carve(TT * 512, 4 * (T + CTX))
        slot = ring[:, 1, :]
        q2T, kz2 = carve(0, 4, T, of=slot), carve(2048, 2, T + CTX, of=slot)
        rope_q, rope_k = carve(12288, 2, 512), carve(11904, 2, P)
        wprobs, wprobsT = packed([(3, 640), (3, 640)], of=ring[:, 2, :], limit=UNIT)
        state = carve(0, 2, 4, 512, of=hT_flat)
        state0, dtxw = packed([(2, 512), (2, 512)], of=hTc_flat, limit=2048)
        dtx, cbm, ytmp = packed([(2, 512), (2, 2, P), (512,)], of=spare, limit=2048)
        decay = u_flat[:, 0:3072].rearrange("p (a b c) -> p a b c", a=3, b=8)
        wattT = carve(TT * 512 + KT * (T + CTX) + AT * 272, 2, P)
        stmp = carve(TT * 512 + KT * (T + CTX) + AT * 272 + 2 * P, 2, 512)
        skip_x = carve(2048 + 2 * (T + CTX), 512, of=slot)
        sm = sb("ssd_small", [P, 10, 96])
        cat = xn

        ps = [ctx.enter_context(nc.psum_tensor(f"bank{i}", [P, 512], F32)) for i in range(8)]
        banks = Banks(ps, [sem(f"bank_filled{i}") for i in range(8)])

        x_in, const_in, more_in, ctx_in = [sem(f"x_in{t}") for t in range(TT)], sem("const_in"), sem("more_in"), sem("ctx_in")
        dist_in = [sem(f"dist_in{i}") for i in range(4)]
        unit_in = {p: sem(f"unit_in_{p}") for p in ("slot0", "slot1", "slot2", "half0", "half1")}
        dve_chain, act_chain, pool_chain = Chain(sem("dve_order")), Chain(sem("act_order")), Chain(sem("pool_order"))

        zero = C("zero")
        XT, XC = range(TT), range(TT, AT)
        NORMS = {
            "norm1": (lambda t: x[:, t, :], XT, [(0, D)], junk1, lambda j: (gains[:, 0, j:j + 1], zero)),
            "mix1": (lambda t: xn[:, t, :], XT, [(0, 512), (512, D)], junk1, lambda j: (gains[:, 1, j:j + 1], zero)),
            "norm2": (lambda t: x[:, t, :], XT, [(0, D)], junk1, lambda j: (gains[:, 2, j:j + 1], zero)),
            "context": (lambda t: xn[:, t, :], XC, [(0, D)], junk_c,
                        lambda j: (mod_gain[:, 1, j:j + 1], mod[:, 0, j, 1:2])),
            "norm1_2": (lambda t: x[:, t, :], XT, [(0, D)], junk2,
                        lambda j: (mod_gain[:, 0, j:j + 1], mod[:, 0, j, 0:1])),
            "mix2": (lambda t: cat[:, t, :], XT, [(0, 512)], u_flat[:, 0:D], lambda j: (gains[:, 4, j:j + 1], zero)),
            "norm2_2": (lambda t: x[:, t, :], XT, [(0, D)], hTc_flat[:, 0:D],
                        lambda j: (mod_gain[:, 2, j:j + 1], mod[:, 3, j, 0:1])),
        }
        norm_keys = [(s, t, a) for s, (_, tiles, parts, _, _) in NORMS.items() for t in tiles for a, _ in parts]
        squared = steps("norm_squared", norm_keys + [("final", t, 0) for t in range(TT)])
        rooted = steps("norm_rooted", [(s, t) for s, n in NORMS.items() for t in n[1]] + [("final", t) for t in range(TT)])
        normed = steps("normed", norm_keys)

        def halves(s):
            return [(s, j) for j in range(KT)]

        SPLIT_NORMS = ("norm1", "mix1", "norm2", "norm1_2", "mix2")
        hT_act = steps("hT_by_act", [k for s in NORMS for k in halves(s) if k[1] % 2 == 0 or s in SPLIT_NORMS])
        hT_dve = steps("hT_by_dve", [k for s in NORMS for k in halves(s) if k[1] % 2 == 1 or s in SPLIT_NORMS])

        def hT_step(k):
            return hT_act if k[1] % 2 == 0 and k[0] not in SPLIT_NORMS else hT_dve

        PROJ = [(c, t) for c in range(5) for t in range(TT)]
        HEADS_OF = [[(0, 8, 0)], [(0, 2, 1), (4, 4, 2)], [(0, 4, 2), (4, 4, 3)], [(0, 4, 3)]]
        conv_ready = steps("conv_weights", ["taps"])
        pj_ready = steps("proj_copied", range(16))
        v_tail = steps("v_tail", range(TT))
        head_summed = steps("head_summed", range(16))
        head_rooted = steps("head_rooted", range(16))
        qk_ready = steps("qk_normed", range(16))
        qk_drained = steps("qk_transposed", range(16))

        NU = 2 * H * TT

        def unit_of(i):
            m, pair, t, par = i // (H * TT), i // (2 * TT) % (H // 2), i // 2 % TT, i % 2
            return m, 2 * pair + par, t

        score_min = steps("score_min", range(NU))
        prob = steps("prob", range(NU))
        pt_act = steps("probsT_by_act", range(0, NU, 2))
        pt_dve = steps("probsT_by_dve", range(1, NU, 2))
        att_copied = steps("attended_copied", range(NU // 2))
        att = steps("attended", range(NU // 2))
        mod_silu = steps("mod_silu", ["c"])
        mod_copied = steps("mod_copied", range(12))
        mod_done = steps("mod_done", list(range(12)) + ["gains"])

        def pt_step(i):
            return pt_dve if i % 2 else pt_act

        def mixed_at(i):
            t = (i - (NU - 2 * TT + 7)) // 2
            return t if 0 <= t < TT - 1 and i % 2 else None

        SIDES = [(t, n) for t in range(TT) for n in range(2)]
        x1 = steps("x_after_attention", SIDES)
        tap_mid = steps("conv_middle_tap", [(f, g) for f in range(FT) for g in range(2)])
        tapped = steps("conv_tapped", [(f, g) for f in range(FT) for g in range(2)])
        gelued = steps("gelued", range(FT))
        hidden = steps("hidden", range(FT))
        ND = FT // 2
        GROWN = {"w_out": (KT // 2, ("out1", TT - 1, 1)), "w_down": (ND, ("down", TT - 1, 1)), "w_kvd": (2, ("kvd", AT - 1)),
                 "w_zq": (KT // 2, ("z", TT - 1)), "w_out2": (KT // 2, ("out2", TT - 1, 1))}
        SPLITS = [(name, i) for name, many in (("w_in", 10), ("w_out", KT // 2), ("w_up", FT), ("w_down", ND), ("w_kvd", 2),
                                               ("w_zq", KT // 2), ("w_xbc", 4), ("w_out2", KT // 2)) for i in range(many)]
        SPLIT_AT = {key: k for k, key in enumerate(SPLITS)}
        high_ready = steps("weights_high_ready", range(len(SPLITS)))
        low_ready = steps("weights_low_ready", range(len(SPLITS)))
        hid_high_ready = steps("hidden_high_ready", range(ND))
        hid_low_ready = steps("hidden_low_ready", range(ND))
        grown = steps("unit_added", [(name, i) for name, i in SPLITS if name in GROWN and i < GROWN[name][0] - 1 or
                                     name == "w_in" and i % 2 == 0])

        def products(eng, key):
            name, i = key
            if name == "w_up":
                banks.filled(eng, ("up", i, 1))
            elif name == "w_xbc":
                banks.filled(eng, ("xbc", 2 * i + 1, 1))
            elif name == "w_in" and i % 2 == 1:
                banks.filled(eng, ("proj", 2 * i + 1))
            elif name == "w_in" or i < GROWN[name][0] - 1:
                grown.wait(eng, key)
            else:
                banks.filled(eng, GROWN[name][1])

        x2 = steps("x_after_ffn", SIDES)

        kvd_copied = steps("kv_dt_copied", range(AT))
        XBC = [(m, c) for m in range(KT) for c in range(2)]
        mid2 = steps("conv2_middle_tap", XBC)
        tapped2 = steps("conv2_tapped", XBC)
        u_ready = steps("conv2_silu", range(KT))
        z_ready = steps("z_silu", range(TT))
        q_copied = steps("q_copied", range(TT))
        roped_k, roped_q = steps("roped_k", range(TT)), steps("roped_q", range(TT))
        tok_copied = steps("tokens_first", [("xs", t) for t in range(AT)] + [("b", t) for t in range(0, AT, 2)])
        kz_ready = steps("k_transposed", range(2))
        q2_ready = steps("q_transposed", range(4))
        csilu_cleared = steps("csilu_cleared", [0])
        row_ready = sem("row_ready")
        dt_abs, dt_exp, dt_log = steps("dt_abs", [0, 1]), steps("dt_exp", [0]), steps("dt_log", [0])
        a_exp = steps("a_exp", [0])
        dta_ready = steps("dt_times_a", [0])
        cs_copied = steps("cumsums", [0])
        cs_exp = steps("cumsum_exps", [0])
        sw_ready = steps("state_weights", [0])

        TILE_AT = [[TT, TT + 1, 0, 1, 2, 3], [TT + 1, TT, 3, 2, 1, 0]]
        STATES = [(d, i) for i in range(5) for d in range(2)]
        NW = H * TT
        YS = [(t, d) for t in range(TT) for d in range(2)]
        ssd = [("state", k) for k in range(len(STATES))] + [("y", k) for k in range(len(YS) + 2)]
        weave, n = [], 0
        for i in range(NW + 4):
            weave.append(("win", i))
            while n * (NW + 4) < len(ssd) * (i + 1) and n < len(ssd):
                weave.append(ssd[n])
                n += 1
        state_decayed = steps("state_decayed", [k for k, (_, pos) in enumerate(STATES) if pos])
        dtxw_ready = steps("weighted_x", range(len(STATES)))
        state_ready = steps("state_ready", range(len(STATES)))
        dtx_ready = steps("dt_x", range(len(YS)))
        cb_masked = steps("cb_masked", range(TT))
        seg_ready = steps("segments", [(k, g) for k in range(len(YS)) for g in range(2)])
        decayed = steps("decay_exp", range(len(YS)))
        m_ready = steps("decay_times_cb", range(len(YS)))
        y_read = steps("y_read", [(k, w) for k in range(len(YS)) for w in ("off", "diag")] )
        y_done = steps("y_done", range(TT))
        wscore = steps("win_score", range(NW))
        wprob = steps("win_prob", range(NW))
        wpt_act = steps("win_probsT", range(NW))
        watt_copied = steps("win_attended_copied", range(NW // 2))
        watt = steps("win_attended", range(NW // 2))

        def window_of(i):
            return 2 * (i // (2 * TT)) + i % 2, i // 2 % TT

        x3 = steps("x_after_mixers", SIDES)

        def near(t):
            return max(0, t - 1), min(TT - 1, t + 1)

        def plan_norm(s):
            for k in halves(s):
                banks.plan(("hT",) + k, (hT_step(k), k))

        plan_norm("norm1")
        for c in range(5):
            for n in range(4 * c, 4 * c + 4):
                banks.plan(("proj", n), (pj_ready, n) if n < 16 else (v_tail, n - 16))
            for n in range(4 * c - 2, 4 * c + 2):
                if 0 <= n < 16:
                    banks.plan(("qkT", n), (qk_drained, n))
        banks.plan("conv_weights", (conv_ready, "taps"))
        for i in range(NU + 4):
            if i < NU:
                banks.plan(("score", i), (prob, i) if i < NU // 2 else (score_min, i))
            if 1 <= i <= NU:
                banks.plan(("probsT", i - 1), (pt_step(i - 1), i - 1))
            if i >= 4 and i % 2 == 0:
                banks.plan(("att", i // 2 - 2), (att_copied, i // 2 - 2))
            if i >= 5 and i % 2 == 1:
                banks.plan(("attT", i // 2 - 2), (att, i // 2 - 2))
            if i % 5 == 2 and i // 5 < 12:
                banks.plan(("modrow", i // 5), (mod_copied, i // 5))
            if i % 5 == 4 and i // 5 < 12:
                banks.plan(("mod", i // 5), (mod_done, i // 5))
        plan_norm("mix1")
        for k in SIDES:
            banks.plan(("out1",) + k, (x1, k))
        plan_norm("norm2")
        for f in range(FT):
            for g in range(2):
                banks.plan(("up", f, g), (tapped, (f, g)))
        plan_norm("context")
        for k in SIDES:
            banks.plan(("down",) + k, (x2, k))
        plan_norm("norm1_2")
        for t in range(AT):
            banks.plan(("kvd", t), (kvd_copied, t))
        for t in range(TT):
            banks.plan(("q2", t), (q_copied, t))
        for t in range(TT):
            banks.plan(("z", t), (z_ready, t))
        banks.plan("cumsum", (cs_copied, 0))
        for k in XBC:
            banks.plan(("xbc",) + k, (tapped2, k))
        for t in range(AT):
            banks.plan(("xs", t), (tok_copied, ("xs", t)))
        for t in range(0, AT, 2):
            banks.plan(("b", t), (tok_copied, ("b", t)))
        for n in range(2):
            banks.plan(("kT", n), (kz_ready, n))
        for j in range(4):
            banks.plan(("q2T", j), (q2_ready, j))
        for what, i in weave:
            if what == "win":
                if i < NW:
                    banks.plan(("wscore", i, 0), (wscore, i))
                    banks.plan(("wscore", i, 1), (wscore, i))
                if 2 <= i <= NW + 1:
                    banks.plan(("wprobsT", i - 2, 0), (wpt_act, i - 2))
                    banks.plan(("wprobsT", i - 2, 1), (wpt_act, i - 2))
                if i >= 4 and i % 2 == 0:
                    banks.plan(("watt", i // 2 - 2), (watt_copied, i // 2 - 2))
                if i >= 5 and i % 2 == 1:
                    banks.plan(("wattT", i // 2 - 2), (watt, i // 2 - 2))
            elif what == "state":
                banks.plan(("state", i), (state_ready, i))
            else:
                if i < len(YS):
                    if i % 2 == 0:
                        banks.plan(("cb", i // 2), (cb_masked, i // 2))
                    banks.plan(("seg", i, 0), (seg_ready, (i, 0)))
                    banks.plan(("seg", i, 1), (seg_ready, (i, 1)))
                if i >= 2:
                    banks.plan(("yoff", i - 2), (y_read, (i - 2, "off")))
                    banks.plan(("ydiag", i - 2), (y_read, (i - 2, "diag")))
        plan_norm("mix2")
        for k in SIDES:
            banks.plan(("out2",) + k, (x3, k))
        plan_norm("norm2_2")

        def by_k(name):
            return inp[name].rearrange("(p j) n -> p j n", j=KT)

        win_v, wout_v, wup_v = by_k("w_in"), by_k("w_out"), by_k("w_up")
        wada_v = inp["w_ada_2"].rearrange("a (p j) n -> p (a j) n", j=KT)
        win2_v = inp["w_in_2"].rearrange("a (p j) n -> p (a j) n", j=KT)
        wout2_v = inp["w_out_2"].rearrange("a (p j) n -> p (a j) n", j=KT)
        wdown_v = inp["w_down"].rearrange("(f p) n -> p f n", p=P)
        PLACES = {"slot0": (0, UNIT), "slot1": (UNIT, UNIT), "slot2": (2 * UNIT, UNIT), "half0": (0, HALF),
                  "half1": (HALF, HALF)}
        UNITS = []

        def unit(key, place, width, parts, free):
            UNITS.append((key, place, width, parts, free))

        def split_unit(key, width, parts):
            unit(key, f"half{SPLIT_AT[key] % 2}", width, parts, ("split", key))

        for i in range(10):
            c, rows = i // 2, slice(4 * (i % 2), 4 * (i % 2) + 4)
            w = min(512, W1 - c * 512)
            split_unit(("w_in", i), w, [(0, win_v[:, rows, c * 512:c * 512 + w])])
        for m in range(12):
            unit(("w_ada", m), f"slot{m % RING}", 512, [(0, wada_v[:, :, m * 512:m * 512 + 512])], ("modrow", m))
        for i in range(KT // 2):
            split_unit(("w_out", i), D, [(0, wout_v[:, 2 * i:2 * i + 2, :])])
        for f in range(FT):
            split_unit(("w_up", f), 256, [(0, wup_v[:, :, f * P:f * P + P]), (P, wup_v[:, :, DFF + f * P:DFF + f * P + P])])
        for i in range(ND):
            split_unit(("w_down", i), D, [(0, wdown_v[:, 2 * i:2 * i + 2, :])])
        for i in range(2):
            rows = slice(4 * i, 4 * i + 4)
            split_unit(("w_kvd", i), 272, [(0, win2_v[:, rows, 1536:1552]), (16, win2_v[:, rows, 2064:2320])])
        for i in range(KT // 2):
            rows = slice(2 * i, 2 * i + 2)
            split_unit(("w_zq", i), D, [(0, win2_v[:, rows, 0:512]), (512, win2_v[:, rows, 1552:2064])])
        for i in range(4):
            split_unit(("w_xbc", i), 256, [(0, win2_v[:, :, 512 + i * 256:768 + i * 256])])
        for i in range(KT // 2):
            split_unit(("w_out2", i), D, [(0, wout2_v[:, 2 * i:2 * i + 2, :])])
        UNIT_AT, UNIT_AFTER, count, lies = {}, {}, {p: 0 for p in PLACES}, {}
        for key, place, width, parts, free in UNITS:
            count[place] += 16 * len(parts)
            UNIT_AT[key] = (place, width, parts[0][1].shape[1], count[place])
            a, n = PLACES[place]
            gone = [p for p in lies if PLACES[p][0] < a + n and a < sum(PLACES[p])]
            UNIT_AFTER[key] = [lies[p] for p in gone]
            if key in (("w_ada", 1), ("w_ada", 2)):
                UNIT_AFTER[key].append(("proj", len(PROJ) - 1))
            for p in gone:
                if PLACES[p][0] >= a and sum(PLACES[p]) <= a + n:
                    lies.pop(p)
            lies[place] = free

        def unit_view(place, width, rows):
            a = PLACES[place][0]
            return ring_flat[:, a:a + rows * width].rearrange("p (j n) -> p j n", n=width)

        def weights(pe, key):
            place, width, rows, value = UNIT_AT[key]
            pe.wait_ge(unit_in[place], value)
            return unit_view(place, width, rows)

        def part_view(part, key):
            _, width, rows, _ = UNIT_AT[key]
            return part[:, SPLIT_AT[key] % 2, 0:rows * width].rearrange("p (j n) -> p j n", n=width)

        def raw_view(key):
            place, width, rows, _ = UNIT_AT[key]
            return unit_view(place, width, rows)

        EXPERT_SLOTS = [arena[:, i * UNIT:(i + 1) * UNIT] for i in range(3)] + [ring[:, i, :] for i in range(3)]
        (hot_p, hot_b, lg, gl, g8, e8, el, ohot, osum, tot, rank, prod, first, novf, over_cnt, start, later,
         pk, bk, quo, over_place, gexp, gsum, wts, tval, lgT) = packed(
            [(8, P), (8, 2, NBLK), (TT, 36), (TT, 8), (TT, 8), (TT, 8), (TT, E), (TT, 2, E), (TT, E), (TT, E),
             (TT, E), (TT, 2, E), (E,), (E,), (E, T // BLK - 1), (2, E), (NOVF, E), (8,), (8,), (8,),
             (8, T // BLK - 1), (TT, 4), (TT,), (TT, 6), (3, 2 * NBLK), (T,)], start=3 * UNIT)
        gi, ei = sb("group_index", [P, TT, 8], U32), sb("expert_index", [P, TT, 8], U32)
        gif, eif = sb("group_index_f", [P, TT]), sb("expert_index_f", [P, TT, 2])
        tok_of, row_of = sb("token_of_place", [P, NBLK], I32), sb("row_of_place", [P, NBLK], I32)
        later_cnt = sb("later_counts", [P, 16])
        ovf = sb("later_blocks", [1, NOVF + 1], I32)
        tok_at, row_at = sb("token_index", [P, 2], I32), sb("row_index", [P, 2], I32)
        xg = carve(0, 2, D, of=spare)
        xT, gu = packed([(2, KT, BLK), (2, 512)], of=hTc_flat, limit=2048)
        sg, hidE, yE = packed([(2, 4, BLK), (2, 4, BLK), (2, 512)], of=hT_flat, limit=KT * T)
        early_gate = xn[:, 0:TT, :].rearrange("p t n -> p (t n)")
        final_gain = carve(0, D, of=xn[:, 0:1, :].rearrange("p a n -> p (a n)"))
        junk3 = carve(0, D, of=xn[:, 1:2, :].rearrange("p a n -> p (a n)"))
        y01 = ring[:, 0:2, :].rearrange("p a n -> p (a n)").rearrange("p (t k n) -> p t k n", t=TT, k=2)
        expert_in = [sem(f"expert_in{i}") for i in range(6)]
        h_stored, y01_in, final_in, stored = sem("h_stored"), [sem(f"y01_in{t}") for t in range(TT)], sem("final_gain_in"), sem("stored")
        tokens_in = [sem("tokens_in0"), sem("tokens_in1")]
        y_stored = [sem("y_stored0"), sem("y_stored1")]
        index_ready, scattered = sem("index_ready"), sem("all_y_stored")
        xt_filled, xt_scaled, xt_ready = sem("expert_x_filled"), sem("expert_x_scaled"), sem("expert_x_ready")
        gu_filled, gu_ready = sem("gate_up_filled"), sem("gate_up_ready")
        ht_filled, silu_ready, hid_ready = sem("hiddenT_filled"), sem("expert_silu"), sem("expert_hidden")
        y_filled, y_ready = sem("expert_y_filled"), sem("expert_y_ready")
        route = steps("route", ["cleared", "odd", "logits", "max", "top2", "hot", "weights", "places", "table"])
        route_act = steps("route_act", ["even", "group_exp", "pair_exp"])
        route_pe = steps("route_pe", ["halves", "logits", "rank", "table"])
        final_x = steps("final_x", range(TT))
        final_y = steps("final_y", range(TT))

        small_loads = []

        def small(dst, src):
            small_loads.append((dst, src))

        FIRST_LOADS = 2
        now = cols["upto"][0]
        small(const[:, 0:now], consts_d[:, 0:now])
        small(gains[:, 0, :], inp["norm1_g"].rearrange("(p j) -> p j", j=KT))
        small(const[:, now:ncols], consts_d[:, now:ncols])
        small(rope1.rearrange("p a t d -> p (a t d)"), rope1_d)
        small(gains[:, 2, :], inp["norm2_g"].rearrange("(p j) -> p j", j=KT))
        small(gains[0:64, 1, :], inp["outa_norm_g"].rearrange("(p j) -> p j", j=KT))
        small(gains[64:128, 1, :], inp["outb_norm_g"].rearrange("(p j) -> p j", j=KT))
        small(gains[:, 3, :], inp["norm1_2"].rearrange("a (p j) -> p (a j)", j=KT))
        small(gains[0:64, 4, :], inp["ssd_norm_2"].rearrange("a (p j) -> p (a j)", j=KT))
        small(gains[:, 5, :], inp["norm2_2"].rearrange("a (p j) -> p (a j)", j=KT))
        for n, name in enumerate(("qa_norm_g", "ka_norm_g", "qb_norm_g", "kb_norm_g")):
            small(head_gain[:, n, :], inp[name].partition_broadcast(P))
        small(conv_rows[0:88, 0, :], inp["conv_w"][0:2, :].rearrange("k (f p) -> (k f) p", p=P))
        small(conv_rows[0:44, 1, :], inp["conv_w"][2, :].rearrange("(f p) -> f p", p=P))
        small(conv_rows[44:88, 1, :], inp["conv_b"].rearrange("(f p) -> f p", p=P))
        small(conv_rows[0:40, 2, :], inp["conv_w_2"].rearrange("a k (f p) -> (a k f) p", p=P))
        small(conv_rows[40:48, 2, :], inp["conv_b_2"].rearrange("a (f p) -> (a f) p", p=P))
        small(ada_bias[:, :, :], inp["b_ada_2"].rearrange("a (s p j) -> p (a s) j", s=6, j=KT))
        small(cvec[:, 0, :], inp["c_2"].rearrange("a (p j) -> p (a j)", j=KT))
        small(cvec[:, 1, :], inp["c_ctx_2"].rearrange("(p j) -> p j", j=KT))
        small(gates[:, 0, :], inp["b_ada_2"][0, 2 * D:3 * D].partition_broadcast(P))
        small(gates[:, 1, :], inp["b_ada_2"][0, 5 * D:6 * D].partition_broadcast(P))
        small(dt_bias[:, :], inp["dt_bias_2"].rearrange("a d h -> (a d h)").partition_broadcast(P))
        small(a_log[:, :], inp["a_log_2"].rearrange("a d h -> (a d h)").partition_broadcast(P))
        small(d_skip[:, :], inp["d_skip_2"].rearrange("a h -> (a h)").partition_broadcast(P))
        small(sinks[:, :], inp["attn_sinks_2"].rearrange("a h -> (a h)").partition_broadcast(P))
        small(route_bias[:, 0:4], inp["b_group_2"].rearrange("a h -> (a h)").partition_broadcast(P))
        small(route_bias[:, 4:36], inp["b_expert_2"].rearrange("a h -> (a h)").partition_broadcast(P))
        small(route_w[:, :, 0:4], inp["w_group_2"].rearrange("a (p j) n -> p (a j) n", j=KT))
        small(route_w[:, :, 4:36], inp["w_expert_2"].rearrange("a (p j) n -> p (a j) n", j=KT))
        CONST_ALL = 16 * FIRST_LOADS
        MORE_ALL = 16 * (len(small_loads) - FIRST_LOADS)
        block = ctx.enter_context(nc.Block())

        def held(eng, value):
            return value if isinstance(value, int) else eng.to_reg(value)

        def rope(eng, products, src, heads, t):
            cos, sin = (C(n).rearrange("p (t d) -> p t d", t=TT)[:, t, :] for n in ("cos2", "sin2"))
            s3, a3, b3 = (v.rearrange("p (h d) -> p h d", d=HD) for v in (src,) + products)
            eng.tensor_tensor(a3, s3, cos.unsqueeze(1).broadcast_to([P, heads, HD]), ALU.mult)
            for half in range(2):
                lo, other = half * 32, 32 - half * 32
                last = eng.tensor_tensor(b3[:, :, lo:lo + 32], s3[:, :, other:other + 32],
                                         sin[:, lo:lo + 32].unsqueeze(1).broadcast_to([P, heads, 32]), ALU.mult)
            return last

        def load_expert(sp, e, par, kpar, reuse, only=range(3)):
            for i, (name, pat) in enumerate((("w_gate_2", "a e (p j) f -> (a e) p (j f)"),
                                             ("w_up_2", "a e (p j) f -> (a e) p (j f)"),
                                             ("w_down_2", "a e (p f) d -> (a e) p (f d)"))):
                if i not in only:
                    continue
                kw = {"f": 4} if i == 2 else {"j": KT}
                if reuse is not None:
                    sp.wait_ge(gu_filled if i < 2 else y_filled, reuse)
                sp.dma_start(EXPERT_SLOTS[3 * par + i], inp[name].rearrange(pat, **kw)[e]).then_inc(
                    expert_in[3 * par + i], 16)

        @block.sync
        def _(sp):
            for t in range(TT):
                sp.dma_start(x[:, t, :], inp["x"][0, t * P:(t + 1) * P, :]).then_inc(x_in[t], 16)
            for key, place, width, parts, _ in UNITS:
                if key == ("w_up", 4):
                    squared.wait(sp, ("norm2", TT - 1, 0))
                    sp.dma_start(xn[:, TT:AT, :], inp["ctx_2"].rearrange("a (t p) n -> p (a t) n", p=P)).then_inc(
                        ctx_in, 16)
                for free in UNIT_AFTER[key]:
                    if free[0] == "split":
                        low_ready.wait(sp, SPLIT_AT[free[1]])
                        if free[1][0] in ("w_kvd", "w_xbc"):
                            products(sp, free[1])
                    else:
                        banks.filled(sp, free)
                for c, src in parts:
                    rows, w = src.shape[1], src.shape[2]
                    sp.dma_start(unit_view(place, width, rows)[:, :, c:c + w], src).then_inc(unit_in[place], 16)
            watt.wait(sp, NW // 2 - 1)
            squared.wait(sp, ("mix2", TT - 1, 0))
            load_expert(sp, 0, 0, 0, None)
            banks.filled(sp, ("out2", TT - 1, 1))
            load_expert(sp, 1, 1, 0, None)
            normed.wait(sp, ("norm2_2", TT - 1, 0))
            sp.dma_start(h_d.rearrange("(t p) n -> p t n", p=P), xn[:, 0:TT, :]).then_inc(h_stored, 16)
            route_pe.wait(sp, "halves")
            sp.wait_ge(h_stored, 16)
            sp.wait_ge(expert_in[0], 16)
            sp.dma_start(early_gate, inp["w_gate_2"].rearrange("a e (p j) f -> (a e) p (j f)", j=KT)[2]).then_inc(
                expert_in[0], 16)
            load_expert(sp, 2, 0, 1, 1, (1, 2))
            load_expert(sp, 3, 1, 1, 2)
            with sp.Fori(2, E // 2) as it:
                for par in range(2):
                    load_expert(sp, 2 * it + par, par, it, 2 * it + par - 1)
            route.wait(sp, "table")
            later_n = sp.value_load(ovf[0:1, NOVF:NOVF + 1], min_val=0, max_val=NOVF)
            with sp.If(later_n > 0):
                with sp.Fori(0, later_n) as i:
                    e = sp.value_load(ovf[0:1, bass.ds(i, 1)], min_val=0, max_val=E - 1)
                    load_expert(sp, e, 0, i + E // 2, i + E)
            sp.wait_ge(h_stored, 16)
            sp.dma_start(final_gain, inp["norm_final_2"].partition_broadcast(P)).then_inc(final_in, 16)
            sp.wait_ge(scattered, 1)
            for t in range(TT):
                sp.dma_start(y01[:, t, :, :].rearrange("p k n -> p (k n)"),
                             y_d[4 * t * P:4 * (t + 1) * P, :].rearrange("(p r) n -> p (r n)", r=4)).then_inc(
                                 y01_in[t], 16)
            for t in range(TT):
                final_y.wait(sp, t)
                sp.dma_start(out[0, t * P:(t + 1) * P, :], y01[:, t, 0, :]).then_inc(stored, 16)
            sp.wait_ge(stored, 16 * TT)

        @block.gpsimd
        def _(pool):
            g = nc.gpsimd
            banks.filled(pool, ("proj", len(PROJ) - 1))
            for h in range(H):
                if h >= 4:
                    score_min.wait(pool, NU // 2 + (h // 2 - 2) * 2 * TT + 2 * (TT - 1) + h % 2)
                pool.dma_start(dists[h % 4], dist_d[h]).then_inc(dist_in[h % 4], 16)
            pool.wait_ge(const_in, CONST_ALL)
            pool.wait_ge(more_in, MORE_ALL)
            for t in range(TT):
                kvd_copied.wait(pool, t)
                k = kvd[:, t, 16:144]
                pool_chain.link(pool, rope(g, (rope_k[:, 0, :], rope_k[:, 1, :]), k, 2, t))
                roped_k.tick(g.tensor_tensor(k, rope_k[:, 0, :], rope_k[:, 1, :], ALU.add), t)
                roped_k.wait(pool, t)
            sw_ready.wait(pool, 0)
            u_ready.wait(pool, KT - 1)
            for what, k in weave:
                if what == "state":
                    d, i = STATES[k]
                    t = TILE_AT[d][i]
                    tok_copied.wait(pool, ("xs", t))
                    if k >= 2:
                        banks.filled(pool, ("state", k - 2))
                    ins = g.tensor_tensor(dtxw[:, k % 2, :].rearrange("p (h d) -> p h d", d=HD),
                                          xs_tok[:, t, :].rearrange("p (h d) -> p h d", d=HD),
                                          wide(sm[:, 9, t * 16 + d * 8:t * 16 + d * 8 + 8], HD), ALU.mult)
                    dtxw_ready.tick(ins, k)
                    if i:
                        old = state0[:, d, :] if i == 1 else state[:, d, i - 2, :]
                        state_ready.wait(pool, STATES.index((d, i - 1)))
                        state_decayed.tick(g.tensor_tensor(
                            stmp[:, k % 2, :].rearrange("p (h d) -> p h d", d=HD), old.rearrange("p (h d) -> p h d", d=HD),
                            wide(sm[:, 8, t * 16 + d * 8:t * 16 + d * 8 + 8], HD), ALU.mult), k)
                elif what == "y":
                    if k >= 2:
                        banks.filled(pool, ("ydiag", k - 2))
                    if k < len(YS):
                        t, d = YS[k]
                        ins = g.tensor_tensor(dtx[:, k % 2, :].rearrange("p (h d) -> p h d", d=HD),
                                              xs_tok[:, t, :].rearrange("p (h d) -> p h d", d=HD),
                                              wide(sm[:, 5, t * 16 + d * 8:t * 16 + d * 8 + 8], HD), ALU.mult)
                        dtx_ready.tick(ins, k)
                    if k >= 2 and YS[k - 2][1] == 1:
                        t, row = YS[k - 2][0], cat[:, YS[k - 2][0], 0:512]
                        pool_chain.link(pool, g.tensor_tensor(
                            skip_x.rearrange("p (h d) -> p h d", d=HD), xs_tok[:, t, :].rearrange("p (h d) -> p h d", d=HD),
                            wide(d_skip[:, :], HD), ALU.mult))
                        y_read.wait(pool, (k - 2, "diag"))
                        pool_chain.link(pool, g.tensor_tensor(row, row, skip_x, ALU.add))
                        y_done.tick(g.tensor_tensor(row, row, zs[:, t, :], ALU.mult), t)
            x3.wait(pool, SIDES[-1])
            pool_chain.link(pool, g.memset(xg, 0.0))
            route.wait(pool, "table")
            pool.wait_ge(h_stored, 16)

            def gather(n, e, par, reuse):
                if reuse is not None:
                    pool.wait_ge(xt_filled, reuse)
                g.tensor_copy(tok_at[:, par:par + 1], tok_of[:, bass.ds(e, 1)]).then_inc(index_ready, 1)
                after = held(pool, n + 1)
                pool.wait_ge(const_in, CONST_ALL)
                pool.wait_ge(index_ready, after)
                g.indirect_dma_start(xg[0:BLK, par, :], None, h_d, bass.IndirectOffsetOnAxis(
                    ap=tok_at[0:BLK, par:par + 1], axis=0), bounds_check=T - 1, oob_is_err=False).then_inc(
                        tokens_in[par], 16)

            def scatter(n, e, par, stored_before):
                if stored_before is not None:
                    pool.wait_ge(y_stored[par], stored_before)
                g.tensor_copy(row_at[:, par:par + 1], row_of[:, bass.ds(e, 1)]).then_inc(row_ready, 1)
                after = held(pool, n + 1)
                pool.wait_ge(const_in, CONST_ALL)
                pool.wait_ge(row_ready, after)
                pool.wait_ge(y_ready, after)
                g.indirect_dma_start(y_d, bass.IndirectOffsetOnAxis(ap=row_at[:, par:par + 1], axis=0),
                                     yE[:, par, :], None, bounds_check=4 * T - 1, oob_is_err=False).then_inc(
                                         y_stored[par], 16)

            gather(0, 0, 0, None)
            gather(1, 1, 1, None)
            gather(2, 2, 0, 1)
            gather(3, 3, 1, 2)
            scatter(0, 0, 0, None)
            with pool.Fori(1, E // 2 - 1) as it:
                gather(2 * it + 2, 2 * it + 2, 0, 2 * it + 1)
                pool.wait_ge(y_stored[0], 16 * it)
                scatter(2 * it - 1, 2 * it - 1, 1, None)
                gather(2 * it + 3, 2 * it + 3, 1, 2 * it + 2)
                pool.wait_ge(y_stored[1], 16 * it)
                scatter(2 * it, 2 * it, 0, None)
            scatter(E - 3, E - 3, 1, 16 * (E // 2 - 2))
            scatter(E - 2, E - 2, 0, 16 * (E // 2 - 1))
            scatter(E - 1, E - 1, 1, 16 * (E // 2 - 1))
            pool.wait_ge(y_stored[0], 16 * (E // 2))
            pool.wait_ge(y_stored[1], 16 * (E // 2))
            later_n = pool.value_load(ovf[0:1, NOVF:NOVF + 1], min_val=0, max_val=NOVF)
            with pool.If(later_n > 0):
                with pool.Fori(0, later_n) as i:
                    gather(i + E, i + E, 0, i + E)
                    scatter(i + E, i + E, 0, None)
                    pool.wait_ge(y_stored[0], 16 * i + 16 * (E // 2 + 1))
            g.memset(tok_at[:, 0:1], 0).then_inc(scattered, 1)

        @block.scalar
        def _(act):
            s = nc.scalar
            for dst, src in small_loads[:FIRST_LOADS]:
                act.dma_start(dst, src).then_inc(const_in, 16)
            act.wait_ge(const_in, CONST_ALL)
            eps = C("eps")

            def root(dst, src, width):
                return s.activation(dst, src, ACT.Sqrt, scale=1.0 / width, bias=eps)

            def high_part(*key):
                k = SPLIT_AT[key]
                act.wait_ge(unit_in[UNIT_AT[key][0]], UNIT_AT[key][-1])
                if key in (("w_out", 0), ("w_out", 1)):
                    banks.filled(act, ("modrow", 11))
                elif k >= 2:
                    products(act, SPLITS[k - 2])
                high_ready.tick(s.activation(part_view(w_high, key), raw_view(key), ACT.Copy), k)

            def hidden_high(i):
                hidden.wait(act, 2 * i + 1)
                if i >= 2:
                    products(act, ("w_down", i - 2))
                else:
                    banks.filled(act, ("up", FT - 1, 1))
                hid_high_ready.tick(s.activation(hid_high[:, i % 2, :, :], hid[:, 2 * i:2 * i + 2, :], ACT.Copy), i)

            def norm(name, before=None, between=None):
                norm_tiles(name, before)
                if between is not None:
                    between()
                norm_drains(name)

            def norm_tiles(name, before=None, some=None):
                src, tiles, parts, junk, _ = NORMS[name]
                n = len(parts)
                for t in some or tiles:
                    if before is not None:
                        before(t)
                    for i, (a, b) in enumerate(parts):
                        squared.tick(s.activation(junk[:, a:b], src(t)[:, a:b], ACT.Square,
                                                  accum_out=sums[:, t * n + i:t * n + i + 1]), (name, t, a))
                    squared.wait(act, (name, t, parts[-1][0]))
                    rooted.tick(root(roots[:, t * n:t * n + n], sums[:, t * n:t * n + n], parts[0][1] - parts[0][0]),
                                (name, t))

            def norm_drains(name):
                gain = NORMS[name][-1]
                for k in halves(name):
                    if k[1] % 2 == 0 or name in SPLIT_NORMS:
                        j = k[1]
                        bank = banks.filled(act, ("hT",) + k)
                        dst = hTc[:, j, :] if name == "context" else (hT_high if name in SPLIT_NORMS else hT)[:, j, :]
                        if name == "norm1_2" and j % 2 == 1:
                            if j >= 3:
                                hT_dve.wait(act, (name, j - 2))
                            sc, sh = gain(j)
                            act_chain.link(act, s.activation(conv_g[:, 1, :], bank[:, :], ACT.Identity, scale=sc, bias=sh))
                            hT_act.tick(s.activation(dst, conv_g[:, 1, :], ACT.Copy), k)
                            continue
                        sc, sh = gain(j)
                        hT_act.tick(s.activation(dst, bank[:, 0:dst.shape[1]], ACT.Identity, scale=sc, bias=sh), k)

            s.activation(warm[:, 4:5], eps, ACT.Sqrt)
            norm("norm1", lambda t: act.wait_ge(x_in[t], 16), lambda: high_part("w_in", 0))
            high_part("w_in", 1)
            for dst, src in small_loads[FIRST_LOADS:]:
                act.dma_start(dst, src).then_inc(more_in, 16)
            low, high = C("low"), C("high")
            act.wait_ge(more_in, MORE_ALL)
            for n in range(18):
                if n < 16:
                    c, t = PROJ[n]
                    if t == 0:
                        high_part("w_in", 2 * c + 2)
                    bank = banks.filled(act, ("proj", n))
                    if n >= 3:
                        banks.filled(act, ("qkT", n - 3))
                    if n >= 2:
                        head_summed.wait(act, n - 2)
                    if c == 1:
                        s.activation(vA[:, t, :], bank[:, 128:256], ACT.Copy)
                    if c == 3:
                        s.activation(vB[:, t, 0:256], bank[:, 256:512], ACT.Copy)
                    s.activation(pj[:, n % 3, :], bank[:, :], ACT.Copy)
                    pj_ready.tick(s.activation(sq[:, n % 2, :], bank[:, :], ACT.Square), n)
                    head_summed.wait(act, n)
                    head_rooted.tick(root(head_root[:, n % 2, :], head_sum[:, n % 2, :], HD), n)
                if n >= 2:
                    m = n - 2
                    c, t = PROJ[m]
                    bank = banks.filled(act, ("qkT", m))
                    b3 = bank[:, :].rearrange("p (j n) -> p j n", j=4)
                    at = slice(t * P, t * P + P)
                    if c == 0:
                        ins = s.activation(qaT[:, :, at], b3, ACT.Copy)
                    if c == 1:
                        s.activation(qbT[:, 0:2, at], b3[:, 2:4, :], ACT.Copy)
                        s.activation(kzA[:, 0, at], b3[:, 0, :], ACT.Copy, scale=low)
                        ins = s.activation(kzA[:, 1, at], b3[:, 0, :], ACT.Copy, scale=high)
                    if c == 2:
                        s.activation(qbT[:, 2:4, at], b3[:, 0:2, :], ACT.Copy)
                    if c >= 2:
                        keys = b3[:, 2:4, :] if c == 2 else b3[:, 0:2, :]
                        dst = kzB[:, 4 * (c - 2):4 * (c - 1), at].rearrange("p (j two) n -> p two j n", two=2)
                        s.activation(dst[:, 0, :, :], keys, ACT.Copy, scale=low)
                        ins = s.activation(dst[:, 1, :, :], keys, ACT.Copy, scale=high)
                    qk_drained.tick(ins, m)
                if n < 16 and n % TT == TT - 1:
                    high_part("w_in", 2 * (n // TT) + 3)
            csilu_cleared.wait(act, 0)
            s.activation(csilu[:, :, 0], cvec[:, 0, :], ACT.Silu)
            mod_silu.tick(s.activation(csilu[:, :, 1], cvec[:, 1, :], ACT.Silu), "c")
            def mixed(t):
                att.wait(act, NU // 2 - TT + t)

            for i in range(NU + 4):
                if i < NU:
                    score_min.wait(act, i)
                    if i >= 3:
                        banks.filled(act, ("probsT", i - 3))
                    src = banks.filled(act, ("score", i))[:, :] if i < NU // 2 else probs[:, i % 3, :]
                    prob.tick(s.activation(probs[:, i % 3, :], src, ACT.Exp, scale=-1.0, bias=nmin[:, i:i + 1],
                                           accum_out=psums[:, i:i + 1]), i)
                n = i - 1
                if 0 <= n < NU and n % 2 == 0:
                    bank = banks.filled(act, ("probsT", n))
                    if n >= 4:
                        banks.filled(act, ("att", n // 2 - 2))
                    pt_act.tick(s.activation(probsT[:, n % 4, :], bank[:, :], ACT.Copy), n)
                if i >= 4 and i % 2 == 0:
                    p = i // 2 - 2
                    bank = banks.filled(act, ("att", p))
                    if p >= 2:
                        banks.filled(act, ("attT", p - 2))
                    att_copied.tick(s.activation(attT[:, p % 2, :], bank[:, 0:P], ACT.Copy), p)
                if i % 5 == 2 and i // 5 < 12:
                    m = i // 5
                    bank = banks.filled(act, ("modrow", m))
                    if m >= 2:
                        mod_done.wait(act, m - 2)
                    mod_copied.tick(s.activation(modrow[:, m % 2, :], bank[:, :], ACT.Copy), m)
                if i in (NU - 6, NU - 4):
                    high_part("w_out", (i - NU + 6) // 2)
                t = mixed_at(i)
                if t is not None:
                    norm_tiles("mix1", mixed, [t])
            norm_tiles("mix1", mixed, [TT - 1])
            norm_drains("mix1")
            for i in range(2, KT // 2):
                high_part("w_out", i)
            s.activation(warm[:, 0:1], eps, ACT.Sqrt)
            norm("norm2", lambda t: x1.wait(act, (t, 1)), lambda: high_part("w_up", 0))
            for f in range(FT + 1):
                if f < FT:
                    high_part(*SPLITS[SPLIT_AT["w_up", f] + 1])
                    if f == FT // 2:
                        norm_tiles("context", lambda t: act.wait_ge(ctx_in, 16))
                    for gv in range(2):
                        bank = banks.filled(act, ("up", f, gv))
                        if f >= 2:
                            hidden.wait(act, f - 2)
                        ch = gv * FT + f
                        tap_mid.tick(s.activation((conv_g, conv_v)[gv][:, f % 2, :], bank[:, :], ACT.Identity,
                                                  scale=convw[:, 44 + ch:45 + ch], bias=convw[:, 132 + ch:133 + ch]),
                                     (f, gv))
                if f >= 1:
                    tapped.wait(act, (f - 1, 1))
                    y = conv_g[:, (f - 1) % 2, :]
                    gelued.tick(s.activation(y, y, ACT.Gelu_apprx_tanh), f - 1)
            hidden_high(0)
            mod_done.wait(act, "gains")
            norm_drains("context")
            high_part("w_down", 1)
            hidden_high(1)
            for i in range(2, ND):
                high_part("w_down", i)
                hidden_high(i)
            high_part("w_kvd", 0)
            s.activation(warm[:, 1:2], eps, ACT.Sqrt)
            norm("norm1_2", lambda t: x2.wait(act, (t, 1)), lambda: high_part("w_kvd", 1))
            high_part("w_zq", 0)
            high_part("w_zq", 1)
            dt_abs.wait(act, 0)
            dt_exp.tick(s.activation(sm[:, 1, :], sm[:, 4, :], ACT.Exp, scale=-1.0), 0)
            a_exp.tick(s.activation(a_log[:, :], a_log[:, :], ACT.Exp), 0)
            high_part("w_zq", 2)
            dt_abs.wait(act, 1)
            dt_log.tick(s.activation(sm[:, 3, :], sm[:, 2, :], ACT.Ln), 0)
            high_part("w_zq", 3)
            high_part("w_xbc", 0)
            for t in range(TT):
                bank = banks.filled(act, ("q2", t))
                q_copied.tick(s.activation(q2[:, t, :], bank[:, :], ACT.Copy, scale=-HD ** -0.5), t)
            for t in range(TT):
                bank = banks.filled(act, ("z", t))
                z_ready.tick(s.activation(zs[:, t, :], bank[:, :], ACT.Silu), t)
            cs_copied.wait(act, 0)
            s.activation(sm[:, 0, :], sm[:, 7, :], ACT.Exp)
            s.activation(sm[:, 1, :], sm[:, 1, :], ACT.Exp)
            cs_exp.tick(s.activation(sm[:, 8, :], sm[:, 2, :], ACT.Exp), 0)
            for m in range(KT + 1):
                if m % 2 == 0 and m < KT - 2:
                    high_part("w_xbc", m // 2 + 1)
                if m < KT:
                    for c in range(2):
                        bank = banks.filled(act, ("xbc", m, c))
                        n, o = (CTX, T) if c else (T, 0)
                        if m >= 2:
                            u_ready.wait(act, m - 2)
                        mid2.tick(s.activation(conv2[:, m % 2, o:o + n], bank[:, 0:n], ACT.Identity,
                                               scale=convw[:, 192 + m:193 + m], bias=convw[:, 216 + m:217 + m]), (m, c))
                if m >= 1:
                    tapped2.wait(act, (m - 1, 1))
                    u_ready.tick(s.activation(u[:, m - 1, :], conv2[:, (m - 1) % 2, :], ACT.Silu), m - 1)
            for t in range(AT):
                bank = banks.filled(act, ("xs", t))
                tok_copied.tick(s.activation(xs_tok[:, t, :], bank[:, :], ACT.Copy), ("xs", t))
            for t in range(0, AT, 2):
                bank = banks.filled(act, ("b", t))
                tok_copied.tick(s.activation(b_tok[:, t:t + 2, :], bank[:, :].rearrange("p (t n) -> p t n", t=2),
                                             ACT.Copy), ("b", t))
            for n in range(2):
                bank = banks.filled(act, ("kT", n))
                w, o = (CTX, T) if n else (T, 0)
                s.activation(kz2[:, 0, o:o + w], bank[:, 0:w], ACT.Copy, scale=low)
                kz_ready.tick(s.activation(kz2[:, 1, o:o + w], bank[:, 0:w], ACT.Copy, scale=high), n)
            for j in range(4):
                bank = banks.filled(act, ("q2T", j))
                q2_ready.tick(s.activation(q2T[:, j, :], bank[:, :], ACT.Copy), j)
            segments = []
            for what, i in weave:
                if what == "win":
                    if i < NW:
                        h, t = window_of(i)
                        lo, hi = near(t)
                        n = (hi - lo + 1) * P + CTX
                        wscore.wait(act, i)
                        row = wprobs[:, i % 3, 0:n]
                        s.activation(row, row, ACT.Exp, scale=-1.0, bias=nmin[:, i:i + 1], accum_out=psums[:, i:i + 1])
                        wprob.tick(s.activation(sink_exp[:, i:i + 1], sinks[:, h:h + 1], ACT.Exp,
                                                bias=nmin[:, i:i + 1]), i)
                    if 2 <= i <= NW + 1:
                        m = i - 2
                        lo, hi = near(window_of(m)[1])
                        n = (hi - lo + 1) * P
                        near_b, far_b = (banks.filled(act, ("wprobsT", m, k)) for k in range(2))
                        if m >= 3:
                            banks.filled(act, ("watt", (m - 3) // 2))
                        s.activation(wprobsT[:, m % 3, 0:n], near_b[:, 0:n], ACT.Copy)
                        wpt_act.tick(s.activation(wprobsT[:, m % 3, n:n + CTX], far_b[:, 0:CTX], ACT.Copy), m)
                    if i >= 4 and i % 2 == 0:
                        p = i // 2 - 2
                        bank = banks.filled(act, ("watt", p))
                        if p >= 2:
                            banks.filled(act, ("wattT", p - 2))
                        watt_copied.tick(s.activation(wattT[:, p % 2, :], bank[:, 0:P], ACT.Copy), p)
                    for k in segments:
                        seg_ready.wait(act, (k, 1))
                        decayed.tick(s.activation(decay[:, k % 3, :, :], decay[:, k % 3, :, :], ACT.Exp), k)
                    segments = []
                elif what == "y" and i < len(YS):
                    segments.append(i)

            def mixed2(t):
                y_done.wait(act, t)

            s.activation(warm[:, 2:3], eps, ACT.Sqrt)
            norm_tiles("mix2", mixed2)
            watt.wait(act, NW // 2 - 1)
            high_part("w_out2", 0)
            norm_drains("mix2")
            for i in range(1, KT // 2):
                high_part("w_out2", i)
            norm("norm2_2", lambda t: x3.wait(act, (t, 1)))
            route_pe.wait(act, "halves")
            route.wait(act, "cleared")
            route_act.tick(s.activation(lgT[0:36, :], ps[0][0:36, :], ACT.Copy), "even")
            route.wait(act, "max")
            for t in range(TT):
                last = s.activation(gexp[:, t, :], gl[:, t, 0:4], ACT.Exp, bias=g8[:, t, 0:1],
                                    accum_out=gsum[:, t:t + 1])
            route_act.tick(last, "group_exp")
            route.wait(act, "top2")
            route_act.tick(s.activation(wts[:, :, 3], wts[:, :, 2], ACT.Exp), "pair_exp")
            s.activation(warm[:, 3:4], eps, ACT.Silu)

            def expert(n, par, kpar, reuse):
                gate_up, hiddenT = ps[2 + par], ps[4 + par]
                act.wait_ge(gu_filled, n + 1)
                if reuse is not None:
                    act.wait_ge(ht_filled, reuse)
                s.activation(gu[:, par, :], gate_up[:, :], ACT.Copy).then_inc(gu_ready, 1)
                act.wait_ge(ht_filled, n + 1)
                if reuse is not None:
                    act.wait_ge(hid_ready, reuse)
                s.activation(sg[:, par, :, :], hiddenT[:, :].rearrange("p (f n) -> p f n", f=4)[:, :, 0:BLK],
                             ACT.Silu).then_inc(silu_ready, 1)

            expert(0, 0, 0, None)
            expert(1, 1, 0, None)
            with act.Fori(1, E // 2) as it:
                for par in range(2):
                    expert(2 * it + par, par, it, 2 * it + par - 1)
            later_n = act.value_load(ovf[0:1, NOVF:NOVF + 1], min_val=0, max_val=NOVF)
            with act.If(later_n > 0):
                with act.Fori(0, later_n) as i:
                    expert(i + E, 0, i + E // 2, i + E)
            s.activation(warm[:, 5:6], eps, ACT.Sqrt)
            for t in range(TT):
                final_x.wait(act, t)
                squared.tick(s.activation(junk3, x[:, t, :], ACT.Square, accum_out=sums[:, t:t + 1]), ("final", t, 0))
                squared.wait(act, ("final", t, 0))
                rooted.tick(root(roots[:, t:t + 1], sums[:, t:t + 1], D), ("final", t))

        @block.tensor
        def _(pe):
            def mm(o, lhsT, rhs, start, stop):
                return nc.tensor.matmul(o, lhsT, rhs, start=start, stop=stop)

            def tr(o, i, n=P):
                return nc.tensor.transpose(o, i, ident[0:n, 0:n])

            def norm(name):
                _, tiles, parts, _, _ = NORMS[name]
                opened = [banks.open(pe, ("hT",) + k) for k in halves(name)]
                for i, t in enumerate(tiles):
                    normed.wait(pe, (name, t, parts[-1][0]))
                    for k in halves(name):
                        j = k[1]
                        last = tr(opened[j][:, i * P:(i + 1) * P],
                                  xn[:, t, :].rearrange("p (q j) -> p j q", j=KT)[:, j, :])
                        if t == tiles[-1]:
                            banks.close(last, ("hT",) + k)

            def hT_row(name, j):
                hT_step((name, j)).wait(pe, (name, j))

            def pairs(a_high, a_low, b_high, b_low):
                return (a_high, b_high), (a_high, b_low), (a_low, b_high)

            pe.wait_ge(const_in, CONST_ALL)
            norm("norm1")

            def heads_transposed(n):
                if 0 <= n < 16:
                    bank = banks.open(pe, ("qkT", n))
                    qk_ready.wait(pe, n)
                    for j in range(4):
                        last = tr(bank[:, j * P:(j + 1) * P], pj[:, n % 3, j * P:(j + 1) * P])
                    banks.close(last, ("qkT", n))

            for c in range(5):
                opened = [banks.open(pe, ("proj", 4 * c + t)) for t in range(TT)]
                for half in range(2):
                    key = ("w_in", 2 * c + half)
                    low_ready.wait(pe, SPLIT_AT[key])
                    wh, wl = part_view(w_high, key), part_view(w_low, key)
                    for t in range(TT):
                        ts = slice(t * P, t * P + P)
                        for r in range(4):
                            j = 4 * half + r
                            if c == t == 0:
                                hT_row("norm1", j)
                            for n, (a, b) in enumerate(pairs(hT_high[:, j, ts], low_row("norm1", j)[:, ts], wh[:, r, :],
                                                             wl[:, r, :])):
                                last = mm(opened[t][:, 0:wh.shape[2]], a, b, j == n == 0, j == KT - 1 and n == 2)
                        if half:
                            banks.close(last, ("proj", 4 * c + t))
                        elif t == TT - 1:
                            grown.tick(last, key)
                        if half == 0 and t % 2 == 1:
                            heads_transposed(4 * c - 2 + t // 2)
                        if half == 1 and t >= 2:
                            heads_transposed(4 * c + t - 2)
            pe.wait_ge(more_in, MORE_ALL)
            bank = banks.open(pe, "conv_weights")
            tr(bank[:, 0:88], conv_rows[0:88, 0, :], 88)
            tr(bank[:, 88:176], conv_rows[0:88, 1, :], 88)
            banks.close(tr(bank[:, 176:224], conv_rows[0:48, 2, :], 48), "conv_weights")
            qk_drained.wait(pe, 15)
            v_tail.wait(pe, TT - 1)
            mod_silu.wait(pe, "c")
            for i in range(NU + 4):
                if i < NU:
                    m, h, t = unit_of(i)
                    bank = banks.open(pe, ("score", i))
                    at = slice(t * P, t * P + P)
                    q, k = (qbT[:, h // 2, at], kzB[:, h, :]) if m else (qaT[:, h % 4, at], kzA[:, h // 4, :])
                    banks.close(mm(bank[:, :], q, k, True, True), ("score", i))
                if 1 <= i <= NU:
                    bank = banks.open(pe, ("probsT", i - 1))
                    prob.wait(pe, i - 1)
                    for k in range(TT):
                        last = tr(bank[:, k * P:(k + 1) * P], probs[:, (i - 1) % 3, k * P:(k + 1) * P])
                    banks.close(last, ("probsT", i - 1))
                p = i // 2 - 2
                if i >= 4 and i % 2 == 0:
                    bank = banks.open(pe, ("att", p))
                    for n in (2 * p, 2 * p + 1):
                        pt_step(n).wait(pe, n)
                    for k in range(TT):
                        for n in (2 * p, 2 * p + 1):
                            m, h, _ = unit_of(n)
                            v = vB[:, k, h * HD:(h + 1) * HD] if m else vA[:, k, (h // 4) * HD:(h // 4 + 1) * HD]
                            half = HD * (n % 2)
                            last = mm(bank[half:half + HD, 0:P], v, probsT[:, n % 4, k * P:(k + 1) * P], k == 0,
                                      k == TT - 1)
                    banks.close(last, ("att", p))
                if i >= 5 and i % 2 == 1:
                    bank = banks.open(pe, ("attT", p))
                    att_copied.wait(pe, p)
                    banks.close(tr(bank[:, 0:P], attT[:, p % 2, :]), ("attT", p))
                if i % 5 == 2 and i // 5 < 12:
                    m = i // 5
                    w = weights(pe, ("w_ada", m))
                    bank = banks.open(pe, ("modrow", m))
                    for j in range(KT):
                        quarter = bank[32 * (j % 4):32 * (j % 4) + 32, :]
                        last = mm(quarter, csilu[:, j, :], w[:, j, :], j < 4, j >= 4)
                    banks.close(last, ("modrow", m))
                if i % 5 == 4 and i // 5 < 12:
                    m = i // 5
                    mod_copied.wait(pe, m)
                    bank = banks.open(pe, ("mod", m))
                    if m // 2 in (2, 5):
                        last = mm(bank[:, :], C("sum_two")[:, 0:1].broadcast_to([P, P]), modrow[:, m % 2, :], True, True)
                    else:
                        for j in range(KT):
                            last = mm(bank[64 * (m % 2):64 * (m % 2) + 64, 2 * j:2 * j + 2],
                                      modrow[:, m % 2, :].rearrange("p (q j) -> p j q", j=KT)[:, j, :], C("sum_two"),
                                      True, True)
                    banks.close(last, ("mod", m))

            def grow(name, outputs, rows_of, before=None, fresh=None):
                many = GROWN[name][0]
                opened = []
                for i in range(many):
                    key = (name, i)
                    low_ready.wait(pe, SPLIT_AT[key])
                    if before is not None:
                        before(i)
                    wh, wl = part_view(w_high, key), part_view(w_low, key)
                    raw = raw_view(key)
                    rows = rows_of(i)
                    if fresh is not None:
                        for j in rows:
                            hT_row(fresh, j)
                    for o, (out_key, (a, b), lhs) in enumerate(outputs):
                        if i == 0:
                            opened.append(banks.open(pe, out_key))
                        bank = opened[o]
                        for r, j in enumerate(rows):
                            left = lhs(i, j)
                            terms = [(left[0], raw[:, r, a:b])] if len(left) == 1 else pairs(
                                left[0], left[1], wh[:, r, a:b], wl[:, r, a:b])
                            for n, (u_, w_) in enumerate(terms):
                                last = mm(bank[:, 0:b - a], u_, w_, i == r == n == 0,
                                          i == many - 1 and r == len(rows) - 1 and n == len(terms) - 1)
                        if i == many - 1:
                            banks.close(last, out_key)
                    if i < many - 1:
                        grown.tick(last, key)

            def token_parts(t):
                ts = slice(t * P, t * P + P)
                return lambda i, j: (hT_high[:, j, ts], hT_low[:, j, ts])

            def two_rows(i):
                return range(2 * i, 2 * i + 2)

            def sides(key, lhs=token_parts):
                return [((key, t, n), (n * 512, n * 512 + 512), lhs(t)) for t, n in SIDES]

            norm("mix1")
            grow("w_out", sides("out1"), two_rows, fresh="mix1")
            norm("norm2")
            for f in range(FT):
                low_ready.wait(pe, SPLIT_AT["w_up", f])
                wh, wl = (part_view(part, ("w_up", f)) for part in (w_high, w_low))
                for gv in range(2):
                    bank = banks.open(pe, ("up", f, gv))
                    cs = slice(gv * P, gv * P + P)
                    for j in range(KT):
                        if f == gv == 0:
                            hT_row("norm2", j)
                        for n, (a, b) in enumerate(pairs(wh[:, j, cs], wl[:, j, cs], hT_high[:, j, :], hT_low[:, j, :])):
                            last = mm(bank[:, :], a, b, j == n == 0, j == KT - 1 and n == 2)
                    banks.close(last, ("up", f, gv))
            norm("context")
            def hidden_parts(t):
                ts = slice(t * P, t * P + P)
                return lambda i, f: (hid_high[:, i % 2, f % 2, ts], hid_low[:, i % 2, f % 2, ts])

            grow("w_down", sides("down", hidden_parts), two_rows, lambda i: hid_low_ready.wait(pe, i))
            norm("norm1_2")

            def context(t):
                return lambda i, j: (hTc[:, j, t * P:(t + 1) * P],)

            grow("w_kvd", [(("kvd", t), (0, 272), token_parts(t) if t < TT else context(t - TT)) for t in range(AT)],
                 lambda i: range(4 * i, 4 * i + 4), fresh="norm1_2")
            grow("w_zq", [((name, t), (a, a + 512), token_parts(t)) for name, a in (("q2", 512), ("z", 0)) for t in range(TT)],
                 two_rows)
            dta_ready.wait(pe, 0)
            bank = banks.open(pe, "cumsum")
            dta = sm[:, 6, :].rearrange("p (t d h) -> p t d h", t=AT, d=2)
            b4 = bank[:, 0:96].rearrange("p (t d h) -> p t d h", t=AT, d=2)
            mm(b4[:, :, 0, :], C("upto"), dta[:, :, 0, :], True, True)
            mm(b4[:, :, 1, :], C("from"), dta[:, :, 1, :], True, True)
            banks.close(mm(bank[:, 96:192], C("one").broadcast_to([P, P]), sm[:, 6, :], True, True), "cumsum")
            for m, c in XBC:
                key, cs = ("w_xbc", m // 2), slice((m % 2) * P, (m % 2) * P + P)
                low_ready.wait(pe, SPLIT_AT[key])
                bank = banks.open(pe, ("xbc", m, c))
                for j in range(KT):
                    if c:
                        last = mm(bank[:, 0:CTX], raw_view(key)[:, j, cs], hTc[:, j, :], j == 0, j == KT - 1)
                        continue
                    for n, (a, b) in enumerate(pairs(part_view(w_high, key)[:, j, cs], part_view(w_low, key)[:, j, cs],
                                                     hT_high[:, j, :], hT_low[:, j, :])):
                        last = mm(bank[:, :], a, b, j == n == 0, j == KT - 1 and n == 2)
                banks.close(last, ("xbc", m, c))
            u_ready.wait(pe, KT - 1)
            roped_q.wait(pe, TT - 1)
            roped_k.wait(pe, TT - 1)
            for t in range(AT):
                bank = banks.open(pe, ("xs", t))
                for m in range(4):
                    last = tr(bank[:, m * P:(m + 1) * P], u[:, m, t * P:(t + 1) * P])
                banks.close(last, ("xs", t))
            for t in range(0, AT, 2):
                bank = banks.open(pe, ("b", t))
                for i in range(2):
                    for m in range(2):
                        o = i * 256 + m * P
                        last = tr(bank[:, o:o + P], u[:, 4 + m, (t + i) * P:(t + i + 1) * P])
                banks.close(last, ("b", t))
            for n in range(2):
                bank = banks.open(pe, ("kT", n))
                if n == 0:
                    roped_k.wait(pe, TT - 1)
                else:
                    kvd_copied.wait(pe, AT - 1)
                for i in range(CT if n else TT):
                    last = tr(bank[:, i * P:(i + 1) * P], kvd[:, n * TT + i, 16:144])
                banks.close(last, ("kT", n))
            for j in range(4):
                bank = banks.open(pe, ("q2T", j))
                roped_q.wait(pe, TT - 1)
                for t in range(TT):
                    last = tr(bank[:, t * P:(t + 1) * P], q2[:, t, j * P:(j + 1) * P])
                banks.close(last, ("q2T", j))
            tok_copied.wait(pe, ("b", AT - 2))
            kz_ready.wait(pe, 1)
            q2_ready.wait(pe, 3)
            for what, i in weave:
                if what == "win":
                    if i < NW:
                        h, t = window_of(i)
                        lo, hi = near(t)
                        q = q2T[:, h % 4, t * P:(t + 1) * P]
                        k = kz2[:, h // 4, :]
                        bank = banks.open(pe, ("wscore", i, 0))
                        banks.close(mm(bank[:, 0:(hi - lo + 1) * P], q, k[:, lo * P:(hi + 1) * P], True, True),
                                    ("wscore", i, 0))
                        bank = banks.open(pe, ("wscore", i, 1))
                        banks.close(mm(bank[:, 0:CTX], q, k[:, T:T + CTX], True, True), ("wscore", i, 1))
                    if 2 <= i <= NW + 1:
                        m = i - 2
                        lo, hi = near(window_of(m)[1])
                        n = hi - lo + 1
                        wprob.wait(pe, m)
                        for part, (a, many) in enumerate(((0, n), (n, CT))):
                            bank = banks.open(pe, ("wprobsT", m, part))
                            for k in range(many):
                                last = tr(bank[:, k * P:(k + 1) * P], wprobs[:, m % 3, (a + k) * P:(a + k + 1) * P])
                            banks.close(last, ("wprobsT", m, part))
                    p = i // 2 - 2
                    if i >= 4 and i % 2 == 0:
                        h, t = window_of(2 * p)
                        lo, hi = near(t)
                        seen = list(range(lo, hi + 1)) + list(range(TT, AT))
                        bank = banks.open(pe, ("watt", p))
                        wpt_act.wait(pe, 2 * p + 1)
                        for n, kt in enumerate(seen):
                            v = kvd[:, kt, 144 + (h // 4) * HD:144 + (h // 4 + 1) * HD]
                            for half in range(2):
                                last = mm(bank[half * HD:(half + 1) * HD, 0:P], v,
                                          wprobsT[:, (2 * p + half) % 3, n * P:(n + 1) * P], n == 0, n == len(seen) - 1)
                        banks.close(last, ("watt", p))
                    if i >= 5 and i % 2 == 1:
                        bank = banks.open(pe, ("wattT", p))
                        watt_copied.wait(pe, p)
                        banks.close(tr(bank[:, 0:P], wattT[:, p % 2, :]), ("wattT", p))
                elif what == "state":
                    d, pos = STATES[i]
                    t = TILE_AT[d][pos]
                    bank = banks.open(pe, ("state", i))
                    dtxw_ready.wait(pe, i)
                    for g in range(2):
                        last = mm(bank[:, g * 256:(g + 1) * 256], b_tok[:, t, g * P:(g + 1) * P],
                                  dtxw[:, i % 2, g * 256:(g + 1) * 256], True, True)
                    banks.close(last, ("state", i))
                else:
                    if i < len(YS):
                        t, d = YS[i]
                        if d == 0:
                            bank = banks.open(pe, ("cb", t))
                            for g in range(2):
                                last = mm(bank[:, g * P:(g + 1) * P], u[:, 4 + g, t * P:(t + 1) * P],
                                          u[:, 6 + g, t * P:(t + 1) * P], True, True)
                            banks.close(last, ("cb", t))
                        for g in range(2):
                            bank = banks.open(pe, ("seg", i, g))
                            for h in range(4):
                                a = t * 16 + d * 8 + g * 4 + h
                                last = mm(bank[:, h * P:(h + 1) * P], sm[:, 6, a:a + 1].broadcast_to([P, P]),
                                          C("from" if d else "upto"), True, True)
                            banks.close(last, ("seg", i, g))
                    if i >= 2:
                        k = i - 2
                        t, d = YS[k]
                        pos = TILE_AT[d].index(t) - 1
                        bank = banks.open(pe, ("yoff", k))
                        state_ready.wait(pe, STATES.index((d, pos)))
                        for g in range(2):
                            last = mm(bank[:, g * 256:(g + 1) * 256], u[:, 6 + g, t * P:(t + 1) * P],
                                      state[:, d, pos - 1, g * 256:(g + 1) * 256], True, True)
                        banks.close(last, ("yoff", k))
                        bank = banks.open(pe, ("ydiag", k))
                        m_ready.wait(pe, k)
                        dtx_ready.wait(pe, k)
                        for h in range(H):
                            last = mm(bank[:, h * HD:(h + 1) * HD], decay[:, k % 3, h, :],
                                      dtx[:, k % 2, h * HD:(h + 1) * HD], True, True)
                        banks.close(last, ("ydiag", k))
            norm("mix2")
            grow("w_out2", sides("out2"), two_rows, fresh="mix2")
            norm("norm2_2")
            for n, (steps_, step) in enumerate(g_[1] for g_ in banks.order[-8:]):
                steps_.wait(pe, step)
            for j in range(KT):
                row = 64 * (j % 2)
                hT_row("norm2_2", j)
                last = mm(ps[0][row:row + 36, :], route_w[:, j, :], hT[:, j, :], j < 2, j >= KT - 2)
            route_pe.tick(last, "halves")
            route_act.wait(pe, "even")
            route.wait(pe, "odd")
            for t in range(TT):
                last = mm(ps[1][:, t * 36:(t + 1) * 36], lgT[:, t * P:(t + 1) * P], C("both_halves"), True, True)
            route_pe.tick(last, "logits")
            route.wait(pe, "hot")
            hot = osum.rearrange("p t e -> p (t e)")
            mm(ps[2][:, 0:TT * E], C("before"), hot, True, True)
            route_pe.tick(mm(ps[2][:, TT * E:2 * TT * E], C("one").broadcast_to([P, P]), hot, True, True), "rank")
            route.wait(pe, "places")
            for n in range(8):
                last = mm(ps[3][:, 0:2 * NBLK], hot_p[:, n, :], hot_b[:, n, :, :].rearrange("p a b -> p (a b)"), n == 0,
                          n == 7)
            route_pe.tick(last, "table")
            route.wait(pe, "table")

            def tokens_in_place(n, par, kpar, reuse):
                xt = ps[par]
                loads, free = held(pe, 16 * kpar + 16), held(pe, reuse) if reuse is not None else None
                pe.wait_ge(const_in, CONST_ALL)
                pe.wait_ge(tokens_in[par], loads)
                if reuse is not None:
                    pe.wait_ge(xt_ready, free)
                for j in range(KT):
                    last = tr(xt[:, j * BLK:(j + 1) * BLK],
                              xg[0:BLK, par, :].rearrange("p (q j) -> p j q", j=KT)[:, j, :], BLK)
                last.then_inc(xt_filled, 1)

            def expert(n, par, kpar, reuse, following=None, gate=None):
                gate_up, hiddenT, y = ps[2 + par], ps[4 + par], ps[6 + par]
                gate_w, up_w, down_w = (EXPERT_SLOTS[3 * par + i] for i in range(3))
                gate_w = gate_w if gate is None else gate
                pe.wait_ge(xt_ready, n + 1)
                pe.wait_ge(expert_in[3 * par], 16 * kpar + 16)
                pe.wait_ge(expert_in[3 * par + 1], 16 * kpar + 16)
                if reuse is not None:
                    pe.wait_ge(gu_ready, reuse)
                for j in range(KT):
                    for half, w in enumerate((gate_w, up_w)):
                        last = mm(gate_up[half * BLK:(half + 1) * BLK, :], xT[:, par, j, :], w[:, j * EF:(j + 1) * EF],
                                  j == 0, j == KT - 1)
                last.then_inc(gu_filled, 1)
                if following is not None:
                    tokens_in_place(*following)
                pe.wait_ge(gu_ready, n + 1)
                if reuse is not None:
                    pe.wait_ge(hid_ready, reuse)
                for f in range(4):
                    last = tr(hiddenT[:, f * P:(f + 1) * P], gu[:, par, :].rearrange("p (q f) -> p f q", f=4)[:, f, :])
                last.then_inc(ht_filled, 1)
                pe.wait_ge(hid_ready, n + 1)
                pe.wait_ge(expert_in[3 * par + 2], 16 * kpar + 16)
                if reuse is not None:
                    pe.wait_ge(y_ready, reuse)
                for f in range(4):
                    for half in range(2):
                        last = mm(y[half * BLK:(half + 1) * BLK, :], hidE[:, par, f, :],
                                  down_w[:, f * D + half * 512:f * D + half * 512 + 512], f == 0, f == 3)
                last.then_inc(y_filled, 1)

            tokens_in_place(0, 0, 0, None)
            expert(0, 0, 0, None, (1, 1, 0, None))
            expert(1, 1, 0, None, (2, 0, 1, 1))
            expert(2, 0, 1, 1, (3, 1, 1, 2), early_gate)
            expert(3, 1, 1, 2, (4, 0, 2, 3))
            with pe.Fori(2, E // 2 - 1) as it:
                for par in range(2):
                    n = 2 * it + par
                    expert(n, par, it, n - 1, (n + 1, 1 - par, it + par, n))
            expert(E - 2, 0, E // 2 - 1, E - 3, (E - 1, 1, E // 2 - 1, E - 2))
            expert(E - 1, 1, E // 2 - 1, E - 2)
            later_n = pe.value_load(ovf[0:1, NOVF:NOVF + 1], min_val=0, max_val=NOVF)
            with pe.If(later_n > 0):
                with pe.Fori(0, later_n) as i:
                    tokens_in_place(i + E, 0, i + E // 2, i + E)
                    expert(i + E, 0, i + E // 2, i + E)

        @block.vector
        def _(dve):
            v = nc.vector

            def link(ins):
                dve_chain.link(dve, ins)

            def low_part(*key):
                k = SPLIT_AT[key]
                high_ready.wait(dve, k)
                low_ready.tick(v.tensor_tensor(part_view(w_low, key), raw_view(key), part_view(w_high, key), ALU.subtract), k)

            def hidden_low(i):
                hid_high_ready.wait(dve, i)
                hid_low_ready.tick(v.tensor_tensor(hid_low[:, i % 2, :, :], hid[:, 2 * i:2 * i + 2, :],
                                                   hid_high[:, i % 2, :, :], ALU.subtract), i)

            def norm(name, between=None):
                norm_tiles(name)
                if between is not None:
                    between()
                norm_drains(name)

            def norm_tiles(name, some=None):
                src, tiles, parts, _, _ = NORMS[name]
                n = len(parts)
                for t in some or tiles:
                    rooted.wait(dve, (name, t))
                    link(v.reciprocal(rstd[:, t * n:t * n + n], roots[:, t * n:t * n + n]))
                    for i, (a, b) in enumerate(parts):
                        normed.tick(v.tensor_scalar(xn[:, t, a:b], src(t)[:, a:b], rstd[:, t * n + i:t * n + i + 1], None,
                                                    ALU.mult), (name, t, a))

            def norm_drains(name):
                gain = NORMS[name][-1]
                for k in halves(name):
                    if name in SPLIT_NORMS:
                        j = k[1]
                        bank = banks.filled(dve, ("hT",) + k)
                        hT_act.wait(dve, k)
                        sc, sh = gain(j)
                        if name == "norm1_2":
                            if j >= 2:
                                hT_dve.wait(dve, (name, j - 2))
                            if j % 2 == 0:
                                link(v.tensor_scalar(conv_g[:, 0, :], bank[:, :], sc, sh, ALU.mult, ALU.add))
                            ins = v.tensor_tensor(hT_low[:, j, :], conv_g[:, j % 2, :], hT_high[:, j, :], ALU.subtract)
                        else:
                            ins = v.scalar_tensor_tensor(low_row(name, j), bank[:, :], sc, hT_high[:, j, :], ALU.mult,
                                                         ALU.subtract)
                        hT_dve.tick(ins, k)
                    elif k[1] % 2 == 1:
                        j = k[1]
                        bank = banks.filled(dve, ("hT",) + k)
                        dst = hTc[:, j, :] if name == "context" else hT[:, j, :]
                        sc, sh = gain(j)
                        hT_dve.tick(v.tensor_scalar(dst, bank[:, 0:dst.shape[1]], sc, sh, ALU.mult, ALU.add), k)

            csilu_cleared.tick(v.memset(csilu[:, :, :], 0.0), 0)
            dve.wait_ge(const_in, CONST_ALL)
            v.memset(gains[64:128, 4, :], 1.0)
            norm("norm1", lambda: low_part("w_in", 0))
            low_part("w_in", 1)
            dve.wait_ge(more_in, MORE_ALL)
            for n in (0, 2):
                link(v.tensor_scalar(head_gain[:, n, :], head_gain[:, n, :], -HD ** -0.5, None, ALU.mult))
            for n in range(20):
                if n >= 4 and n % TT == 0:
                    low_part("w_in", 2 * (n // TT) + 1)
                if n >= 16:
                    bank = banks.filled(dve, ("proj", n))
                    v_tail.tick(v.tensor_copy(vB[:, n - 16, 256:512], bank[:, 0:256]), n - 16)
                    continue
                c, t = PROJ[n]
                if t == 0:
                    low_part("w_in", 2 * c + 2)
                pj_ready.wait(dve, n)
                if n >= 2:
                    head_rooted.wait(dve, n - 2)
                head_summed.tick(v.tensor_reduce(head_sum[:, n % 2, :], sq[:, n % 2, :].rearrange(
                    "p (h d) -> p h d", d=HD), AXX, ALU.add), n)
                head_rooted.wait(dve, n)
                link(v.reciprocal(head_sum[:, n % 2, :], head_root[:, n % 2, :]))
                row = pj[:, n % 3, :].rearrange("p (h d) -> p h d", d=HD)
                for a, many, gain in HEADS_OF[c]:
                    seg = row[:, a:a + many, :]
                    last = v.tensor_tensor(seg, seg, wide(head_sum[:, n % 2, a:a + many], HD), ALU.mult)
                link(last)
                for a, many, gain in HEADS_OF[c]:
                    seg = row[:, a:a + many, :]
                    last = v.tensor_tensor(seg, seg, head_gain[:, gain, :].unsqueeze(1).broadcast_to([P, many, HD]),
                                           ALU.mult)
                if c >= 2:
                    qk_ready.tick(last, n)
                    continue
                link(last)
                heads = 8 if c == 0 else 2
                cos, sin = rope1[:, 0, t, :], rope1[:, 1, t, :]
                a3, b3 = (rope_t[:, i, 0:heads * HD] for i in range(2))
                src = row[:, 0:heads, :]
                v.tensor_tensor(a3.rearrange("p (h d) -> p h d", d=HD), src,
                                cos.unsqueeze(1).broadcast_to([P, heads, HD]), ALU.mult)
                split = "p h (a b d) -> p h a b d"
                s5 = src.rearrange(split, a=2, b=2)
                b5 = b3.rearrange("p (h a b d) -> p h a b d", h=heads, a=2, b=2)
                sin4 = sin.rearrange("p (a b d) -> p a b d", a=2, b=2)
                for half in range(2):
                    last = v.tensor_tensor(b5[:, :, :, half, :], s5[:, :, :, 1 - half, :],
                                           sin4[:, :, half, :].unsqueeze(1).broadcast_to([P, heads, 2, 16]), ALU.mult)
                link(last)
                if c == 0:
                    dst = pj[:, n % 3, :].rearrange("p (j half d) -> p half j d", j=4, half=2)
                    order = "p (half j d) -> p half j d"
                    ins = v.tensor_tensor(dst, a3.rearrange(order, j=4, half=2), b3.rearrange(order, j=4, half=2),
                                          ALU.add)
                else:
                    ins = v.tensor_tensor(pj[:, n % 3, 0:128], a3, b3, ALU.add)
                qk_ready.tick(ins, n)
            bank = banks.filled(dve, "conv_weights")
            conv_ready.tick(v.tensor_copy(convw[:, :], bank[:, 0:224]), "taps")
            for i in range(NU + 4):
                if i < NU:
                    bank = banks.filled(dve, ("score", i))
                    if i < NU // 2:
                        score_min.tick(v.tensor_reduce(nmin[:, i:i + 1], bank[:, :], AXX, ALU.min), i)
                    else:
                        _, h, t = unit_of(i)
                        dve.wait_ge(dist_in[h % 4], 16 * (h // 4 + 1))
                        banks.filled(dve, ("probsT", i - 3))
                        a = (TT - 1 - t) * P
                        score_min.tick(v.tensor_tensor_reduce(probs[:, i % 3, :], bank[:, :], dists[h % 4][:, a:a + T],
                                                              1.0, 3e38, ALU.add, ALU.min, nmin[:, i:i + 1]), i)
                n = i - 1
                if 0 <= n < NU and n % 2 == 1:
                    bank = banks.filled(dve, ("probsT", n))
                    if n >= 4:
                        banks.filled(dve, ("att", n // 2 - 2))
                    pt_dve.tick(v.tensor_copy(probsT[:, n % 4, :], bank[:, :]), n)
                if i >= 5 and i % 2 == 1:
                    p = i // 2 - 2
                    n = 2 * p
                    bank = banks.filled(dve, ("attT", p))
                    link(v.reciprocal(rsums[:, n:n + 2], psums[:, n:n + 2]))
                    for n in (2 * p, 2 * p + 1):
                        m, h, t = unit_of(n)
                        ins = v.tensor_scalar(xn[:, t, m * 512 + h * HD:m * 512 + (h + 1) * HD],
                                              bank[:, (n % 2) * HD:(n % 2 + 1) * HD], rsums[:, n:n + 1], None, ALU.mult)
                    att.tick(ins, p)
                if i % 5 == 4 and i // 5 < 12:
                    m = i // 5
                    bank = banks.filled(dve, ("mod", m))
                    if m // 2 in (2, 5):
                        row = gates[:, m // 6, (m % 2) * 512:(m % 2) * 512 + 512]
                        ins = v.tensor_tensor(row, bank[:, :], row, ALU.add)
                    else:
                        q = slice(64 * (m % 2), 64 * (m % 2) + 64)
                        ins = v.tensor_tensor(mod[q, m // 2, :, :], bank[q, 0:16].rearrange("p (j c) -> p j c", c=2),
                                              wide(ada_bias[q, m // 2, :], 2), ALU.add)
                    mod_done.tick(ins, m)
                if i in (NU - 6, NU - 4):
                    low_part("w_out", (i - NU + 6) // 2)
                t = mixed_at(i)
                if t is not None:
                    norm_tiles("mix1", [t])
            mod_done.wait(dve, 11)
            v.scalar_tensor_tensor(mod_gain[:, 0, :], mod[:, 1, :, 0], 1.0, gains[:, 3, :], ALU.add, ALU.mult)
            v.scalar_tensor_tensor(mod_gain[:, 1, :], mod[:, 1, :, 1], 1.0, gains[:, 3, :], ALU.add, ALU.mult)
            mod_done.tick(v.scalar_tensor_tensor(mod_gain[:, 2, :], mod[:, 4, :, 0], 1.0, gains[:, 5, :], ALU.add,
                                                 ALU.mult), "gains")
            norm_tiles("mix1", [TT - 1])
            norm_drains("mix1")
            for i in range(2, KT // 2):
                low_part("w_out", i)
            for t, n in SIDES:
                bank = banks.filled(dve, ("out1", t, n))
                side = x[:, t, n * 512:(n + 1) * 512]
                x1.tick(v.tensor_tensor(side, bank[:, :], side, ALU.add), (t, n))
            norm("norm2", lambda: low_part("w_up", 0))
            for f in range(FT + 1):
                if f < FT:
                    low_part(*SPLITS[SPLIT_AT["w_up", f] + 1])
                    if f == FT // 2:
                        norm_tiles("context")
                    for gv in range(2):
                        bank = banks.filled(dve, ("up", f, gv))
                        tap_mid.wait(dve, (f, gv))
                        y = (conv_g, conv_v)[gv][:, f % 2, :]
                        ch = gv * FT + f
                        link(v.scalar_tensor_tensor(y[:, 1:T], bank[:, 0:T - 1], convw[:, ch:ch + 1], y[:, 1:T],
                                                    ALU.mult, ALU.add))
                        tapped.tick(v.scalar_tensor_tensor(y[:, 0:T - 1], bank[:, 1:T], convw[:, 88 + ch:89 + ch],
                                                           y[:, 0:T - 1], ALU.mult, ALU.add), (f, gv))
                if f >= 1:
                    gelued.wait(dve, f - 1)
                    hidden.tick(v.tensor_tensor(hid[:, f - 1, :], conv_g[:, (f - 1) % 2, :], conv_v[:, (f - 1) % 2, :],
                                                ALU.mult), f - 1)
            hidden_low(0)
            norm_drains("context")
            low_part("w_down", 1)
            hidden_low(1)
            for i in range(2, ND):
                low_part("w_down", i)
                hidden_low(i)
            low_part("w_kvd", 0)
            for t, n in SIDES:
                bank = banks.filled(dve, ("down", t, n))
                side = x[:, t, n * 512:(n + 1) * 512]
                x2.tick(v.tensor_tensor(side, bank[:, :], side, ALU.add), (t, n))
            norm("norm1_2", lambda: low_part("w_kvd", 1))
            low_part("w_zq", 0)
            for t in range(AT):
                bank = banks.filled(dve, ("kvd", t))
                kvd_copied.tick(v.tensor_copy(kvd[:, t, :], bank[:, 0:272]), t)
            kvd_copied.wait(dve, AT - 1)
            raw = sm[:, 0, :].rearrange("p (t k) -> p t k", t=AT)
            link(v.tensor_tensor(raw, kvd[:, :, 0:16], dt_bias[:, :].unsqueeze(1).broadcast_to([P, AT, 16]), ALU.add))
            dt_abs.tick(v.scalar_tensor_tensor(sm[:, 4, :], sm[:, 0, :], -1.0, sm[:, 0, :], ALU.mult, ALU.max), 0)
            low_part("w_zq", 1)
            dt_exp.wait(dve, 0)
            dt_abs.tick(v.tensor_scalar(sm[:, 2, :], sm[:, 1, :], 1.0, None, ALU.add), 1)
            dt_abs.wait(dve, 1)
            link(v.tensor_scalar(sm[:, 4, :], sm[:, 2, :], -1.0, None, ALU.add))
            link(v.tensor_scalar(sm[:, 5, :], sm[:, 4, :], 0.0, None, ALU.is_equal))
            link(v.tensor_tensor(sm[:, 4, :], sm[:, 4, :], sm[:, 5, :], ALU.add))
            link(v.reciprocal(sm[:, 4, :], sm[:, 4, :]))
            link(v.tensor_tensor(sm[:, 4, :], sm[:, 4, :], sm[:, 1, :], ALU.mult))
            low_part("w_zq", 2)
            dt_log.wait(dve, 0)
            link(v.tensor_tensor(sm[:, 4, :], sm[:, 4, :], sm[:, 3, :], ALU.mult))
            link(v.tensor_tensor(sm[:, 5, :], sm[:, 5, :], sm[:, 1, :], ALU.mult))
            link(v.tensor_tensor(sm[:, 4, :], sm[:, 4, :], sm[:, 5, :], ALU.add))
            link(v.scalar_tensor_tensor(sm[:, 5, :], sm[:, 0, :], 0.0, sm[:, 4, :], ALU.max, ALU.add))
            a_exp.wait(dve, 0)
            dta_ready.tick(v.scalar_tensor_tensor(
                sm[:, 6, :].rearrange("p (t k) -> p t k", t=AT), sm[:, 5, :].rearrange("p (t k) -> p t k", t=AT), -1.0,
                a_log[:, :].unsqueeze(1).broadcast_to([P, AT, 16]), ALU.mult, ALU.mult), 0)
            low_part("w_zq", 3)
            low_part("w_xbc", 0)
            bank = banks.filled(dve, "cumsum")
            v.tensor_copy(sm[:, 7, :], bank[:, 0:96])
            link(v.tensor_copy(sm[:, 2, :], bank[:, 96:192]))
            cs_copied.tick(v.tensor_tensor(sm[:, 1, :], sm[:, 2, :], sm[:, 7, :], ALU.subtract), 0)
            cs_exp.wait(dve, 0)
            sw_ready.tick(v.tensor_tensor(sm[:, 9, :], sm[:, 1, :], sm[:, 5, :], ALU.mult), 0)
            link(v.tensor_scalar(win_min[:, 64:72], sinks[:, :], -1.0, None, ALU.mult))
            for t in range(TT):
                q_copied.wait(dve, t)
                link(rope(v, (rope_q[:, 0, :], rope_q[:, 1, :]), q2[:, t, :], H, t))
                order = "p (half j d) -> p half j d"
                ins = v.tensor_tensor(q2[:, t, :].rearrange("p (j half d) -> p half j d", j=4, half=2),
                                      rope_q[:, 0, :].rearrange(order, half=2, j=4),
                                      rope_q[:, 1, :].rearrange(order, half=2, j=4), ALU.add)
                roped_q.tick(ins, t)
                roped_q.wait(dve, t)
            for m, c in XBC:
                if m % 2 == c == 0 and m < KT - 2:
                    low_part("w_xbc", m // 2 + 1)
                bank = banks.filled(dve, ("xbc", m, c))
                mid2.wait(dve, (m, c))
                n, o = (CTX, T) if c else (T, 0)
                y = conv2[:, m % 2, o:o + n]
                for k, off in ((0, -2), (1, -1), (3, 1), (4, 2)):
                    a, b = max(0, -off), min(n, n - off)
                    w = convw[:, 176 + 8 * k + m:177 + 8 * k + m]
                    ins = v.scalar_tensor_tensor(y[:, a:b], bank[:, a + off:b + off], w, y[:, a:b], ALU.mult, ALU.add)
                    if k < 4:
                        link(ins)
                tapped2.tick(ins, (m, c))

            def y_rows(k):
                t, d = YS[k]
                row = cat[:, t, 0:512]
                off = banks.filled(dve, ("yoff", k))
                ea = wide(sm[:, 0, t * 16 + d * 8:t * 16 + d * 8 + 8], HD)
                ins = v.tensor_tensor(ytmp.rearrange("p (h d) -> p h d", d=HD),
                                      off[:, :].rearrange("p (h d) -> p h d", d=HD), ea, ALU.mult)
                y_read.tick(ins, (k, "off"))
                y_read.wait(dve, (k, "off"))
                diag = banks.filled(dve, ("ydiag", k))
                if d == 0:
                    y_read.tick(v.tensor_tensor(row, diag[:, :], ytmp, ALU.add), (k, "diag"))
                    y_read.wait(dve, (k, "diag"))
                    return
                link(v.tensor_tensor(row, row, ytmp, ALU.add))
                y_read.tick(v.tensor_tensor(row, diag[:, :], row, ALU.add), (k, "diag"))
                y_read.wait(dve, (k, "diag"))

            for what, i in weave:
                if what == "win":
                    if i < NW:
                        h, t = window_of(i)
                        lo, hi = near(t)
                        n = (hi - lo + 1) * P
                        if i >= 3:
                            banks.filled(dve, ("wprobsT", i - 3, 1))
                        mask = C("window")
                        a = (lo - t + 1) * P
                        near_b, far_b = (banks.filled(dve, ("wscore", i, k)) for k in range(2))
                        v.tensor_tensor_reduce(wprobs[:, i % 3, 0:n], near_b[:, 0:n], mask[:, a:a + n], 1.0, 3e38,
                                               ALU.add, ALU.min, win_min[:, 2 * i:2 * i + 1])
                        link(v.tensor_tensor_reduce(wprobs[:, i % 3, n:n + CTX], far_b[:, 0:CTX],
                                                    mask[:, 3 * P:3 * P + CTX], 1.0, 3e38, ALU.add, ALU.min,
                                                    win_min[:, 2 * i + 1:2 * i + 2]))
                        wscore.tick(v.tensor_scalar(nmin[:, i:i + 1], win_min[:, 2 * i:2 * i + 1], win_min[:, 2 * i + 1:2 * i + 2],
                                                    win_min[:, 64 + h:65 + h], ALU.min, ALU.min), i)
                    if i >= 5 and i % 2 == 1:
                        p = i // 2 - 2
                        both = slice(2 * p, 2 * p + 2)
                        bank = banks.filled(dve, ("wattT", p))
                        link(v.tensor_tensor(rsums[:, both], psums[:, both], sink_exp[:, both], ALU.add))
                        link(v.reciprocal(rsums[:, both], rsums[:, both]))
                        for m in (2 * p, 2 * p + 1):
                            h, t = window_of(m)
                            ins = v.tensor_scalar(cat[:, t, 512 + h * HD:512 + (h + 1) * HD],
                                                  bank[:, (m % 2) * HD:(m % 2 + 1) * HD], rsums[:, m:m + 1], None, ALU.mult)
                        watt.tick(ins, p)
                elif what == "state":
                    d, pos = STATES[i]
                    t = TILE_AT[d][pos]
                    bank = banks.filled(dve, ("state", i))
                    if pos == 0:
                        ins = v.tensor_copy(state0[:, d, :], bank[:, :])
                    else:
                        state_decayed.wait(dve, i)
                        ins = v.tensor_tensor(state[:, d, pos - 1, :], bank[:, :], stmp[:, i % 2, :], ALU.add)
                    state_ready.tick(ins, i)
                else:
                    if 1 <= i <= len(YS):
                        k = i - 1
                        if k % 2 == 0:
                            cb_masked.wait(dve, k // 2)
                        decayed.wait(dve, k)
                        for g in range(2):
                            rows = decay[:, k % 3, 4 * g:4 * g + 4, :]
                            ins = v.tensor_tensor(rows, rows, cbm[:, YS[k][1], g, :].unsqueeze(1).broadcast_to([P, 4, P]),
                                                  ALU.mult)
                        m_ready.tick(ins, k)
                    if i < len(YS):
                        t, d = YS[i]
                        if d == 0:
                            if i:
                                m_ready.wait(dve, i - 1)
                            bank = banks.filled(dve, ("cb", t))
                            b3 = bank[:, 0:256].rearrange("p (g n) -> p g n", g=2)
                            v.tensor_tensor(cbm[:, 0, :, :], b3, C("upto").unsqueeze(1).broadcast_to([P, 2, P]),
                                            ALU.mult)
                            cb_masked.tick(v.tensor_tensor(
                                cbm[:, 1, :, :], b3, C("from").unsqueeze(1).broadcast_to([P, 2, P]), ALU.mult), t)
                        if i >= 3:
                            banks.filled(dve, ("ydiag", i - 3))
                        for g in range(2):
                            bank = banks.filled(dve, ("seg", i, g))
                            for h in range(4):
                                a = t * 16 + d * 8 + g * 4 + h
                                ins = v.tensor_scalar(decay[:, i % 3, g * 4 + h, :], bank[:, h * P:(h + 1) * P],
                                                      sm[:, 7, a:a + 1], 0.0, ALU.subtract, ALU.min)
                            seg_ready.tick(ins, (i, g))
                    if i >= 2:
                        y_rows(i - 2)
            norm("mix2", lambda: low_part("w_out2", 0))
            for i in range(1, KT // 2):
                low_part("w_out2", i)
            for t, n in SIDES:
                bank = banks.filled(dve, ("out2", t, n))
                side = x[:, t, n * 512:(n + 1) * 512]
                gated = (ytmp, dtx[:, 0, :])[n]
                link(v.tensor_tensor(gated, bank[:, :], gates[:, 0, n * 512:(n + 1) * 512], ALU.mult))
                x3.tick(v.tensor_tensor(side, side, gated, ALU.add), (t, n))
            v.memset(gl[:, :, :], -3e38)
            route.tick(v.memset(lgT, 0.0), "cleared")
            norm("norm2_2")
            y_gate = gates[:, 0, 0:512]
            v.tensor_copy(gates[0:64, 0, 0:512], gates[0:64, 1, 0:512])
            link(v.tensor_copy(gates[64:128, 0, 0:512], gates[64:128, 1, 512:1024]))
            route_pe.wait(dve, "halves")
            route.wait(dve, "cleared")
            route.tick(v.tensor_copy(lgT[64:100, :], ps[0][64:100, :]), "odd")
            route_pe.wait(dve, "logits")
            link(v.tensor_tensor(lg[:, :, :], ps[1][:, 0:TT * 36].rearrange("p (t n) -> p t n", t=TT),
                                 route_bias[:, :].unsqueeze(1).broadcast_to([P, TT, 36]), ALU.add))
            link(v.tensor_copy(gl[:, :, 0:4], lg[:, :, 0:4]))
            for t in range(TT):
                ins = v.max(g8[:, t, :], gl[:, t, :])
            link(ins)
            for t in range(TT):
                ins = v.max_index(gi[:, t, :], g8[:, t, :], gl[:, t, :])
            route.tick(ins, "logits")
            route.wait(dve, "logits")
            link(v.tensor_copy(gif[:, :], gi[:, :, 0]))
            route.tick(v.tensor_scalar(g8[:, :, 0:1], g8[:, :, 0:1], -1.0, None, ALU.mult), "max")
            for t in range(TT):
                ins = v.tensor_scalar(el[:, t, :], C("group"), gif[:, t:t + 1], BIG, ALU.is_equal, ALU.mult)
            link(ins)
            link(v.scalar_tensor_tensor(el[:, :, :], el[:, :, :], -BIG, lg[:, :, 4:36], ALU.add, ALU.add))
            for t in range(TT):
                ins = v.max(e8[:, t, :], el[:, t, :])
            link(ins)
            for t in range(TT):
                ins = v.max_index(ei[:, t, :], e8[:, t, :], el[:, t, :])
            link(ins)
            link(v.tensor_copy(eif[:, :, :], ei[:, :, 0:2]))
            route.tick(v.tensor_tensor(wts[:, :, 2], e8[:, :, 1], e8[:, :, 0], ALU.subtract), "top2")
            pairs = [P, TT, 2, E]
            link(v.tensor_tensor(ohot[:, :, :, :], C("expert").unsqueeze(1).unsqueeze(1).broadcast_to(pairs), wide(eif[:, :, :], E),
                                 ALU.is_equal))
            route.tick(v.tensor_tensor(osum[:, :, :], ohot[:, :, 0, :], ohot[:, :, 1, :], ALU.add), "hot")
            route_act.wait(dve, "pair_exp")
            link(v.tensor_scalar(wts[:, :, 4], wts[:, :, 3], 1.0, None, ALU.add))
            link(v.tensor_tensor(wts[:, :, 4], wts[:, :, 4], gsum[:, :], ALU.mult))
            link(v.reciprocal(wts[:, :, 0], wts[:, :, 4]))
            route.tick(v.tensor_tensor(wts[:, :, 1], wts[:, :, 0], wts[:, :, 3], ALU.mult), "weights")
            route_pe.wait(dve, "rank")
            v.tensor_copy(rank[:, 0, :], ps[2][:, 0:E])
            link(v.tensor_copy(tot[:, :, :], ps[2][:, TT * E:2 * TT * E].rearrange("p (t e) -> p t e", t=TT)))
            for t in range(1, TT):
                ins = v.tensor_tensor(rank[:, t, :], ps[2][:, t * E:(t + 1) * E], tot[:, t - 1, :], ALU.add)
                link(v.tensor_tensor(tot[:, t, :], tot[:, t, :], tot[:, t - 1, :], ALU.add))
            cnt = tot[:, TT - 1, :]
            link(v.tensor_tensor(over_cnt, wide(cnt, T // BLK - 1), C("full_blocks").unsqueeze(1).broadcast_to(
                [P, E, T // BLK - 1]), ALU.is_gt))
            link(v.tensor_reduce(novf, over_cnt, AXX, ALU.add))
            a, b = 0, 1
            v.tensor_tensor(prod, ohot[:, :, :, :], rank[:, :, :].unsqueeze(2).broadcast_to(pairs), ALU.mult)
            link(v.tensor_copy(start[:, 0, :], novf))
            for k in (1, 2, 4, 8, 16):
                v.tensor_copy(start[:, b, 0:k], start[:, a, 0:k])
                link(v.tensor_tensor(start[:, b, k:E], start[:, a, k:E], start[:, a, 0:E - k], ALU.add))
                a, b = b, a
            v.tensor_reduce(pk.rearrange("p (t k) -> p t k", t=TT), prod, AXX, ALU.add)
            link(v.tensor_tensor(first, start[:, a, :], novf, ALU.subtract))
            link(v.tensor_tensor(first, first, C("blocks_on"), ALU.add))
            v.tensor_tensor(over_place, wide(pk, T // BLK - 1), C("full_blocks").unsqueeze(1).broadcast_to(
                [P, 8, T // BLK - 1]), ALU.is_ge)
            link(v.tensor_tensor(prod, ohot[:, :, :, :], first.unsqueeze(1).unsqueeze(1).broadcast_to(pairs), ALU.mult))
            v.tensor_reduce(quo, over_place, AXX, ALU.add)
            link(v.tensor_reduce(bk.rearrange("p (t k) -> p t k", t=TT), prod, AXX, ALU.add))
            v.scalar_tensor_tensor(pk, quo, -float(BLK), pk, ALU.mult, ALU.add)
            link(v.tensor_tensor(bk, bk, quo, ALU.add))
            link(v.scalar_tensor_tensor(bk, quo, 1.0, bk, ALU.is_ge, ALU.mult))
            link(v.tensor_tensor(bk, bk, eif[:, :, :].rearrange("p t k -> p (t k)"), ALU.add))
            by_block = [P, 8, 2, NBLK]
            link(v.tensor_tensor(hot_b[:, :, :, :], C("block").unsqueeze(1).unsqueeze(1).broadcast_to(by_block),
                                 wide(wide(bk, 2), NBLK), ALU.is_equal))
            v.tensor_tensor(hot_p.rearrange("p n (a b) -> p n a b", a=2),
                            C("place").unsqueeze(1).unsqueeze(1).broadcast_to([P, 8, 2, BLK]), wide(wide(pk, 2), BLK),
                            ALU.is_equal)
            route.tick(v.tensor_tensor(hot_b[:, :, :, :], hot_b[:, :, :, :], wide(C("numbers").rearrange(
                "p (n k) -> p n k", k=2), NBLK), ALU.mult), "places")
            v.tensor_tensor(later, start[:, a, :].unsqueeze(1).broadcast_to([P, NOVF, E]),
                            C("block")[:, 0:NOVF].unsqueeze(2).broadcast_to([P, NOVF, E]), ALU.is_le)
            link(v.tensor_copy(ovf[0:1, NOVF:NOVF + 1], start[0:1, a, E - 1:E]))
            link(v.tensor_reduce(later_cnt[:, 0:NOVF], later, AXX, ALU.add))
            link(v.tensor_scalar(later_cnt[:, 0:NOVF], later_cnt[:, 0:NOVF], float(E - 1), None, ALU.min))
            link(v.tensor_copy(ovf[0:1, 0:NOVF], later_cnt[0:1, 0:NOVF]))
            route_pe.wait(dve, "table")
            numbers = ps[3][:, 0:2 * NBLK]
            v.tensor_scalar(tval[:, 1, :], numbers, 0.0, 16384.0, ALU.is_equal, ALU.mult)
            link(v.tensor_scalar(tval[:, 0, NBLK:2 * NBLK], numbers[:, NBLK:2 * NBLK], 2.0, C("half2"), ALU.mult, ALU.add))
            v.scalar_tensor_tensor(tok_of[:, :], numbers[:, 0:NBLK], -1.0, tval[:, 1, 0:NBLK], ALU.add, ALU.add)
            route.tick(v.tensor_tensor(row_of[:, :], tval[:, 0, NBLK:2 * NBLK], tval[:, 1, NBLK:2 * NBLK], ALU.add), "table")

            def tokens_scaled(n, par, reuse):
                dve.wait_ge(xt_filled, n + 1)
                if reuse is not None:
                    dve.wait_ge(gu_filled, reuse)
                v.tensor_tensor(xT[:, par, :, :], ps[par][:, :].rearrange("p (j n) -> p j n", j=KT),
                                wide(mod_gain[:, 2, :], BLK), ALU.mult).then_inc(xt_scaled, 1)
                dve.wait_ge(xt_scaled, n + 1)
                v.tensor_tensor(xT[:, par, :, :], xT[:, par, :, :], wide(mod[:, 3, :, 0], BLK), ALU.add).then_inc(
                    xt_ready, 1)

            def expert(n, par, kpar, reuse, following=None):
                hiddenT, y = ps[4 + par], ps[6 + par]
                dve.wait_ge(silu_ready, n + 1)
                if reuse is not None:
                    dve.wait_ge(y_filled, reuse)
                v.tensor_tensor(hidE[:, par, :, :], sg[:, par, :, :],
                                hiddenT[:, :].rearrange("p (f n) -> p f n", f=4)[:, :, BLK:2 * BLK],
                                ALU.mult).then_inc(hid_ready, 1)
                if following is not None:
                    tokens_scaled(*following)
                dve.wait_ge(y_filled, n + 1)
                if reuse is not None:
                    dve.wait_ge(y_stored[par], 16 * kpar)
                v.tensor_tensor(yE[:, par, :], y[:, :], y_gate, ALU.mult).then_inc(y_ready, 1)

            tokens_scaled(0, 0, None)
            expert(0, 0, 0, None, (1, 1, None))
            expert(1, 1, 0, None, (2, 0, 1))
            with dve.Fori(1, E // 2 - 1) as it:
                for par in range(2):
                    n = 2 * it + par
                    expert(n, par, it, n - 1, (n + 1, 1 - par, n))
            expert(E - 2, 0, E // 2 - 1, E - 3, (E - 1, 1, E - 2))
            expert(E - 1, 1, E // 2 - 1, E - 2)
            later_n = dve.value_load(ovf[0:1, NOVF:NOVF + 1], min_val=0, max_val=NOVF)
            with dve.If(later_n > 0):
                with dve.Fori(0, later_n) as i:
                    tokens_scaled(i + E, 0, i + E)
                    expert(i + E, 0, i + E // 2, i + E)
            dve.wait_ge(final_in, 16)
            for t in range(TT + 1):
                if t < TT:
                    dve.wait_ge(y01_in[t], 16)
                    link(v.scalar_tensor_tensor(x[:, t, :], y01[:, t, 0, :], wts[:, t, 0:1], x[:, t, :], ALU.mult,
                                                ALU.add))
                    final_x.tick(v.scalar_tensor_tensor(x[:, t, :], y01[:, t, 1, :], wts[:, t, 1:2], x[:, t, :],
                                                        ALU.mult, ALU.add), t)
                if t >= 1:
                    rooted.wait(dve, ("final", t - 1))
                    link(v.reciprocal(rstd[:, t - 1:t], roots[:, t - 1:t]))
                    final_y.tick(v.scalar_tensor_tensor(y01[:, t - 1, 0, :], x[:, t - 1, :], rstd[:, t - 1:t], final_gain,
                                                        ALU.mult, ALU.mult), t - 1)


INPUTS = ["x", "norm1_g", "w_in", "qa_norm_g", "ka_norm_g", "qb_norm_g", "kb_norm_g", "outa_norm_g", "outb_norm_g",
          "w_out", "norm2_g", "w_up", "conv_w", "conv_b", "w_down", "c_2", "ctx_2", "c_ctx_2", "w_ada_2", "b_ada_2",
          "norm1_2", "w_in_2", "conv_w_2", "conv_b_2", "dt_bias_2", "a_log_2", "d_skip_2", "ssd_norm_2",
          "attn_sinks_2", "w_out_2", "norm2_2", "w_group_2", "b_group_2", "w_expert_2", "b_expert_2", "w_gate_2",
          "w_up_2", "w_down_2", "norm_final_2"]


def kernel(**inputs):
    import concourse.bacc as bacc
    from concourse.bass_utils import run_bass_kernel_spmd

    nc = bacc.Bacc("TRN2", target_bir_lowering=False, num_devices=1)
    arrays, aps = {}, {}
    for name in INPUTS:
        a = np.ascontiguousarray(inputs[name])
        arrays[f"in_{name}"] = a
        aps[name] = nc.dram_tensor(f"in_{name}", a.shape, F32, kind="ExternalInput").ap()
    tables = {"tables": constants()[1], "rotary": constants()[2], "distances": distance_tables()}
    for name, a in tables.items():
        arrays[name] = a
    consts_d, rope1_d, dist_d = (nc.dram_tensor(n, a.shape, F32, kind="ExternalInput").ap() for n, a in tables.items())
    h_d = nc.dram_tensor("normed_tokens", (T, D), F32, kind="Internal").ap()
    y_d = nc.dram_tensor("expert_outputs", (4 * T, D // 2), F32, kind="Internal").ap()
    out = nc.dram_tensor("out", (1, T, D), F32, kind="ExternalOutput").ap()
    two_blocks(nc, consts_d, rope1_d, dist_d, h_d, y_d, aps, out)
    r = run_bass_kernel_spmd(nc, [arrays], core_ids=[0])
    return r.results[0]["out"]
```
